# Optimizing a Trainium2 kernel written in Bass

```python
import jax
import jax.numpy as jnp
from jax import lax
import numpy as np

D_MODEL = 1024
BATCH = 1
SEQ = 256
DEPTH = 2

GRID_W = 64
CTX_LEN = 256
N_MIXERS = 2
N_CONV_LAYERS = (DEPTH + 1) // 2
N_ATTN_LAYERS = DEPTH // 2
CONV_CH = D_MODEL
CONV_WIDTH = 31
CONV_PAD = CONV_WIDTH // 2
HEAD_DIM = 64
N_HEADS = D_MODEL // HEAD_DIM
N_KV_HEADS = N_HEADS // 4
GROUP = N_HEADS // N_KV_HEADS
Q_DIM = N_HEADS * HEAD_DIM
KV_DIM = N_KV_HEADS * HEAD_DIM
WINDOW = 128
BLOCK = 128
ROPE_THETA = 10000.0
ROPE_PAIRS = HEAD_DIM // 4
N_EXPERTS = 16
N_GROUPS = 4
EXPERTS_PER_GROUP = N_EXPERTS // N_GROUPS
TOP_K = 2
D_EXPERT = D_MODEL // 2
EPS = 1e-6
NEG_INF = -1e30

kernel_name = "hybrid_conv_swa_moe_diffusion_block"

def _rmsnorm(x, g):
    xf = x.astype(jnp.float32)
    xf = xf * lax.rsqrt(jnp.mean(xf * xf, axis=-1, keepdims=True) + EPS)
    return xf.astype(x.dtype) * g

def _layernorm(x, g, b):
    xf = x.astype(jnp.float32)
    mu = jnp.mean(xf, axis=-1, keepdims=True)
    var = jnp.mean(jnp.square(xf - mu), axis=-1, keepdims=True)
    return ((xf - mu) * lax.rsqrt(var + EPS)).astype(x.dtype) * g + b

def _adaln(cond, w, b):
    mod = jax.nn.silu(cond) @ w + b
    parts = jnp.split(mod, 6, axis=-1)
    if cond.ndim == 2:
        parts = [p[:, None, :] for p in parts]
    return parts

def _modulate(h, shift, scale):
    return h * (1 + scale) + shift

def _axial_rope_tables(seq_len, dtype):
    rows = seq_len // GRID_W
    row = jnp.broadcast_to(jnp.arange(rows, dtype=jnp.int32)[:, None], (rows, GRID_W)).reshape(seq_len)
    col = jnp.broadcast_to(jnp.arange(GRID_W, dtype=jnp.int32)[None, :], (rows, GRID_W)).reshape(seq_len)
    inv_freq = jnp.power(jnp.float32(ROPE_THETA), -jnp.arange(ROPE_PAIRS, dtype=jnp.float32) / ROPE_PAIRS)
    ang_r = row.astype(jnp.float32)[:, None] * inv_freq
    ang_c = col.astype(jnp.float32)[:, None] * inv_freq
    return (jnp.cos(ang_r).astype(dtype), jnp.sin(ang_r).astype(dtype),
            jnp.cos(ang_c).astype(dtype), jnp.sin(ang_c).astype(dtype))

def _rotate(x, cos, sin):
    x1, x2 = x[..., :ROPE_PAIRS], x[..., ROPE_PAIRS:]
    return jnp.concatenate([x1 * cos - x2 * sin, x2 * cos + x1 * sin], axis=-1)

def _apply_axial_rope(x, rope):
    cos_r, sin_r, cos_c, sin_c = rope
    shape = (1, x.shape[1]) + (1,) * (x.ndim - 3) + (ROPE_PAIRS,)
    half = HEAD_DIM // 2
    return jnp.concatenate([
        _rotate(x[..., :half], cos_r.reshape(shape), sin_r.reshape(shape)),
        _rotate(x[..., half:], cos_c.reshape(shape), sin_c.reshape(shape)),
    ], axis=-1)

def _conformer_conv(h, w_pw1, b_pw1, w_dw, b_dw, ln_g, ln_b, w_pw2, b_pw2):
    u = h @ w_pw1 + b_pw1
    a, gate = jnp.split(u, 2, axis=-1)
    u = a * jax.nn.sigmoid(gate)
    u = lax.conv_general_dilated(
        u, w_dw[:, None, :], window_strides=(1,), padding=[(CONV_PAD, CONV_PAD)],
        dimension_numbers=("NWC", "WIO", "NWC"), feature_group_count=CONV_CH) + b_dw
    u = jax.nn.silu(_layernorm(u, ln_g, ln_b))
    return u @ w_pw2 + b_pw2

def _scores(q, k):
    return jnp.einsum("bqhgd,bkhd->bhgqk", q, k, preferred_element_type=jnp.float32)

def _sink_softmax(score_parts, sink):
    b, kvh, g, q = score_parts[0].shape[:4]
    col = jnp.broadcast_to(sink.astype(jnp.float32).reshape(1, kvh, g, 1, 1), (b, kvh, g, q, 1))
    p = jax.nn.softmax(jnp.concatenate(score_parts + [col], axis=-1), axis=-1)
    outs = []
    off = 0
    for sp in score_parts:
        n = sp.shape[-1]
        outs.append(p[..., off:off + n])
        off += n
    return outs

def _attend(probs, values):
    out = None
    for p, v in zip(probs, values):
        o = jnp.einsum("bhgqk,bkhd->bqhgd", p.astype(v.dtype), v)
        out = o if out is None else out + o
    return out.reshape(out.shape[0], out.shape[1], Q_DIM)

def _windowed_sink_gqa(h, hc, w_qkv, w_o, sink, rope, with_ctx_out):
    b, s, _ = h.shape
    lc = hc.shape[1]
    sink = sink.reshape(N_KV_HEADS, GROUP)
    qkv = h @ w_qkv
    q = qkv[..., :Q_DIM].reshape(b, s, N_KV_HEADS, GROUP, HEAD_DIM)
    k = qkv[..., Q_DIM:Q_DIM + KV_DIM].reshape(b, s, N_KV_HEADS, HEAD_DIM)
    v = qkv[..., Q_DIM + KV_DIM:].reshape(b, s, N_KV_HEADS, HEAD_DIM)
    q = _apply_axial_rope(q, rope) * (HEAD_DIM ** -0.5)
    k = _apply_axial_rope(k, rope)
    kvc = hc @ w_qkv[:, Q_DIM:]
    kc = kvc[..., :KV_DIM].reshape(b, lc, N_KV_HEADS, HEAD_DIM)
    vc = kvc[..., KV_DIM:].reshape(b, lc, N_KV_HEADS, HEAD_DIM)
    pad = ((0, 0), (WINDOW, WINDOW), (0, 0), (0, 0))
    kp = jnp.pad(k, pad)
    vp = jnp.pad(v, pad)
    span = BLOCK + 2 * WINDOW

    def block(i):
        start = i * BLOCK
        qb = lax.dynamic_slice_in_dim(q, start, BLOCK, axis=1)
        kb = lax.dynamic_slice_in_dim(kp, start, span, axis=1)
        vb = lax.dynamic_slice_in_dim(vp, start, span, axis=1)
        qpos = start + jnp.arange(BLOCK)
        kpos = start - WINDOW + jnp.arange(span)
        valid = ((jnp.abs(qpos[:, None] - kpos[None, :]) <= WINDOW)
                 & (kpos[None, :] >= 0) & (kpos[None, :] < s))
        s_band = jnp.where(valid, _scores(qb, kb), NEG_INF)
        s_ctx = _scores(qb, kc)
        p_band, p_ctx = _sink_softmax([s_band, s_ctx], sink)
        return _attend([p_band, p_ctx], [vb, vc])

    out = lax.map(block, jnp.arange(s // BLOCK))
    out = jnp.transpose(out, (1, 0, 2, 3)).reshape(b, s, Q_DIM)
    y = out @ w_o
    if not with_ctx_out:
        return y, None
    qc = (hc @ w_qkv[:, :Q_DIM]).reshape(b, lc, N_KV_HEADS, GROUP, HEAD_DIM) * (HEAD_DIM ** -0.5)
    (p_c,) = _sink_softmax([_scores(qc, kc)], sink)
    yc = _attend([p_c], [vc]) @ w_o
    return y, yc

def _route(h, router_w, router_b):
    t = h.shape[0]
    s = jax.nn.sigmoid(h.astype(jnp.float32) @ router_w.astype(jnp.float32))
    sel = s + router_b.astype(jnp.float32)
    sel_g = sel.reshape(t, N_GROUPS, EXPERTS_PER_GROUP)
    group_score = jnp.sum(lax.top_k(sel_g, TOP_K)[0], axis=-1)
    best_group = jnp.argmax(group_score, axis=-1)
    in_group = best_group[:, None] == jnp.arange(N_GROUPS)[None, :]
    sel_masked = jnp.where(in_group[:, :, None], sel_g, NEG_INF).reshape(t, N_EXPERTS)
    _, top_idx = lax.top_k(sel_masked, TOP_K)
    w = jnp.take_along_axis(s, top_idx, axis=-1)
    w = w / jnp.sum(w, axis=-1, keepdims=True)
    return jnp.sum(jax.nn.one_hot(top_idx, N_EXPERTS, dtype=jnp.float32) * w[..., None], axis=1)

def _grouped_moe(h, router_w, router_b, w_gate, w_up, w_down):
    gates = _route(h, router_w, router_b).astype(h.dtype)
    y = jnp.zeros_like(h)
    for e in range(N_EXPERTS):
        act = jax.nn.silu(h @ w_gate[e]) * (h @ w_up[e])
        y = y + gates[:, e:e + 1] * (act @ w_down[e])
    return y

def setup_inputs(seed: int = 0) -> dict:
    key = jax.random.key(seed)
    ks = jax.random.split(key, 25)

    def nrm(k, shape, scale):
        return jax.random.normal(k, shape, jnp.float32) * scale

    d, f = D_MODEL, D_EXPERT
    return {
        "x": nrm(ks[0], (BATCH, SEQ, d), 1.0),
        "c": nrm(ks[1], (BATCH, d), 1.0),
        "ctx": nrm(ks[2], (BATCH, CTX_LEN, d), 1.0),
        "c_ctx": nrm(ks[3], (d,), 1.0),
        "w_mod": nrm(ks[4], (DEPTH, d, 6 * d), 0.5 * d ** -0.5),
        "b_mod": nrm(ks[5], (DEPTH, 6 * d), 0.02),
        "norm1_g": 1.0 + nrm(ks[6], (DEPTH, d), 0.02),
        "norm2_g": 1.0 + nrm(ks[7], (DEPTH, d), 0.02),
        "conv_w_pw1": nrm(ks[8], (N_CONV_LAYERS, d, 2 * CONV_CH), d ** -0.5),
        "conv_b_pw1": nrm(ks[9], (N_CONV_LAYERS, 2 * CONV_CH), 0.02),
        "conv_w_dw": nrm(ks[10], (N_CONV_LAYERS, CONV_WIDTH, CONV_CH), CONV_WIDTH ** -0.5),
        "conv_b_dw": nrm(ks[11], (N_CONV_LAYERS, CONV_CH), 0.02),
        "conv_ln_g": 1.0 + nrm(ks[12], (N_CONV_LAYERS, CONV_CH), 0.02),
        "conv_ln_b": nrm(ks[13], (N_CONV_LAYERS, CONV_CH), 0.02),
        "conv_w_pw2": nrm(ks[14], (N_CONV_LAYERS, CONV_CH, d), CONV_CH ** -0.5),
        "conv_b_pw2": nrm(ks[15], (N_CONV_LAYERS, d), 0.02),
        "attn_w_qkv": nrm(ks[16], (N_ATTN_LAYERS, d, Q_DIM + 2 * KV_DIM), d ** -0.5),
        "attn_w_o": nrm(ks[17], (N_ATTN_LAYERS, Q_DIM, d), Q_DIM ** -0.5),
        "attn_sink": nrm(ks[18], (N_ATTN_LAYERS, N_HEADS), 1.0),
        "router_w": nrm(ks[19], (d, N_EXPERTS), d ** -0.5),
        "router_b": nrm(ks[20], (N_EXPERTS,), 0.01),
        "moe_w_gate": nrm(ks[21], (DEPTH, N_EXPERTS, d, f), d ** -0.5),
        "moe_w_up": nrm(ks[22], (DEPTH, N_EXPERTS, d, f), d ** -0.5),
        "moe_w_down": nrm(ks[23], (DEPTH, N_EXPERTS, f, d), f ** -0.5),
        "final_g": 1.0 + nrm(ks[24], (d,), 0.02),
    }

def reference(x, c, ctx, c_ctx, w_mod, b_mod, norm1_g, norm2_g,
              conv_w_pw1, conv_b_pw1, conv_w_dw, conv_b_dw, conv_ln_g, conv_ln_b, conv_w_pw2, conv_b_pw2,
              attn_w_qkv, attn_w_o, attn_sink, router_w, router_b,
              moe_w_gate, moe_w_up, moe_w_down, final_g):
    b, s, d = x.shape
    lc = ctx.shape[1]
    rope = _axial_rope_tables(s, x.dtype)
    for i in range(DEPTH):
        last = i == DEPTH - 1
        is_attn = (i % N_MIXERS) == 1
        j = i // N_MIXERS
        sh1, sc1, g1, sh2, sc2, g2 = _adaln(c, w_mod[i], b_mod[i])
        csh1, csc1, cg1, csh2, csc2, cg2 = _adaln(c_ctx, w_mod[i], b_mod[i])
        h = _modulate(_rmsnorm(x, norm1_g[i]), sh1, sc1)
        if is_attn:
            hc = _modulate(_rmsnorm(ctx, norm1_g[i]), csh1, csc1)
            y, yc = _windowed_sink_gqa(h, hc, attn_w_qkv[j], attn_w_o[j], attn_sink[j], rope, not last)
        else:
            conv_p = (conv_w_pw1[j], conv_b_pw1[j], conv_w_dw[j], conv_b_dw[j],
                      conv_ln_g[j], conv_ln_b[j], conv_w_pw2[j], conv_b_pw2[j])
            y = _conformer_conv(h, *conv_p)
            if not last:
                hc = _modulate(_rmsnorm(ctx, norm1_g[i]), csh1, csc1)
                yc = _conformer_conv(hc, *conv_p)
        x = x + g1 * y
        h2 = _modulate(_rmsnorm(x, norm2_g[i]), sh2, sc2)
        if last:
            out = _grouped_moe(h2.reshape(b * s, d), router_w, router_b,
                               moe_w_gate[i], moe_w_up[i], moe_w_down[i]).reshape(b, s, d)
            x = x + g2 * out
        else:
            ctx = ctx + cg1 * yc
            hc2 = _modulate(_rmsnorm(ctx, norm2_g[i]), csh2, csc2)
            tokens = jnp.concatenate([hc2, h2], axis=1).reshape(b * (lc + s), d)
            out = _grouped_moe(tokens, router_w, router_b,
                               moe_w_gate[i], moe_w_up[i], moe_w_down[i]).reshape(b, lc + s, d)
            ctx = ctx + cg2 * out[:, :lc]
            x = x + g2 * out[:, lc:]
    return _rmsnorm(x, final_g)


_drawn_inputs = setup_inputs


def setup_inputs(seed=0):
    import zlib

    import numpy as np

    out = dict(_drawn_inputs(seed))
    spreads = {}
    factors = {'norm1_g': 5.793,
     'conv_b_pw1': 4.241,
     'conv_b_dw': 3.925,
     'conv_ln_g': 5.039,
     'conv_ln_b': 6.082,
     'conv_b_pw2': 2.725,
     'attn_sink': 8.0,
     'final_g': 2.852}
    for name, (base, spread) in spreads.items():
        noise = np.random.default_rng([zlib.crc32(name.encode()), seed]).standard_normal(out[name].shape)
        drawn = base * np.exp(spread * noise) if base else spread * noise
        out[name] = jnp.asarray(drawn.astype(out[name].dtype))
    for name, factor in factors.items():
        out[name] = (out[name] * factor).astype(out[name].dtype)
    return out
```

```python
import numpy as np
import concourse.bass as bass
from concourse import mybir
from contextlib import ExitStack

FP32 = mybir.dt.float32
I32 = mybir.dt.int32
ALU = mybir.AluOpType
ACT = mybir.ActivationFunctionType
AX = mybir.AxisListType

P = 128
D = 1024
KD = D // P
SEQ, CTX = 256, 256
NT = (SEQ + CTX) // P
NX = SEQ // P
HALF = 512
TAPS, PAD = 31, 15
HD, NH, NKV, GROUP = 64, 16, 4, 4
WINDOW = 128
GRID_W, ROPE_PAIRS, THETA = 64, 16, 10000.0
NE, NG, EPG = 16, 4, 4
F = 512
EPS = 1e-6
BIG = 1e30
TILE = 64
NTOK = (NT * P, NX * P)
MAXJ = tuple(n // TILE for n in NTOK)
ROWS = (NE + (2 * NTOK[0] - NE) // TILE) * TILE + TILE
ROOM = ROWS + (MAXJ[0] - 1) * TILE
MOD_THIRD = 2048
KV_BANKS = ((2, 4), (3, 6), (0, 0), (1, 2))
Q_BANKS = ((0, 0, 1), (0, 1, 3), (1, 0, 5), (1, 1, 7))
FIRST_ORDER = (1, 2, 3, 0)


def shape_constants():
    i = np.arange(P)
    ident = np.eye(P)
    before = (i[:, None] < i[None, :]) * 1.0
    ones = np.ones((P, P))
    mask = np.zeros((P, NX, 2 * SEQ))
    for b in range(NX):
        mask[:, b, :SEQ] = np.where(np.abs(b * P + i[:, None] - np.arange(SEQ)[None, :]) <= WINDOW, 0.0, -BIG)
    inv = np.power(np.float32(THETA), -np.arange(ROPE_PAIRS, dtype=np.float32) / np.float32(ROPE_PAIRS))
    tok = np.arange(SEQ)
    ang = np.stack([(tok // GRID_W).astype(np.float32)[:, None] * inv,
                    (tok % GRID_W).astype(np.float32)[:, None] * inv], axis=1)
    cos, sin = np.cos(ang), np.sin(ang)
    rope = np.concatenate([np.stack([cos, cos], 2).reshape(SEQ, HD),
                           np.stack([-sin, sin], 2).reshape(SEQ, HD)], axis=1)
    rope = rope.reshape(NX, P, 2 * HD).transpose(1, 0, 2)
    down = np.concatenate([np.broadcast_to(NE - np.arange(NE), (P, NE)),
                           np.broadcast_to(NG - np.arange(NG), (P, NG))], axis=1)
    small = np.concatenate([ident, before, ones, rope.reshape(P, -1), down], axis=1)
    return small.astype(np.float32), mask.reshape(P, -1).astype(np.float32)


class Order:

    def __init__(self, eng, sem, base=0):
        self.eng, self.sem, self.base, self.n = eng, sem, base, 0

    def step(self, ins):
        self.n += 1
        ins.then_inc(self.sem, 1)
        self.eng.wait_ge(self.sem, self.base + self.n)


def backbone(nc, x, c, ctx_in, c_ctx, w_mod, b_mod, norm1_g, norm2_g, w_pw1, b_pw1, w_dw, b_dw, ln_g, ln_b,
             w_pw2, b_pw2, w_qkv, w_o, sink, router_w, router_b, w_gate, w_up, w_down, final_g,
             small_c, mask_c, out):
    mod_d = nc.dram_tensor("mod_d", [6, 2, MOD_THIRD], FP32, kind="Internal").ap()
    xs_d = nc.dram_tensor("xs_d", [ROOM, D], FP32, kind="Internal").ap()
    x_src = [x[0, t * P:(t + 1) * P, :] for t in range(NX)] + [ctx_in[0, t * P:(t + 1) * P, :] for t in range(NX)]

    es = ExitStack()
    with es:
        def sb(name, shape, dt=FP32):
            return es.enter_context(nc.sbuf_tensor(name, shape, dt))

        def sem(name):
            return es.enter_context(nc.semaphore(name))

        R = sb("R", [P, 24576])
        V = sb("V", [P, 8192])
        E = sb("E", [P, 2048])
        P1 = sb("P1", [P, 4096])
        P2 = sb("P2", [P, 4096])
        xr = sb("xr", [P, NT, D])
        small = sb("small", [P, 3 * P + NX * 2 * HD + NE + NG])
        ident, before, ones = small[:, 0:P], small[:, P:2 * P], small[:, 2 * P:3 * P]
        rope = small[:, 3 * P:3 * P + NX * 2 * HD].rearrange("p (t s d) -> p t s d", t=NX, s=2)
        down_e = small[:, 3 * P + NX * 2 * HD:3 * P + NX * 2 * HD + NE]
        down_g = small[:, 3 * P + NX * 2 * HD + NE:3 * P + NX * 2 * HD + NE + NG]
        cT = sb("cT", [P, 2, KD])
        cs = sb("cs", [P, KD, 32])
        vpad = sb("vpad", [P, 2, 2, SEQ + 2 * PAD])
        sg = sb("sg", [P, HALF])
        par = sb("par", [P, 2 * KD + KD + KD + KD + 2 * KD])
        b1_c = par[:, 0:2 * KD].rearrange("p (h m) -> p h m", h=2)
        bdw_c, lng_c, lnb_c = (par[:, (2 + i) * KD:(3 + i) * KD] for i in range(3))
        n1_c = par[:, 5 * KD:7 * KD].rearrange("p (l m) -> p l m", l=2)
        wdw = sb("wdw", [P, TAPS, KD])
        rw = sb("rw", [P, KD, NE])
        rb = sb("rb", [P, NE])
        sink_b = sb("sink_b", [P, NH])
        eps_t = sb("eps_t", [P, 1])
        mod1 = sb("mod1", [P, 2, 2, 2, KD])
        A1 = sb("A1", [P, 2, 2, KD])
        zrow = sb("zrow", [P, HALF])
        ssq = sb("ssq", [P, NT])
        rstd = sb("rstd", [P, NT])
        lg_s = sb("lg_s", [P, NT, NE])
        r_a = sb("r_a", [P, NT, NE])
        r_b = sb("r_b", [P, NT, NE])
        r_c = sb("r_c", [P, NT, NE])
        oh = [sb(f"oh{i}", [P, NT, NE]) for i in range(2)]
        msk = sb("msk", [P, NT, NE])
        g_a = [sb(f"g_a{i}", [P, NT, NG]) for i in range(4)]
        cum = [sb(f"cum{i}", [P, 8 + NE]) for i in range(2)]
        m1 = sb("m1", [P, NT])
        wt = sb("wt", [P, 2, NT])
        wsum = sb("wsum", [P, NT])
        slot_f = sb("slot_f", [P, 2, NT])
        slot = sb("slot", [P, 2, NT], I32)
        cnt_i = sb("cnt_i", [P, NE], I32)
        more = sb("more", [P, NE + 2], I32)
        first = sb("first", [P, NE + 2], I32)
        stat = sb("stat", [P, NX, 4, NH])
        mx = sb("mx", [P, 2])

        bank = [es.enter_context(nc.psum_tensor(f"bank{i}", [P, HALF], FP32)) for i in range(8)]

        pw1 = R[:, 0:16384].rearrange("p (j h c m) -> p j h c m", j=KD, h=2, m=KD)
        pw2 = R[:, 16384:24576].rearrange("p (m n) -> p m n", m=KD)
        mod0_w = [R[:, 16384 + MOD_THIRD * k:16384 + MOD_THIRD * (k + 1)] for k in range(4)] + \
                 [V[:, MOD_THIRD * k:MOD_THIRD * (k + 1)] for k in range(4)]
        modk_w = [V[:, MOD_THIRD * q:MOD_THIRD * (q + 1)] for q in range(4)] + [E[:, :]]
        hT0 = P1[:, :].rearrange("p (j t) -> p j t", j=KD)
        xn0 = P2[:, :].rearrange("p (t d) -> p t d", t=NT)
        u = P2[:, :].rearrange("p (m t) -> p m t", m=KD)
        modb = P1[:, 0:5 * HALF].rearrange("p (q n) -> p q n", q=5)
        mean, rs, sq0 = (P1[:, HALF * i:HALF * (i + 1)] for i in range(5, 8))
        Vb = V[:, :].rearrange("p (v d) -> p v d", v=8)
        G1b = [Vb[:, 0, :], Vb[:, 1, :]]
        A2b = [Vb[:, 2, :], Vb[:, 3, :]]
        B2b = [Vb[:, 4, :], Vb[:, 5, :]]
        G2b = [Vb[:, 6, :], Vb[:, 7, :]]
        n2b, b2b = E[:, 0:D], E[:, D:2 * D]
        h2 = P1[:, :].rearrange("p (t d) -> p t d", t=NT)
        h2T = [P2[:, :].rearrange("p (j t) -> p j t", j=KD), E[:, :].rearrange("p (j t) -> p j t", j=KD)]
        SLOTW = 12288
        gu_w = [R[:, s * SLOTW:s * SLOTW + 8192].rearrange("p (g k f) -> p g k f", g=2, k=8) for s in range(2)]
        d_w = [R[:, s * SLOTW + 8192:(s + 1) * SLOTW].rearrange("p (k n) -> p k n", k=4) for s in range(2)]
        X = [P2[:, HALF * i:HALF * (i + 1)] for i in range(3)]
        XT = [P2[:, HALF * (3 + i):HALF * (4 + i)].rearrange("p (j h s) -> p j h s", j=4, h=2) for i in range(3)]
        H = [P2[:, 3072 + 256 * i:3072 + 256 * (i + 1)] for i in range(2)]
        HT = [P2[:, 3584 + 256 * i:3584 + 256 * (i + 1)].rearrange("p (j h s) -> p j h s", j=2, h=2) for i in range(2)]
        Y = [E[:, HALF * i:HALF * (i + 1)] for i in range(3)]
        comb = P1[:, :].rearrange("p (t d) -> p t d", t=4)
        hT1 = P2[:, :].rearrange("p (j t) -> p j t", j=KD)
        wqkv = R[:, 0:12288].rearrange("p (j n) -> p j n", j=KD)
        wo = R[:, 12288:20480].rearrange("p (j n) -> p j n", j=KD)
        kd = P1[:, 0:2048].rearrange("p (t k u d) -> p t k u d", t=NT, k=NKV, u=2)
        kT = P1[:, 2048:4096].rearrange("p (k n) -> p k n", k=NKV)
        vv = V[:, 4096:5120].rearrange("p (t n) -> p t n", t=NT)
        qr = V[:, 5120:7168].rearrange("p (t n) -> p t n", t=NX)
        rt = V[:, 7168:8192]
        qT = E[:, :].rearrange("p (j t) -> p j t", j=KD)
        Sm = [R[:, 20480 + HALF * i:20480 + HALF * (i + 1)] for i in range(2)]
        Pm = [R[:, 21504 + HALF * i:21504 + HALF * (i + 1)] for i in range(2)]
        PT = [R[:, 22528 + HALF * i:22528 + HALF * (i + 1)] for i in range(2)]
        mask = R[:, 23552:24576].rearrange("p (b n) -> p b n", b=NX)
        o_t = P2[:, 0:2048].rearrange("p (t n) -> p t n", t=NX)
        oT = P2[:, 2048:4096].rearrange("p (j t) -> p j t", j=KD)
        fin_b = Vb[:, 7, :]
        G1n, B2n, A2n, G2n, n2n = (Vb[:, i, :] for i in range(5))

        c_in, cs_zero, cs_ready = sem("c_in"), sem("cs_zero"), sem("cs_ready")
        x_in = [sem(f"x_in{t}") for t in range(NT)]
        small_in, par_in = sem("small_in"), sem("par_in")
        modb_zero, modb_in = sem("modb_zero"), sem("modb_in")
        mod0_in = [sem(f"mod0_in{i}") for i in range(4)]
        pw1_in, pw2_in = sem("pw1_in"), sem("pw2_in")
        modk_in = [sem(f"modk_in{i}") for i in range(3)]
        mod_used = sem("mod_used")
        mod_done = sem("mod_done")
        mod_row = sem("mod_row")
        mod_out, mods_out = sem("mod_out"), sem("mods_out")
        mod1_in, A1_ready = sem("mod1_in"), sem("A1_ready")
        vec_in, A2_ready = sem("vec_in"), sem("A2_ready")
        ssq_done, sqrt_done, xn_ready = sem("ssq_done"), sem("sqrt_done"), sem("xn_ready")
        xT_ps, hT_act, hT_dve = sem("xT_ps"), sem("hT_act"), sem("hT_dve")
        vpad_zero = sem("vpad_zero")
        g_ps, a_ps, sg_ready, v_ready, conv_done = sem("g_ps"), sem("a_ps"), sem("sg_ready"), sem("v_ready"), sem("conv_done")
        pw1_used, sum_ps, mean_ready = sem("pw1_used"), sem("sum_ps"), sem("mean_ready")
        dif_ready, sq_ready, sq_used, var_ps = sem("dif_ready"), sem("sq_ready"), sem("sq_used"), sem("var_ps")
        std_ready, z_ready, y_ready = sem("std_ready"), sem("z_ready"), sem("y_ready")
        mix_ps, mix_read = sem("mix_ps"), sem("mix_read")
        ssq2_done, sqrt2_done = sem("ssq2_done"), sem("sqrt2_done")
        h2_ready, h2T_ps, h2T_ready, logit_ps = sem("h2_ready"), sem("h2T_ps"), sem("h2T_ready"), sem("logit_ps")
        sig_ready, mask_ready, rank_ps = sem("sig_ready"), sem("mask_ready"), sem("rank_ps")
        routed, scattered = sem("routed"), sem("scattered")
        xs_zero_src, xs_zero = sem("xs_zero_src"), sem("xs_zero")
        L = range(2)
        S2 = range(2)

        def sems(name):
            return [sem(f"{name}{s}") for s in S2]

        gu_in, d_in = sems("gu_in"), sems("d_in")
        gu_ps, d_ps = sems("gu_ps"), sems("d_ps")
        x_tile = sems("x_tile")
        xt_ps, xt_ready = sems("xt_ps"), sems("xt_ready")
        silu_done, h_ready = sems("silu_done"), sems("h_ready")
        ht_ps, ht_ready = sems("ht_ps"), sems("ht_ready")
        y_ready_m, y_out = sems("y_ready_m"), sems("y_out")
        ov = {k: sem(f"further_{k}") for k in ("x", "xt_ps", "xt", "gu", "silu", "h", "ht_ps", "ht", "y_ps", "y", "out")}
        PAIRS = NE // 2
        moe_done = [sem(f"moe_done{l}") for l in L]
        got, comb_read = [sem(f"got{i}") for i in range(2)], sem("comb_read")
        scaled = sem("scaled")
        comb_done = sem("comb_done")
        qkv_in, wo_in, mask_in = sem("qkv_in"), sem("wo_in"), sem("mask_in")
        proj_ps, v_copied, k_ready, kT_ps, kT_ready = sem("proj_ps"), sem("v_copied"), sem("k_ready"), sem("kT_ps"), sem("kT_ready")
        q_ready, qT_ps, qT_ready = sem("q_ready"), sem("qT_ps"), sem("qT_ready")
        s_ps, s_ready, p_ready, pT_ps, pT_ready, o_ps = (sem(n) for n in ("s_ps", "s_ready", "p_ready", "pT_ps", "pT_ready", "o_ps"))
        sinkarg, sinkexp, o_ready, oT_ps, oT_ready = (sem(n) for n in ("sinkarg", "sinkexp", "o_ready", "oT_ps", "oT_ready"))
        vec1_in, fin_in = sem("vec1_in"), sem("fin_in")
        out_ready, out_done = sem("out_ready"), sem("out_done")
        dve_order, act_order = sem("dve_order"), sem("act_order")
        conv_order, tail_order = sem("conv_order"), sem("tail_order")

        block = es.enter_context(nc.Block())

        def row(v, n):
            return v.partition_broadcast(n)

        wg_v = [w_gate[l].rearrange("e (h p j) f -> e p h (j f)", h=2, j=4) for l in L]
        wu_v = [w_up[l].rearrange("e (h p j) f -> e p h (j f)", h=2, j=4) for l in L]
        wd_v = [w_down[l].rearrange("e (h p j) n -> e p h (j n)", h=2, j=2) for l in L]

        @block.sync
        def _(sp):
            for i in range(4):
                for k in (2 * i, 2 * i + 1):
                    sp.dma_start(mod0_w[k], w_mod[0].rearrange("(p k) n -> p k n", k=KD)[:, k, 0:MOD_THIRD]).then_inc(mod0_in[i], 16)
            sp.dma_start(R[:, 0:16384], w_pw1[0].rearrange("(p j) n -> p (j n)", j=KD)).then_inc(pw1_in, 16)
            sp.wait_ge(mod_done, 1)
            with sp.Fori(0, KD) as k:
                w_k = [w_mod[l].rearrange("(p k) n -> k p n", k=KD) for l in L]
                sp.wait_ge(mod_used, k * 3)
                sp.dma_start(V[:, 0:4096], w_k[0][bass.ds(k, 1), :, MOD_THIRD:3 * MOD_THIRD].rearrange("k p n -> (k p) n")).then_inc(modk_in[0], 16)
                sp.wait_ge(mod_used, k * 3)
                sp.dma_start(V[:, 4096:8192], w_k[1][bass.ds(k, 1), :, 0:2 * MOD_THIRD].rearrange("k p n -> (k p) n")).then_inc(modk_in[1], 16)
                sp.dma_start(E[:, :], w_k[1][bass.ds(k, 1), :, 2 * MOD_THIRD:3 * MOD_THIRD].rearrange("k p n -> (k p) n")).then_inc(modk_in[2], 16)
            sp.dma_start(R[:, 16384:24576], w_pw2[0].rearrange("(p m) n -> p (m n)", m=KD)).then_inc(pw2_in, 16)

            extra = [sp.alloc_register(f"further{s}") for s in S2]
            for s in S2:
                sp.reg_mov(extra[s], 0)

            def count_pair(i, l):
                for s in S2:
                    n = sp.value_load(more[0:1, bass.ds(2 * i + s, 1)], min_val=0, max_val=MAXJ[l] - 1)
                    sp.reg_add(extra[s], extra[1 - s], n)

            def moe_weights(l):
                def gate_up(e, s):
                    for g, w in ((0, wg_v[l]), (1, wu_v[l])):
                        sp.dma_start(gu_w[s][:, g, :, :].rearrange("p (h j) f -> p h (j f)", h=2),
                                     w[bass.ds(e, 1)].rearrange("e p h n -> (e p) h n")).then_inc(gu_in[s], 16)

                def down(e, s):
                    sp.dma_start(d_w[s].rearrange("p (h j) n -> p h (j n)", h=2),
                                 wd_v[l][bass.ds(e, 1)].rearrange("e p h n -> (e p) h n")).then_inc(d_in[s], 16)

                if l == 0:
                    sp.wait_ge(pw1_used, 1)
                else:
                    sp.wait_ge(proj_ps, 8)
                gate_up(0, 0)
                down(0, 0)
                sp.wait_ge(mix_ps, NT if l == 0 else NT + NX)
                gate_up(1, 1)
                down(1, 1)
                sp.wait_ge(routed, l + 1)
                with sp.Fori(1, NE // 2) as i:
                    count_pair(i - 1, l)
                    served = [sp.snap(extra[s]) for s in S2]
                    for s in S2:
                        sp.wait_ge(gu_ps[s], PAIRS * l + i)
                        sp.wait_ge(ov["gu"], served[s])
                        gate_up(2 * i + s, s)
                    for s in S2:
                        sp.wait_ge(d_ps[s], PAIRS * l + i)
                        sp.wait_ge(ov["y_ps"], served[s])
                        down(2 * i + s, s)
                if l == 0:
                    count_pair(PAIRS - 1, l)

            moe_weights(0)
            sp.wait_ge(moe_done[0], 1)
            sp.dma_start(R[:, 0:12288], w_qkv[0].rearrange("(p j) n -> p (j n)", j=KD)).then_inc(qkv_in, 16)
            sp.dma_start(wo, w_o[0].rearrange("(j p) n -> p j n", p=P)).then_inc(wo_in, 16)
            sp.dma_start(R[:, 23552:24576], mask_c).then_inc(mask_in, 16)
            moe_weights(1)
            for t in range(NX):
                sp.wait_ge(out_ready, t + 1)
                sp.dma_start(out[0, t * P:(t + 1) * P, :], xr[:, t, :]).then_inc(out_done, 16)
            sp.wait_ge(out_done, 16 * NX)

        @block.gpsimd
        def _(pool):
            further = pool.alloc_register("further_pool")
            pool.reg_mov(further, 0)
            nc.gpsimd.memset(cs[:, :, :], 0.0).then_inc(cs_zero, 1)
            nc.gpsimd.memset(eps_t[:, :], EPS).then_inc(cs_zero, 1)
            nc.gpsimd.memset(modb[:, 0, :], 0.0).then_inc(modb_zero, 1)
            nc.gpsimd.memset(vpad[:, :, :, :], 0.0).then_inc(vpad_zero, 1)
            nc.gpsimd.memset(more[:, :], 0).then_inc(vpad_zero, 1)
            nc.gpsimd.memset(first[:, :], 0).then_inc(vpad_zero, 1)
            for i in range(2):
                nc.gpsimd.memset(cum[i][:, :], 0.0).then_inc(vpad_zero, 1)
            nc.gpsimd.memset(zrow[:, :], 0.0).then_inc(xs_zero_src, 1)
            pool.dma_start(small[:, :], small_c).then_inc(small_in, 16)

            def bias_rows(slot0, third):
                for g in range(4):
                    src = b_mod[third // 3:third // 3 + 1, (third % 3) * MOD_THIRD + g * HALF:(third % 3) * MOD_THIRD + (g + 1) * HALF]
                    pool.dma_start(modb[32 * g:32 * g + 2, slot0, :], src.broadcast_to([2, HALF])).then_inc(modb_in, 16)

            pool.wait_ge(modb_zero, 1)
            bias_rows(0, 0)
            loads = [(b1_c, b_pw1[0].rearrange("(h p m) -> p h m", h=2, m=KD)), (bdw_c, b_dw[0].rearrange("(p m) -> p m", m=KD)),
                     (lng_c, ln_g[0].rearrange("(p m) -> p m", m=KD)), (lnb_c, ln_b[0].rearrange("(p m) -> p m", m=KD)),
                     (n1_c, norm1_g.rearrange("l (p m) -> p l m", m=KD)),
                     (wdw[:, :, :], w_dw[0].rearrange("k (p m) -> p k m", m=KD)),
                     (rw[:, :, :], router_w.rearrange("(p m) e -> p m e", m=KD)),
                     (rb[:, :], row(router_b, P)), (sink_b[:, :], row(sink[0], P))]
            for dst, src in loads:
                pool.dma_start(dst, src).then_inc(par_in, 16)

            until = pool.alloc_register("until")

            def wait_count(signal, count):
                pool.reg_mov(until, count)
                pool.wait_ge(routed, 1)
                pool.wait_ge(signal, until)

            def shift_scale(l):
                pool.dma_start(mod1[:, l].rearrange("p r v j -> p (r v) j"),
                               mod_d[3 * l].rearrange("r (v p j) -> p (r v) j", v=2, j=KD)).then_inc(mod1_in, 16)

            pool.wait_ge(mod_out, 64)
            shift_scale(0)
            pool.wait_ge(xs_zero_src, 1)
            pool.wait_ge(v_ready, 2)
            pool.dma_start(xs_d[0:ROWS, :].rearrange("(p a) (b n) -> p (a b) n", p=P, n=HALF),
                           zrow[:, :].unsqueeze(1).to_broadcast([P, ROWS // P * 2, HALF])).then_inc(xs_zero, 16)
            pool.wait_ge(pw1_used, 1)
            nc.gpsimd.memset(modb[:, :, :], 0.0).then_inc(modb_zero, 1)
            pool.wait_ge(modb_zero, 2)
            for third in range(1, 6):
                bias_rows(third - 1, third)
            pool.wait_ge(mod_row, 2)
            for g in range(4):
                pool.dma_start(mod_d[1:6, :, g * HALF:(g + 1) * HALF].rearrange("q r n -> r q n"), modb[32 * g:32 * g + 2, :, :]).then_inc(mods_out, 16)
            pool.wait_ge(mods_out, 64)
            shift_scale(1)
            vecs = [(G1b, 1, 0), (B2b, 1, D), (A2b, 2, 0), (G2b, 2, D)]
            for dst, third, off in vecs:
                for r in range(2):
                    pool.dma_start(dst[r], row(mod_d[third, r, off:off + D], P)).then_inc(vec_in, 16)
            pool.dma_start(n2b, row(norm2_g[0], P)).then_inc(vec_in, 16)
            pool.dma_start(b2b, row(b_pw2[0], P)).then_inc(vec_in, 16)

            def moe_rows(l):
                nt = NTOK[l] // P
                pool.wait_ge(routed, l + 1)
                if l == 0:
                    pool.wait_ge(xs_zero, 16)
                for k in range(2):
                    for t in range(nt):
                        pool.indirect_dma_start(xs_d[0:ROWS, :], bass.IndirectOffsetOnAxis(ap=slot[:, k, t:t + 1].bitcast(mybir.dt.uint32), axis=0),
                                                h2[:, t, :], None).then_inc(scattered, 16)
                if l == 0:
                    for dst, src in [(G1n, mod_d[4, 0, 0:D]), (B2n, mod_d[4, 0, D:2 * D]), (A2n, mod_d[5, 0, 0:D]),
                                     (G2n, mod_d[5, 0, D:2 * D]), (n2n, norm2_g[1])]:
                        pool.dma_start(dst, row(src, P)).then_inc(vec1_in, 16)
                else:
                    pool.dma_start(fin_b, row(final_g, P)).then_inc(fin_in, 16)
                pool.wait_ge(scattered, 32 * (nt if l == 0 else NT + NX))

                def load_rows(dst, at, signal):
                    for h in range(2):
                        pool.dma_start(dst[h * TILE:(h + 1) * TILE, :], xs_d[bass.ds(at, TILE), h * HALF:(h + 1) * HALF]).then_inc(signal, 16)

                def store_rows(src, at, signal):
                    for h in range(2):
                        pool.dma_start(xs_d[bass.ds(at, TILE), h * HALF:(h + 1) * HALF], src[h * TILE:(h + 1) * TILE, :]).then_inc(signal, 16)

                for s in S2:
                    at = pool.value_load(first[0:1, s:s + 1], min_val=0, max_val=ROWS - TILE)
                    load_rows(X[s], at, x_tile[s])
                with pool.Fori(0, NE // 2) as i:
                    for s in S2:
                        wait_count(xt_ps[s], (PAIRS + 1) * l + i + 1)
                        at = pool.value_load(first[0:1, bass.ds(2 * i + 2 + s, 1)], min_val=0, max_val=ROWS - TILE)
                        load_rows(X[s], at, x_tile[s])
                    for s in S2:
                        e = 2 * i + s
                        at = pool.value_load(first[0:1, bass.ds(e, 1)], min_val=0, max_val=ROWS - TILE)
                        n = pool.value_load(more[0:1, bass.ds(e, 1)], min_val=0, max_val=MAXJ[l] - 1)
                        wait_count(y_ready_m[s], PAIRS * l + i + 1)
                        store_rows(Y[s], at, y_out[s])
                        with pool.If(n > 0):
                            with pool.Fori(1, MAXJ[l]) as j:
                                with pool.If(j < n + 1):
                                    q = pool.snap(further)
                                    row0 = pool.snap(at + j * TILE)
                                    wait_count(ov["xt_ps"], q)
                                    load_rows(X[2], row0, ov["x"])
                                    wait_count(ov["y"], q + 1)
                                    store_rows(Y[2], row0, ov["out"])
                                    pool.reg_add(further, further, 1)
                for s in S2:
                    pool.wait_ge(y_out[s], 32 * PAIRS * (l + 1))
                wait_count(ov["out"], 32 * pool.snap(further))
                for t in range(nt):
                    b = t % 2
                    if t >= 2:
                        pool.wait_ge(xT_ps, NT + t - 1)
                    for k in range(2):
                        pool.indirect_dma_start(comb[:, 2 * b + k, :], None, xs_d[0:ROWS, :],
                                                bass.IndirectOffsetOnAxis(ap=slot[:, k, t:t + 1].bitcast(mybir.dt.uint32), axis=0)).then_inc(got[b], 16)

            moe_rows(0)
            moe_rows(1)

        @block.scalar
        def _(act):
            further = act.alloc_register("further_act")
            act.reg_mov(further, 0)
            order = Order(act, act_order)
            for r, v in ((0, c[0]), (1, c_ctx)):
                act.dma_start(cT[:, r, :], v.rearrange("(p j) -> p j", j=KD)).then_inc(c_in, 16)
            for t in range(NT):
                act.dma_start(xr[:, t, :], x_src[t]).then_inc(x_in[t], 16)
            act.wait_ge(c_in, 32)
            act.wait_ge(cs_zero, 2)
            nc.scalar.activation(cs[:, :, 0:2].rearrange("p j r -> p r j"), cT[:, :, :], ACT.Silu).then_inc(cs_ready, 1)
            for t in range(NT):
                act.wait_ge(x_in[t], 16)
                nc.scalar.activation(xn0[:, t, :], xr[:, t, :], ACT.Square, accum_out=ssq[:, t:t + 1]).then_inc(ssq_done, 1)
            act.wait_ge(ssq_done, NT)
            nc.scalar.activation(rstd[:, :], ssq[:, :], ACT.Sqrt, bias=eps_t[:, 0:1], scale=1.0 / D).then_inc(sqrt_done, 1)
            act.wait_ge(mod_row, 1)
            for g in range(4):
                act.dma_start(mod_d[0, :, g * HALF:(g + 1) * HALF], modb[32 * g:32 * g + 2, 0, :]).then_inc(mod_out, 16)

            def modulated(l, hT, t, n):
                act.wait_ge(xT_ps, n)
                for j in range(KD // 2):
                    last = nc.scalar.activation(hT[:, j, t * P:(t + 1) * P], bank[2 * t][:, j * P:(j + 1) * P],
                                                ACT.Identity, bias=mod1[:, l, t // NX, 0, j:j + 1], scale=A1[:, l, t // NX, j:j + 1])
                last.then_inc(hT_act, 1)

            act.wait_ge(A1_ready, 1)
            for n, t in enumerate(FIRST_ORDER):
                modulated(0, hT0, t, n + 1)
            act.wait_ge(par_in, 16 * 9)
            with act.Fori(0, KD) as m:
                act.wait_ge(g_ps, m + 1)
                act.wait_ge(v_ready, m)
                nc.scalar.activation(sg[:, :], bank[6][:, :], ACT.Sigmoid, bias=b1_c[:, 1, bass.ds(m, 1)]).then_inc(sg_ready, 1)
            act.wait_ge(sum_ps, 1)
            nc.scalar.activation(mean, bank[7][:, :], ACT.Copy, scale=1.0 / D).then_inc(mean_ready, 1)
            sq = [sq0, sg[:, :]]
            for m in range(KD):
                act.wait_ge(dif_ready, m + 1)
                if m >= 2:
                    act.wait_ge(sq_used, m - 1)
                nc.scalar.activation(sq[m % 2], u[:, m, :], ACT.Square).then_inc(sq_ready, 1)
            act.wait_ge(var_ps, 1)
            nc.scalar.activation(rs, bank[7][:, :], ACT.Sqrt, bias=eps_t[:, 0:1], scale=1.0 / D).then_inc(std_ready, 1)
            for m in range(KD):
                act.wait_ge(z_ready, m + 1)
                nc.scalar.activation(u[:, m, :], u[:, m, :], ACT.Silu, bias=lnb_c[:, m:m + 1], scale=lng_c[:, m:m + 1]).then_inc(y_ready, 1)

            def second_norm(l, ts, base):
                for n, t in enumerate(ts):
                    act.wait_ge(mix_read, base + n + 1)
                    nc.scalar.activation(h2[:, t, :], xr[:, t, :], ACT.Square, accum_out=ssq[:, t:t + 1]).then_inc(ssq2_done, 1)
                    act.wait_ge(ssq2_done, base + n + 1)
                    nc.scalar.activation(rstd[:, t:t + 1], ssq[:, t:t + 1], ACT.Sqrt, bias=eps_t[:, 0:1], scale=1.0 / D).then_inc(sqrt2_done, 1)
                for n, t in enumerate(ts):
                    act.wait_ge(h2T_ps, base + n + 1)
                    for half in range(2):
                        last = nc.scalar.activation(h2T[l][:, 4 * half:4 * half + 4, t * P:(t + 1) * P],
                                                    bank[2 * t + half][:, :].rearrange("p (j t) -> p j t", j=4), ACT.Copy)
                    last.then_inc(h2T_ready, 1)
                nt = len(ts)
                act.wait_ge(logit_ps, l + 1)
                nc.scalar.activation(lg_s[:, 0:nt, :], bank[0][:, 0:nt * NE].rearrange("p (t e) -> p t e", t=nt), ACT.Sigmoid).then_inc(sig_ready, 1)

            def moe_act(l):
                act.wait_ge(routed, l + 1)
                with act.Fori(0, NE // 2) as i:
                    for s in S2:
                        act.wait_ge(gu_ps[s], PAIRS * l + i + 1)
                        nc.scalar.activation(H[s], bank[s][:, 0:256], ACT.Silu).then_inc(silu_done[s], 1)
                    for s in S2:
                        n = act.value_load(more[0:1, bass.ds(2 * i + s, 1)], min_val=0, max_val=MAXJ[l] - 1)
                        act.wait_ge(d_ps[s], PAIRS * l + i + 1)
                        act.wait_ge(y_out[s], 32 * (PAIRS * l + i))
                        nc.scalar.activation(Y[s], bank[2 + s][:, :], ACT.Copy).then_inc(y_ready_m[s], 1)
                        with act.If(n > 0):
                            with act.Fori(1, MAXJ[l]) as j:
                                with act.If(j < n + 1):
                                    q = act.snap(further)
                                    act.wait_ge(ov["gu"], q + 1)
                                    nc.scalar.activation(H[s], bank[s][:, 0:256], ACT.Silu).then_inc(ov["silu"], 1)
                                    act.wait_ge(ov["y_ps"], q + 1)
                                    act.wait_ge(ov["out"], q * 32)
                                    nc.scalar.activation(Y[2], bank[2 + s][:, :], ACT.Copy).then_inc(ov["y"], 1)
                                    act.reg_add(further, further, 1)

            def combine_act(t, n):
                b = t % 2
                act.wait_ge(got[b], 32 * n)
                nc.scalar.activation(comb[:, 2 * b, :], comb[:, 2 * b, :], ACT.Copy, scale=wt[:, 0, t:t + 1]).then_inc(scaled, 1)

            second_norm(0, range(NT), 0)
            moe_act(0)
            for t in range(NT):
                combine_act(t, t // 2 + 1)
                act.wait_ge(comb_done, t + 1)
                nc.scalar.activation(comb[:, 2 * (t % 2) + 1, :], xr[:, t, :], ACT.Square, accum_out=ssq[:, t:t + 1]).then_inc(ssq_done, 1)
                act.wait_ge(ssq_done, NT + t + 1)
                nc.scalar.activation(rstd[:, t:t + 1], ssq[:, t:t + 1], ACT.Sqrt, bias=eps_t[:, 0:1], scale=1.0 / D).then_inc(sqrt_done, 1)
                act.wait_ge(A1_ready, 2)
                modulated(1, hT1, t, NT + t + 1)
            for n, (t, b) in enumerate(KV_BANKS):
                act.wait_ge(proj_ps, n + 1)
                nc.scalar.activation(vv[:, t, :], bank[b][:, 256:512], ACT.Copy).then_inc(v_copied, 1)
            for n, (t, b) in enumerate(KV_BANKS):
                act.wait_ge(kT_ps, n + 1)
                nc.scalar.activation(kT[:, :, t * P:(t + 1) * P], bank[b][:, :].rearrange("p (k t) -> p k t", k=NKV), ACT.Copy).then_inc(kT_ready, 1)
            for n, (t, h, b) in enumerate(Q_BANKS):
                act.wait_ge(qT_ps, n + 1)
                nc.scalar.activation(qT[:, 4 * h:4 * h + 4, t * P:(t + 1) * P], bank[b][:, :].rearrange("p (k t) -> p k t", k=4), ACT.Copy).then_inc(qT_ready, 1)

            def probs(n):
                b, h = n // NH, n % NH
                act.wait_ge(s_ready, n + 1)
                if n >= 2:
                    act.wait_ge(pT_ps, n - 1)
                nc.scalar.activation(Pm[n % 2], Sm[n % 2], ACT.Exp, bias=stat[:, b, 1, h:h + 1],
                                     accum_out=stat[:, b, 0, h:h + 1]).then_inc(p_ready, 1)

            def probs_T(n):
                act.wait_ge(pT_ps, n + 1)
                if n >= 2:
                    act.wait_ge(o_ps, n - 1)
                nc.scalar.activation(PT[n % 2], bank[4 + 2 * (n % 2)][:, :], ACT.Copy).then_inc(pT_ready, 1)

            for n in range(NX * NH):
                probs(n)
                if n:
                    probs_T(n - 1)
            probs_T(NX * NH - 1)
            act.wait_ge(sinkarg, 1)
            nc.scalar.activation(stat[:, :, 2, :], stat[:, :, 2, :], ACT.Exp).then_inc(sinkexp, 1)
            for t in range(NX):
                for h in range(2):
                    act.wait_ge(oT_ps, 2 * t + h + 1)
                    nc.scalar.activation(oT[:, 4 * h:4 * h + 4, t * P:(t + 1) * P], bank[4 * t + 2 * h + 1][:, :].rearrange("p (k t) -> p k t", k=4), ACT.Copy).then_inc(oT_ready, 1)
            second_norm(1, range(NX), NT)
            moe_act(1)
            for t in range(NX):
                combine_act(t, NT // 2 + 1)
                act.wait_ge(comb_done, NT + t + 1)
                nc.scalar.activation(comb[:, 2 * t + 1, :], xr[:, t, :], ACT.Square, accum_out=ssq[:, t:t + 1]).then_inc(ssq_done, 1)
                act.wait_ge(ssq_done, 2 * NT + t + 1)
                nc.scalar.activation(rstd[:, t:t + 1], ssq[:, t:t + 1], ACT.Sqrt, bias=eps_t[:, 0:1], scale=1.0 / D).then_inc(sqrt_done, 1)

        @block.tensor
        def _(pe):
            further = pe.alloc_register("further_pe")
            pe.reg_mov(further, 0)
            def transposes(dst, srcs, signal):
                for i, src in enumerate(srcs):
                    last = nc.tensor.transpose(dst[:, i * P:(i + 1) * P], src, ident)
                last.then_inc(signal, 1)

            def rows_T(t, rows, signal):
                v = rows.rearrange("p (c j) -> p j c", j=KD)
                for j in range(KD):
                    last = nc.tensor.transpose(bank[2 * t + j // 4][:, (j % 4) * P:(j % 4 + 1) * P], v[:, j, :], ident)
                last.then_inc(signal, 1)

            pe.wait_ge(small_in, 16)
            for n, t in enumerate(FIRST_ORDER[:3]):
                pe.wait_ge(xn_ready, n + 1)
                rows_T(t, xn0[:, t, :], xT_ps)
            pe.wait_ge(cs_ready, 1)
            for k in range(KD):
                pe.wait_ge(mod0_in[k // 2], 32)
                for g in range(4):
                    last = nc.tensor.matmul(bank[0][32 * g:32 * g + 32, :], cs[:, k, :], mod0_w[k][:, g * HALF:(g + 1) * HALF],
                                            start=(k == 0), stop=(k == KD - 1))
            last.then_inc(mod_done, 1)
            pe.wait_ge(mod_row, 1)
            pe.wait_ge(xn_ready, NT)
            rows_T(0, xn0[:, 0, :], xT_ps)

            pe.wait_ge(hT_act, NT)
            pe.wait_ge(hT_dve, NT)
            pe.wait_ge(pw1_in, 16)
            for m in range(KD):
                for half, b, signal in ((1, 6, g_ps), (0, 5, a_ps)):
                    if m and half:
                        pe.wait_ge(sg_ready, m)
                    elif m:
                        pe.wait_ge(v_ready, m)
                    for j in range(KD):
                        last = nc.tensor.matmul(bank[b][:, :], pw1[:, j, half, :, m], hT0[:, j, :], start=(j == 0), stop=(j == KD - 1))
                    last.then_inc(signal, 1)
                for q in range(5):
                    pe.wait_ge(modk_in[(0, 0, 1, 1, 2)[q]], 16 * (m + 1))
                    for g in range(4):
                        last = nc.tensor.matmul(bank[q][32 * g:32 * g + 32, :], cs[:, m, :], modk_w[q][:, g * HALF:(g + 1) * HALF],
                                                start=(m == 0), stop=(m == KD - 1))
                    if q in (1, 3, 4):
                        last.then_inc(mod_used, 1)
                if m:
                    pe.wait_ge(conv_done, m)
                    last = nc.tensor.matmul(bank[7][:, :], ones, u[:, m - 1, :], start=(m == 1), stop=False)
                if m == KD - 1:
                    last.then_inc(pw1_used, 1)
            pe.wait_ge(conv_done, KD)
            nc.tensor.matmul(bank[7][:, :], ones, u[:, KD - 1, :], start=False, stop=True).then_inc(sum_ps, 1)
            for m in range(KD):
                pe.wait_ge(sq_ready, m + 1)
                last = nc.tensor.matmul(bank[7][:, :], ones, [sq0, sg[:, :]][m % 2], start=(m == 0), stop=(m == KD - 1))
                last.then_inc(sq_used if m < KD - 1 else var_ps, 1)

            def project(lhs, rhs, ts):
                for t in ts:
                    for half in range(2):
                        for j in range(KD):
                            last = nc.tensor.matmul(bank[2 * t + half][:, :], lhs[:, j, t * P:(t + 1) * P],
                                                    rhs[:, j, half * HALF:(half + 1) * HALF], start=(j == 0), stop=(j == KD - 1))
                    last.then_inc(mix_ps, 1)

            def router(l, ts, base):
                for n, t in enumerate(ts):
                    pe.wait_ge(h2_ready, base + n + 1)
                    rows_T(t, h2[:, t, :], h2T_ps)
                pe.wait_ge(h2T_ready, base + len(ts))
                for t in ts:
                    for j in range(KD):
                        last = nc.tensor.matmul(bank[0][:, t * NE:(t + 1) * NE], h2T[l][:, j, t * P:(t + 1) * P], rw[:, j, :],
                                                start=(j == 0), stop=(j == KD - 1))
                last.then_inc(logit_ps, 1)
                pe.wait_ge(mask_ready, l + 1)
                nt = len(ts)
                for t in range(nt + 1):
                    own = [(ones, i) for i in range(min(t, nt))] + ([(before, t)] if t < nt else [])
                    for i, (w, c) in enumerate(own):
                        last = nc.tensor.matmul(bank[1][:, t * NE:(t + 1) * NE], w, msk[:, c, :], start=(i == 0), stop=(i == len(own) - 1))
                last.then_inc(rank_ps, 1)

            def gate_up(s, xt, signal):
                for h in range(2):
                    for j in range(4):
                        for fh in range(2):
                            last = nc.tensor.matmul(bank[s][TILE * fh:TILE * (fh + 1), :].rearrange("p (g f) -> p g f", g=2), XT[xt][:, j, h, :],
                                                    gu_w[s][:, :, 4 * h + j, fh * 256:(fh + 1) * 256], start=(h + j == 0), stop=(h + j == 4))
                last.then_inc(signal, 1)

            def down(s, signal):
                for h in range(2):
                    for j in range(2):
                        for nh in range(2):
                            last = nc.tensor.matmul(bank[2 + s][TILE * nh:TILE * (nh + 1), :], HT[s][:, j, h, :],
                                                    d_w[s][:, 2 * h + j, nh * HALF:(nh + 1) * HALF], start=(h + j == 0), stop=(h + j == 2))
                last.then_inc(signal, 1)

            def x_T(i, s, signal):
                transposes(bank[4 + s], [X[i].rearrange("p (c j) -> p j c", j=4)[:, j, :] for j in range(4)], signal)

            def h_T(s, signal):
                transposes(bank[6 + s], [H[s].rearrange("p (c j) -> p j c", j=2)[:, j, :] for j in range(2)], signal)

            def moe(l):
                pe.wait_ge(routed, l + 1)
                for s in S2:
                    pe.wait_ge(x_tile[s], 32 * (PAIRS + 1) * l + 32)
                    x_T(s, s, xt_ps[s])
                with pe.Fori(0, NE // 2) as i:
                    for s in S2:
                        pe.wait_ge(gu_in[s], 32 * (PAIRS * l + i + 1))
                        pe.wait_ge(xt_ready[s], (PAIRS + 1) * l + i + 1)
                        pe.wait_ge(h_ready[s], PAIRS * l + i)
                        gate_up(s, s, gu_ps[s])
                    for s in S2:
                        n = pe.value_load(more[0:1, bass.ds(2 * i + s, 1)], min_val=0, max_val=MAXJ[l] - 1)
                        pe.wait_ge(h_ready[s], PAIRS * l + i + 1)
                        pe.wait_ge(ht_ready[s], PAIRS * l + i)
                        h_T(s, ht_ps[s])
                        pe.wait_ge(x_tile[s], 32 * ((PAIRS + 1) * l + i + 2))
                        x_T(s, s, xt_ps[s])
                        pe.wait_ge(d_in[s], 16 * (PAIRS * l + i + 1))
                        pe.wait_ge(ht_ready[s], PAIRS * l + i + 1)
                        pe.wait_ge(y_ready_m[s], PAIRS * l + i)
                        down(s, d_ps[s])
                        with pe.If(n > 0):
                            with pe.Fori(1, MAXJ[l]) as j:
                                with pe.If(j < n + 1):
                                    q = pe.snap(further)
                                    pe.wait_ge(ov["x"], 32 * q + 32)
                                    pe.wait_ge(xt_ready[s], (PAIRS + 1) * l + i + 2)
                                    x_T(2, s, ov["xt_ps"])
                                    pe.wait_ge(ov["xt"], q + 1)
                                    gate_up(s, 2, ov["gu"])
                                    pe.wait_ge(ov["h"], q + 1)
                                    h_T(s, ov["ht_ps"])
                                    pe.wait_ge(ov["ht"], q + 1)
                                    pe.wait_ge(y_ready_m[s], PAIRS * l + i + 1)
                                    down(s, ov["y_ps"])
                                    pe.wait_ge(ov["y"], q + 1)
                                    pe.reg_add(further, further, 1)
                pe.wait_ge(y_ready_m[0], PAIRS * (l + 1))
                pe.wait_ge(y_ready_m[1], PAIRS * (l + 1))
                nc.tensor.transpose(bank[6][:, 0:P], ident, ident).then_inc(moe_done[l], 1)

            pe.wait_ge(y_ready, KD)
            pe.wait_ge(mod_row, 2)
            pe.wait_ge(pw2_in, 16)
            project(u, pw2, range(NT))
            router(0, range(NT), 0)
            moe(0)
            for t in range(NT):
                pe.wait_ge(xn_ready, NT + t + 1)
                rows_T(t, comb[:, 2 * (t % 2), :], xT_ps)
            pe.wait_ge(hT_act, 2 * NT)
            pe.wait_ge(hT_dve, 2 * NT)
            pe.wait_ge(qkv_in, 16)
            for t, b, n0 in [(t, b, 2) for t, b in KV_BANKS] + [(t, b, h) for t, h, b in Q_BANKS]:
                for j in range(KD):
                    last = nc.tensor.matmul(bank[b][:, :], hT1[:, j, t * P:(t + 1) * P], wqkv[:, j, n0 * HALF:(n0 + 1) * HALF],
                                            start=(j == 0), stop=(j == KD - 1))
                last.then_inc(proj_ps, 1)
            for n, (t, b) in enumerate(KV_BANKS):
                pe.wait_ge(k_ready, n + 1)
                transposes(bank[b], [kd[:, t, k, :, :].rearrange("p u d -> p (u d)") for k in range(NKV)], kT_ps)
            for n, (t, h, b) in enumerate(Q_BANKS):
                pe.wait_ge(q_ready, n + 1)
                transposes(bank[b], [qr[:, t, (4 * h + i) * P:(4 * h + i + 1) * P] for i in range(4)], qT_ps)
            pe.wait_ge(kT_ready, NT)
            pe.wait_ge(qT_ready, 4)

            def scores(n):
                b, h = n // NH, n % NH
                r = (h % 2) * HD
                if n >= 2:
                    pe.wait_ge(s_ready, n - 1)
                nc.tensor.matmul(bank[2 * (n % 2)][:, :], qT[r:r + HD, h // 2, b * P:(b + 1) * P], kT[r:r + HD, h // GROUP, :],
                                 start=True, stop=True).then_inc(s_ps, 1)

            def values(n):
                b, h = n // NH, n % NH
                pe.wait_ge(pT_ready, n + 1)
                at = bank[4 * b + 1 + 2 * (h // 8)][:, (h % 8) * HD:(h % 8 + 1) * HD]
                for k in range(4):
                    last = nc.tensor.matmul(at, PT[n % 2][:, k * P:(k + 1) * P], vv[:, k, (h // GROUP) * HD:(h // GROUP + 1) * HD],
                                            start=(k == 0), stop=(k == 3))
                last.then_inc(o_ps, 1)

            scores(0)
            for n in range(NX * NH):
                if n + 1 < NX * NH:
                    scores(n + 1)
                if n:
                    values(n - 1)
                pe.wait_ge(p_ready, n + 1)
                if n >= 2:
                    pe.wait_ge(pT_ready, n - 1)
                transposes(bank[4 + 2 * (n % 2)], [Pm[n % 2][:, k * P:(k + 1) * P] for k in range(4)], pT_ps)
            values(NX * NH - 1)
            for t in range(NX):
                for h in range(2):
                    pe.wait_ge(o_ready, 2 * t + h + 1)
                    transposes(bank[4 * t + 2 * h + 1], [o_t[:, t, (4 * h + i) * P:(4 * h + i + 1) * P] for i in range(4)], oT_ps)
            pe.wait_ge(oT_ready, 4)
            pe.wait_ge(wo_in, 16)
            project(oT, wo, range(NX))
            router(1, range(NX), NT)
            moe(1)

        @block.vector
        def _(dve):
            further = dve.alloc_register("further_dve")
            dve.reg_mov(further, 0)
            order = Order(dve, dve_order)
            step = order.step
            V_ = nc.vector

            dve.wait_ge(sqrt_done, 1)
            step(V_.reciprocal(rstd[:, :], rstd[:, :]))
            for t in FIRST_ORDER:
                V_.tensor_scalar(xn0[:, t, :], xr[:, t, :], rstd[:, t:t + 1], None, ALU.mult).then_inc(xn_ready, 1)
            dve.wait_ge(mod_done, 1)
            dve.wait_ge(modb_in, 64)
            V_.tensor_tensor(modb[:, 0, :], bank[0][:, :], modb[:, 0, :], ALU.add).then_inc(mod_row, 1)

            def scale_1(l):
                dve.wait_ge(mod1_in, 16 * (l + 1))
                V_.scalar_tensor_tensor(A1[:, l], mod1[:, l, :, 1, :], 1.0, n1_c[:, l:l + 1, :].to_broadcast([P, 2, KD]),
                                        ALU.add, ALU.mult).then_inc(A1_ready, 1)
                dve.wait_ge(A1_ready, l + 1)

            dve.wait_ge(par_in, 16 * 9)
            scale_1(0)

            def modulated(l, hT, t, n):
                dve.wait_ge(xT_ps, n)
                for j in range(KD // 2, KD):
                    last = V_.tensor_scalar(hT[:, j, t * P:(t + 1) * P], bank[2 * t + 1][:, (j - 4) * P:(j - 3) * P],
                                            A1[:, l, t // NX, j:j + 1], mod1[:, l, t // NX, 0, j:j + 1], ALU.mult, ALU.add)
                last.then_inc(hT_dve, 1)

            for n, t in enumerate(FIRST_ORDER):
                modulated(0, hT0, t, n + 1)

            dve.wait_ge(vpad_zero, 1)
            with dve.Fori(0, KD // 2) as mm:
                conv = Order(dve, conv_order, base=mm * 2 * (TAPS - 1))
                for b in range(2):
                    m = 2 * mm + b
                    dve.wait_ge(a_ps, m + 1)
                    dve.wait_ge(sg_ready, m + 1)
                    V_.scalar_tensor_tensor(vpad[:, b, :, PAD:PAD + SEQ], bank[5][:, :].rearrange("p (s t) -> p s t", s=2),
                                            b1_c[:, 0, bass.ds(m, 1)], sg[:, :].rearrange("p (s t) -> p s t", s=2), ALU.add, ALU.mult).then_inc(v_ready, 1)
                    dve.wait_ge(v_ready, m + 1)
                    um = u[:, bass.ds(m, 1), :].rearrange("p m (s t) -> p (m s) t", s=2)
                    conv.step(V_.tensor_scalar(um, vpad[:, b, :, 0:SEQ], wdw[:, 0, bass.ds(m, 1)], bdw_c[:, bass.ds(m, 1)], ALU.mult, ALU.add))
                    for k in range(1, TAPS - 1):
                        conv.step(V_.scalar_tensor_tensor(um, vpad[:, b, :, k:k + SEQ], wdw[:, k, bass.ds(m, 1)], um, ALU.mult, ALU.add))
                    V_.scalar_tensor_tensor(um, vpad[:, b, :, TAPS - 1:TAPS - 1 + SEQ], wdw[:, TAPS - 1, bass.ds(m, 1)], um, ALU.mult, ALU.add).then_inc(conv_done, 1)

            dve.wait_ge(conv_done, KD)
            dve.wait_ge(mean_ready, 1)
            for m in range(KD):
                V_.tensor_tensor(u[:, m, :], u[:, m, :], mean, ALU.subtract).then_inc(dif_ready, 1)
            dve.wait_ge(modb_in, 64 * 6)
            for q in range(5):
                last = V_.tensor_tensor(modb[:, q, :], bank[q][:, :], modb[:, q, :], ALU.add)
            last.then_inc(mod_row, 1)
            dve.wait_ge(std_ready, 1)
            step(V_.reciprocal(rs, rs))
            for m in range(KD):
                V_.tensor_tensor(u[:, m, :], u[:, m, :], rs, ALU.mult).then_inc(z_ready, 1)

            scale_1(1)
            dve.wait_ge(vec_in, 16 * 10)
            for r in range(2):
                last = V_.scalar_tensor_tensor(A2b[r], A2b[r], 1.0, n2b, ALU.add, ALU.mult)
            last.then_inc(A2_ready, 1)
            dve.wait_ge(A2_ready, 1)

            def residual(l, t, n, G1):
                dve.wait_ge(mix_ps, n)
                for half in range(2):
                    cols = slice(half * HALF, (half + 1) * HALF)
                    if l == 0:
                        step(V_.tensor_tensor(h2[:, t, cols], bank[2 * t + half][:, :], b2b[:, cols], ALU.add))
                        step(V_.tensor_tensor(h2[:, t, cols], h2[:, t, cols], G1[:, cols], ALU.mult))
                    else:
                        step(V_.tensor_tensor(h2[:, t, cols], bank[2 * t + half][:, :], G1[:, cols], ALU.mult))
                V_.tensor_tensor(xr[:, t, :], xr[:, t, :], h2[:, t, :], ALU.add).then_inc(mix_read, 1)

            def second_norm(t, n, A2, B2):
                dve.wait_ge(sqrt2_done, n)
                step(V_.reciprocal(rstd[:, t:t + 1], rstd[:, t:t + 1]))
                step(V_.scalar_tensor_tensor(h2[:, t, :], xr[:, t, :], rstd[:, t:t + 1], A2, ALU.mult, ALU.mult))
                V_.tensor_tensor(h2[:, t, :], h2[:, t, :], B2, ALU.add).then_inc(h2_ready, 1)

            def route(l, nt):
                def e3(x):
                    return x[:, 0:nt, :]

                def g4(x):
                    return x[:, 0:nt, :].rearrange("p t (g e) -> p t g e", g=NG)

                def over_e(x):
                    return x.unsqueeze(2).to_broadcast([P, nt, NE])

                sel, t_b, t_c = e3(r_a), e3(r_b), e3(r_c)
                dve.wait_ge(sig_ready, l + 1)
                step(V_.tensor_tensor(sel, e3(lg_s), rb[:, :].unsqueeze(1).to_broadcast([P, nt, NE]), ALU.add))
                hi, lo, top, sec = (x[:, 0:nt, :] for x in g_a)
                a, b, c_, d = (g4(r_a)[:, :, :, i] for i in range(4))
                pair = g4(r_b)
                step(V_.tensor_tensor(pair[:, :, :, 0], a, b, ALU.max))
                step(V_.tensor_tensor(pair[:, :, :, 1], a, b, ALU.min))
                step(V_.tensor_tensor(pair[:, :, :, 2], c_, d, ALU.max))
                step(V_.tensor_tensor(pair[:, :, :, 3], c_, d, ALU.min))
                step(V_.tensor_tensor(top, pair[:, :, :, 0], pair[:, :, :, 2], ALU.max))
                step(V_.tensor_tensor(hi, pair[:, :, :, 0], pair[:, :, :, 2], ALU.min))
                step(V_.tensor_tensor(lo, pair[:, :, :, 1], pair[:, :, :, 3], ALU.max))
                step(V_.tensor_tensor(sec, hi, lo, ALU.max))
                step(V_.tensor_tensor(top, top, sec, ALU.add))

                def first_max(out, vals, n, desc, tmp):
                    wide = [P, nt, n]
                    mt = m1[:, 0:nt]
                    step(V_.tensor_reduce(mt, vals, AX.X, ALU.max))
                    step(V_.tensor_tensor(tmp, vals, mt.unsqueeze(2).to_broadcast(wide), ALU.is_equal))
                    step(V_.tensor_tensor(tmp, tmp, desc.unsqueeze(1).to_broadcast(wide), ALU.mult))
                    step(V_.tensor_reduce(mt, tmp, AX.X, ALU.max))
                    step(V_.tensor_tensor(out, mt.unsqueeze(2).to_broadcast(wide), desc.unsqueeze(1).to_broadcast(wide), ALU.is_equal))

                first_max(hi, top, NG, down_g, lo)
                step(V_.tensor_scalar(lo, hi, BIG, -BIG, ALU.mult, ALU.add))
                step(V_.tensor_tensor(g4(r_a), g4(r_a), lo.unsqueeze(3).to_broadcast([P, nt, NG, EPG]), ALU.add))
                first_max(e3(oh[0]), sel, NE, down_e, t_b)
                step(V_.scalar_tensor_tensor(sel, e3(oh[0]), -2 * BIG, sel, ALU.mult, ALU.add))
                first_max(e3(oh[1]), sel, NE, down_e, t_b)
                V_.tensor_tensor(e3(msk), e3(oh[0]), e3(oh[1]), ALU.add).then_inc(mask_ready, 1)
                for i in range(2):
                    step(V_.tensor_tensor(t_b, e3(lg_s), e3(oh[i]), ALU.mult))
                    step(V_.tensor_reduce(wt[:, i, 0:nt], t_b, AX.X, ALU.add))
                ws = wsum[:, 0:nt]
                step(V_.tensor_tensor(ws, wt[:, 0, 0:nt], wt[:, 1, 0:nt], ALU.add))
                step(V_.reciprocal(ws, ws))
                step(V_.tensor_tensor(wt[:, :, 0:nt], wt[:, :, 0:nt], ws.unsqueeze(1).to_broadcast([P, 2, nt]), ALU.mult))
                dve.wait_ge(rank_ps, l + 1)
                dve.wait_ge(vpad_zero, 5)
                ranks, total = bank[1][:, 0:nt * NE].rearrange("p (t e) -> p t e", t=nt), bank[1][:, nt * NE:(nt + 1) * NE]
                step(V_.tensor_scalar(cnt_i[:, :], total, -1.0, None, ALU.add))
                step(V_.tensor_single_scalar(cnt_i[:, :], cnt_i[:, :], TILE.bit_length() - 1, ALU.arith_shift_right))
                step(V_.tensor_scalar(more[:, 0:NE], cnt_i[:, :], 0, None, ALU.max))
                step(V_.tensor_scalar(cum[0][:, 8:8 + NE], more[:, 0:NE], 1, None, ALU.add))
                for i, d_ in enumerate((1, 2, 4, 8)):
                    x_, y_ = cum[i % 2], cum[(i + 1) % 2]
                    step(V_.tensor_tensor(y_[:, 8:8 + NE], x_[:, 8:8 + NE], x_[:, 8 - d_:8 + NE - d_], ALU.add))
                step(V_.tensor_scalar(r_c[:, 0, :], cum[0][:, 7:7 + NE], float(TILE), None, ALU.mult))
                step(V_.tensor_copy(first[:, 0:NE], r_c[:, 0, :]))
                step(V_.tensor_tensor(sel, ranks, r_c[:, 0:1, :].to_broadcast([P, nt, NE]), ALU.add))
                for i in range(2):
                    step(V_.tensor_tensor(t_b, sel, e3(oh[i]), ALU.mult))
                    step(V_.tensor_reduce(slot_f[:, i, 0:nt], t_b, AX.X, ALU.add))
                V_.tensor_copy(slot[:, :, 0:nt], slot_f[:, :, 0:nt]).then_inc(routed, 1)
                dve.wait_ge(routed, l + 1)

            def moe_dve(l):

                def xt_copy(i, s):
                    return V_.tensor_copy(XT[i].rearrange("p j h s -> p (j h s)"), bank[4 + s][:, :])

                for s in S2:
                    dve.wait_ge(xt_ps[s], (PAIRS + 1) * l + 1)
                    xt_copy(s, s).then_inc(xt_ready[s], 1)
                with dve.Fori(0, NE // 2) as i:
                    for s in S2:
                        dve.wait_ge(silu_done[s], PAIRS * l + i + 1)
                        V_.tensor_tensor(H[s], H[s], bank[s][:, 256:512], ALU.mult).then_inc(h_ready[s], 1)
                    for s in S2:
                        n = dve.value_load(more[0:1, bass.ds(2 * i + s, 1)], min_val=0, max_val=MAXJ[l] - 1)
                        dve.wait_ge(ht_ps[s], PAIRS * l + i + 1)
                        V_.tensor_copy(HT[s].rearrange("p j h s -> p (j h s)"), bank[6 + s][:, 0:256]).then_inc(ht_ready[s], 1)
                        dve.wait_ge(xt_ps[s], (PAIRS + 1) * l + i + 2)
                        xt_copy(s, s).then_inc(xt_ready[s], 1)
                        with dve.If(n > 0):
                            with dve.Fori(1, MAXJ[l]) as j:
                                with dve.If(j < n + 1):
                                    q = dve.snap(further)
                                    dve.wait_ge(ov["xt_ps"], q + 1)
                                    xt_copy(2, s).then_inc(ov["xt"], 1)
                                    dve.wait_ge(ov["silu"], q + 1)
                                    V_.tensor_tensor(H[s], H[s], bank[s][:, 256:512], ALU.mult).then_inc(ov["h"], 1)
                                    dve.wait_ge(ov["ht_ps"], q + 1)
                                    V_.tensor_copy(HT[s].rearrange("p j h s -> p (j h s)"), bank[6 + s][:, 0:256]).then_inc(ov["ht"], 1)
                                    dve.reg_add(further, further, 1)

            def combine(l, t, n, G2):
                b = t % 2
                dve.wait_ge(scaled, n)
                step(V_.scalar_tensor_tensor(comb[:, 2 * b + 1, :], comb[:, 2 * b + 1, :], wt[:, 1, t:t + 1], comb[:, 2 * b, :], ALU.mult, ALU.add))
                step(V_.tensor_tensor(comb[:, 2 * b + 1, :], comb[:, 2 * b + 1, :], G2, ALU.mult))
                V_.tensor_tensor(xr[:, t, :], xr[:, t, :], comb[:, 2 * b + 1, :], ALU.add).then_inc(comb_done, 1)

            for t in range(NT):
                residual(0, t, t + 1, G1b[t // NX])
                second_norm(t, t + 1, A2b[t // NX], B2b[t // NX])
            route(0, NT)
            moe_dve(0)
            dve.wait_ge(vec1_in, 16 * 5)
            step(V_.scalar_tensor_tensor(A2n, A2n, 1.0, n2n, ALU.add, ALU.mult))
            for t in range(NT):
                combine(0, t, t + 1, G2b[t // NX])
                dve.wait_ge(sqrt_done, 1 + t + 1)
                step(V_.reciprocal(rstd[:, t:t + 1], rstd[:, t:t + 1]))
                V_.tensor_scalar(comb[:, 2 * (t % 2), :], xr[:, t, :], rstd[:, t:t + 1], None, ALU.mult).then_inc(xn_ready, 1)
                modulated(1, hT1, t, NT + t + 1)

            def rotated(dst, raw, n, t, copies):
                a, b = rt[:, 0:n * HD], rt[:, n * HD:2 * n * HD] if copies else None
                cos = rope[:, t, 0, :].unsqueeze(1).to_broadcast([P, n, HD])
                first_half = dst if copies == 0 else a.rearrange("p (k d) -> p k d", d=HD)
                swapped = (a if copies == 0 else b)
                step(V_.tensor_tensor(first_half, raw.rearrange("p (k d) -> p k d", d=HD), cos, ALU.mult))
                src = raw.rearrange("p (k h q i) -> p k h q i", h=2, q=2, i=ROPE_PAIRS)
                to = swapped.rearrange("p (k h q i) -> p k h q i", h=2, q=2, i=ROPE_PAIRS)
                sin = rope[:, t, 1, :].rearrange("p (h q i) -> p h q i", h=2, q=2)
                for q in range(2):
                    step(V_.tensor_tensor(to[:, :, :, q, :], src[:, :, :, 1 - q, :],
                                          sin[:, :, q, :].unsqueeze(1).to_broadcast([P, n, 2, ROPE_PAIRS]), ALU.mult))
                return first_half, swapped.rearrange("p (k d) -> p k d", d=HD)

            for n, (t, b) in enumerate(KV_BANKS):
                dve.wait_ge(v_copied, n + 1)
                if t >= NX:
                    for up in range(2):
                        last = V_.tensor_copy(kd[:, t, :, up, :], bank[b][:, 0:256].rearrange("p (k d) -> p k d", d=HD))
                else:
                    x_, y_ = rotated(None, bank[b][:, 0:256], NKV, t, 2)
                    for up in range(2):
                        last = V_.tensor_tensor(kd[:, t, :, up, :], x_, y_, ALU.add)
                last.then_inc(k_ready, 1)
                dve.wait_ge(k_ready, n + 1)
            for n, (t, h, b) in enumerate(Q_BANKS):
                dve.wait_ge(proj_ps, NT + n + 1)
                to = qr[:, t, h * HALF:(h + 1) * HALF].rearrange("p (k d) -> p k d", d=HD)
                x_, y_ = rotated(to, bank[b][:, :], 8, t, 0)
                V_.tensor_tensor(to, x_, y_, ALU.add).then_inc(q_ready, 1)
                dve.wait_ge(q_ready, n + 1)

            dve.wait_ge(mask_in, 16)
            for n in range(NX * NH):
                b, h = n // NH, n % NH
                dve.wait_ge(s_ps, n + 1)
                if n >= 2:
                    dve.wait_ge(p_ready, n - 1)
                step(V_.tensor_tensor_reduce(out=Sm[n % 2], in0=bank[2 * (n % 2)][:, :], in1=mask[:, b, :], scale=HD ** -0.5,
                                             scalar=-3e38, op0=ALU.add, op1=ALU.max, accum_out=mx[:, n % 2:n % 2 + 1]))
                V_.tensor_scalar(stat[:, b, 1, h:h + 1], mx[:, n % 2:n % 2 + 1], sink_b[:, h:h + 1], -1.0, ALU.max, ALU.mult).then_inc(s_ready, 1)
            dve.wait_ge(s_ready, NX * NH)
            V_.tensor_tensor(stat[:, :, 2, :], stat[:, :, 1, :], sink_b[:, :].unsqueeze(1).to_broadcast([P, NX, NH]), ALU.add).then_inc(sinkarg, 1)
            dve.wait_ge(sinkexp, 1)
            step(V_.tensor_tensor(stat[:, :, 3, :], stat[:, :, 0, :], stat[:, :, 2, :], ALU.add))
            step(V_.reciprocal(stat[:, :, 3, :], stat[:, :, 3, :]))
            dve.wait_ge(o_ps, NX * NH)
            for t in range(NX):
                for h in range(2):
                    V_.tensor_tensor(o_t[:, t, h * HALF:(h + 1) * HALF].rearrange("p (k d) -> p k d", d=HD),
                                     bank[4 * t + 1 + 2 * h][:, :].rearrange("p (k d) -> p k d", d=HD),
                                     stat[:, t, 3, 8 * h:8 * h + 8].unsqueeze(2).to_broadcast([P, 8, HD]), ALU.mult).then_inc(o_ready, 1)
            for t in range(NX):
                residual(1, t, NT + t + 1, G1n)
                second_norm(t, NT + t + 1, A2n, B2n)
            route(1, NX)
            moe_dve(1)
            dve.wait_ge(fin_in, 16)
            for t in range(NX):
                combine(1, t, NT + t + 1, G2n)
                dve.wait_ge(sqrt_done, 1 + NT + t + 1)
                step(V_.reciprocal(rstd[:, t:t + 1], rstd[:, t:t + 1]))
                V_.scalar_tensor_tensor(xr[:, t, :], xr[:, t, :], rstd[:, t:t + 1], fin_b, ALU.mult, ALU.mult).then_inc(out_ready, 1)


_INS = ["x", "c", "ctx", "c_ctx", "w_mod", "b_mod", "norm1_g", "norm2_g", "conv_w_pw1", "conv_b_pw1", "conv_w_dw",
        "conv_b_dw", "conv_ln_g", "conv_ln_b", "conv_w_pw2", "conv_b_pw2", "attn_w_qkv", "attn_w_o", "attn_sink",
        "router_w", "router_b", "moe_w_gate", "moe_w_up", "moe_w_down", "final_g"]


def kernel(**inputs):
    import concourse.bacc as bacc
    from concourse.bass_utils import run_bass_kernel_spmd

    nc = bacc.Bacc("TRN2", target_bir_lowering=False, num_devices=1)
    small_c, mask_c = shape_constants()
    arrays = {f"in_{name}": np.ascontiguousarray(inputs[name]) for name in _INS}
    arrays["small_c"], arrays["mask_c"] = small_c, mask_c
    args = [nc.dram_tensor(name, a.shape, mybir.dt.from_np(a.dtype), kind="ExternalInput").ap() for name, a in arrays.items()]
    args.append(nc.dram_tensor("result", (1, SEQ, D), FP32, kind="ExternalOutput").ap())
    backbone(nc, *args)
    r = run_bass_kernel_spmd(nc, [arrays], core_ids=[0])
    return r.results[0]["result"]
```

```python
import numpy as np
import concourse.bass as bass
from concourse import mybir
from contextlib import ExitStack

FP32 = mybir.dt.float32
I32 = mybir.dt.int32
ALU = mybir.AluOpType
ACT = mybir.ActivationFunctionType
AX = mybir.AxisListType

P = 128
D = 1024
KD = D // P
SEQ, CTX = 256, 256
NT = (SEQ + CTX) // P
NX = SEQ // P
HALF = 512
TAPS, PAD = 31, 15
HD, NH, NKV, GROUP = 64, 16, 4, 4
WINDOW = 128
GRID_W, ROPE_PAIRS, THETA = 64, 16, 10000.0
NE, NG, EPG = 16, 4, 4
F = 512
EPS = 1e-6
BIG = 1e30
TILE = 64
NTOK = (NT * P, NX * P)
MAXJ = tuple(n // TILE for n in NTOK)
ROWS = (NE + (2 * NTOK[0] - NE) // TILE) * TILE + TILE
ROOM = ROWS + MAXJ[0] * TILE
MOD_THIRD = 2048
SLOTS, SLOTW = 3, 3 * D * F // P
RING = ((0, 1, 2), (1, 0, 2))
KV_BANKS = ((2, 4), (3, 6), (0, 0), (1, 2))
Q_BANKS = ((0, 0, 1), (0, 1, 3), (1, 0, 5), (1, 1, 7))
FIRST_ORDER = (1, 2, 3, 0)


def shape_constants():
    i = np.arange(P)
    ident = np.eye(P)
    before = (i[:, None] < i[None, :]) * 1.0
    ones = np.ones((P, P))
    mask = np.zeros((P, NX, 2 * SEQ))
    for b in range(NX):
        mask[:, b, :SEQ] = np.where(np.abs(b * P + i[:, None] - np.arange(SEQ)[None, :]) <= WINDOW, 0.0, -BIG)
    inv = np.power(np.float32(THETA), -np.arange(ROPE_PAIRS, dtype=np.float32) / np.float32(ROPE_PAIRS))
    tok = np.arange(SEQ)
    ang = np.stack([(tok // GRID_W).astype(np.float32)[:, None] * inv,
                    (tok % GRID_W).astype(np.float32)[:, None] * inv], axis=1)
    cos, sin = np.cos(ang), np.sin(ang)
    rope = np.concatenate([np.stack([cos, cos], 2).reshape(SEQ, HD),
                           np.stack([-sin, sin], 2).reshape(SEQ, HD)], axis=1)
    rope = rope.reshape(NX, P, 2 * HD).transpose(1, 0, 2)
    down = np.concatenate([np.broadcast_to(NE - np.arange(NE), (P, NE)),
                           np.broadcast_to(NG - np.arange(NG), (P, NG))], axis=1)
    small = np.concatenate([ident, before, ones, rope.reshape(P, -1), down], axis=1)
    return small.astype(np.float32), mask.reshape(P, -1).astype(np.float32)


class Order:

    def __init__(self, eng, sem, base=0):
        self.eng, self.sem, self.base, self.n = eng, sem, base, 0

    def step(self, ins):
        self.n += 1
        ins.then_inc(self.sem, 1)
        self.eng.wait_ge(self.sem, self.base + self.n)


def backbone(nc, x, c, ctx_in, c_ctx, w_mod, b_mod, norm1_g, norm2_g, w_pw1, b_pw1, w_dw, b_dw, ln_g, ln_b,
             w_pw2, b_pw2, w_qkv, w_o, sink, router_w, router_b, w_gate, w_up, w_down, final_g,
             small_c, mask_c, out):
    mod_d = nc.dram_tensor("mod_d", [6, 2, MOD_THIRD], FP32, kind="Internal").ap()
    xs_d = nc.dram_tensor("xs_d", [ROOM, D], FP32, kind="Internal").ap()
    x_src = [x[0, t * P:(t + 1) * P, :] for t in range(NX)] + [ctx_in[0, t * P:(t + 1) * P, :] for t in range(NX)]

    es = ExitStack()
    with es:
        def sb(name, shape, dt=FP32):
            return es.enter_context(nc.sbuf_tensor(name, shape, dt))

        def sem(name):
            return es.enter_context(nc.semaphore(name))

        W = sb("W", [P, SLOTS * SLOTW])
        R = W[:, 0:24576]
        V = W[:, 24576:32768]
        P1 = W[:, 32768:36864]
        E = sb("E", [P, 2048])
        P2 = sb("P2", [P, 4096])
        xr = sb("xr", [P, NT, D])
        small = sb("small", [P, 3 * P + NX * 2 * HD + NE + NG])
        ident, before, ones = small[:, 0:P], small[:, P:2 * P], small[:, 2 * P:3 * P]
        rope = small[:, 3 * P:3 * P + NX * 2 * HD].rearrange("p (t s d) -> p t s d", t=NX, s=2)
        down_e = small[:, 3 * P + NX * 2 * HD:3 * P + NX * 2 * HD + NE]
        down_g = small[:, 3 * P + NX * 2 * HD + NE:3 * P + NX * 2 * HD + NE + NG]
        cT = sb("cT", [P, 2, KD])
        cs = sb("cs", [P, KD, 32])
        vpad = sb("vpad", [P, 2, 2, SEQ + 2 * PAD])
        sg = sb("sg", [P, HALF])
        odd_sum = sb("odd_sum", [P, HALF])
        par = sb("par", [P, 2 * KD + KD + KD + KD + 2 * KD])
        b1_c = par[:, 0:2 * KD].rearrange("p (h m) -> p h m", h=2)
        bdw_c, lng_c, lnb_c = (par[:, (2 + i) * KD:(3 + i) * KD] for i in range(3))
        n1_c = par[:, 5 * KD:7 * KD].rearrange("p (l m) -> p l m", l=2)
        wdw = sb("wdw", [P, TAPS, KD])
        rw = sb("rw", [P, KD, NE])
        rb = sb("rb", [P, NE])
        sink_b = sb("sink_b", [P, NH])
        eps_t = sb("eps_t", [P, 1])
        mod1 = sb("mod1", [P, 2, 2, 2, KD])
        A1 = sb("A1", [P, 2, 2, KD])
        zrow = sb("zrow", [P, HALF])
        ssq = sb("ssq", [P, NT])
        rstd = sb("rstd", [P, NT])
        lg_s = sb("lg_s", [P, NT, NE])
        r_a = sb("r_a", [P, NT, NE])
        r_b = sb("r_b", [P, NT, NE])
        r_c = sb("r_c", [P, NT, NE])
        oh = [sb(f"oh{i}", [P, NT, NE]) for i in range(2)]
        msk = sb("msk", [P, NT, NE])
        g_a = [sb(f"g_a{i}", [P, NT, NG]) for i in range(4)]
        cum = [sb(f"cum{i}", [P, 8 + NE]) for i in range(2)]
        m1 = sb("m1", [P, NT])
        wt = sb("wt", [P, 2, NT])
        wsum = sb("wsum", [P, NT])
        slot_f = sb("slot_f", [P, 2, NT])
        slot = sb("slot", [P, 2, NT], I32)
        cnt_i = sb("cnt_i", [P, NE], I32)
        more = sb("more", [P, NE + 4], I32)
        first = sb("first", [P, NE + 4], I32)
        stat = sb("stat", [P, NX, 4, NH])
        mx = sb("mx", [P, 2])

        bank = [es.enter_context(nc.psum_tensor(f"bank{i}", [P, HALF], FP32)) for i in range(8)]

        pw1 = R[:, 0:16384].rearrange("p (j h c m) -> p j h c m", j=KD, h=2, m=KD)
        pw2 = R[:, 16384:24576].rearrange("p (m n) -> p m n", m=KD)
        mod0_w = [R[:, 16384 + MOD_THIRD * k:16384 + MOD_THIRD * (k + 1)] for k in range(4)] + \
                 [V[:, MOD_THIRD * k:MOD_THIRD * (k + 1)] for k in range(4)]
        modk_w = [V[:, MOD_THIRD * q:MOD_THIRD * (q + 1)] for q in range(4)] + [E[:, :]]
        hT0 = P1[:, :].rearrange("p (j t) -> p j t", j=KD)
        xn0 = P2[:, :].rearrange("p (t d) -> p t d", t=NT)
        u = P2[:, :].rearrange("p (m t) -> p m t", m=KD)
        modb = P1[:, 0:5 * HALF].rearrange("p (q n) -> p q n", q=5)
        mean, rs, sq0 = (P1[:, HALF * i:HALF * (i + 1)] for i in range(5, 8))
        Vb = V[:, :].rearrange("p (v d) -> p v d", v=8)
        G1b = [Vb[:, 0, :], Vb[:, 1, :]]
        A2b = [Vb[:, 2, :], Vb[:, 3, :]]
        B2b = [Vb[:, 4, :], Vb[:, 5, :]]
        G2b = [Vb[:, 6, :], Vb[:, 7, :]]
        n2b, b2b = E[:, 0:D], E[:, D:2 * D]
        h2 = P1[:, :].rearrange("p (t d) -> p t d", t=NT)
        h2T = [P2[:, :].rearrange("p (j t) -> p j t", j=KD), E[:, :].rearrange("p (j t) -> p j t", j=KD)]
        ring = [W[:, s * SLOTW:(s + 1) * SLOTW] for s in range(SLOTS)]
        gu_w = [w[:, 0:8192].rearrange("p (g k f) -> p g k f", g=2, k=8) for w in ring]
        d_w = [w[:, 8192:12288].rearrange("p (k n) -> p k n", k=4) for w in ring]
        X = [P2[:, HALF * i:HALF * (i + 1)] for i in range(3)] + [E[:, 3 * HALF:4 * HALF]]
        XT = [P2[:, HALF * (3 + i):HALF * (4 + i)].rearrange("p (j h s) -> p j h s", j=4, h=2) for i in range(3)]
        H = [P2[:, 3072 + 256 * i:3072 + 256 * (i + 1)] for i in range(2)]
        HT = [P2[:, 3584 + 256 * i:3584 + 256 * (i + 1)].rearrange("p (j h s) -> p j h s", j=2, h=2) for i in range(2)]
        Y = [E[:, HALF * i:HALF * (i + 1)] for i in range(3)]
        comb = P1[:, :].rearrange("p (t d) -> p t d", t=4)
        hT1 = P2[:, :].rearrange("p (j t) -> p j t", j=KD)
        wqkv = R[:, 12288:24576].rearrange("p (j n) -> p j n", j=KD)
        wo = R[:, 0:8192].rearrange("p (j n) -> p j n", j=KD)
        kd = P1[:, 0:2048].rearrange("p (t k u d) -> p t k u d", t=NT, k=NKV, u=2)
        kT = P1[:, 2048:4096].rearrange("p (k n) -> p k n", k=NKV)
        vv = V[:, 4096:5120].rearrange("p (t n) -> p t n", t=NT)
        qr = V[:, 5120:7168].rearrange("p (t n) -> p t n", t=NX)
        rt = V[:, 7168:8192]
        qT = E[:, :].rearrange("p (j t) -> p j t", j=KD)
        Sm = [R[:, 8192 + HALF * i:8192 + HALF * (i + 1)] for i in range(2)]
        Pm = [R[:, 9216 + HALF * i:9216 + HALF * (i + 1)] for i in range(2)]
        PT = [R[:, 10240 + HALF * i:10240 + HALF * (i + 1)] for i in range(2)]
        mask = R[:, 11264:12288].rearrange("p (b n) -> p b n", b=NX)
        o_t = P2[:, 0:2048].rearrange("p (t n) -> p t n", t=NX)
        oT = P2[:, 2048:4096].rearrange("p (j t) -> p j t", j=KD)
        fin_b = Vb[:, 7, :]
        G1n, B2n, A2n, G2n, n2n = (Vb[:, i, :] for i in range(5))

        c_in, cs_zero, cs_ready = sem("c_in"), sem("cs_zero"), sem("cs_ready")
        x_in = [sem(f"x_in{t}") for t in range(NT)]
        small_in, par_in = sem("small_in"), sem("par_in")
        modb_zero, modb_in = sem("modb_zero"), sem("modb_in")
        mod0_in = [sem(f"mod0_in{i}") for i in range(4)]
        pw1_in, pw2_in = sem("pw1_in"), sem("pw2_in")
        modk_in = [sem(f"modk_in{i}") for i in range(3)]
        mod_used = sem("mod_used")
        mod_done = sem("mod_done")
        mod_row = sem("mod_row")
        mod_out, mods_out = sem("mod_out"), sem("mods_out")
        mod1_in, A1_ready = sem("mod1_in"), sem("A1_ready")
        vec_in, A2_ready = sem("vec_in"), sem("A2_ready")
        ssq_done, sqrt_done, xn_ready = sem("ssq_done"), sem("sqrt_done"), sem("xn_ready")
        xT_ps, hT_act, hT_dve = sem("xT_ps"), sem("hT_act"), sem("hT_dve")
        vpad_zero = sem("vpad_zero")
        g_ps, a_ps, sg_ready, v_ready, conv_done = sem("g_ps"), sem("a_ps"), sem("sg_ready"), sem("v_ready"), sem("conv_done")
        pw1_used, sum_ps, mean_ready = sem("pw1_used"), sem("sum_ps"), sem("mean_ready")
        dif_ready, sq_ready, sq_used, var_ps = sem("dif_ready"), sem("sq_ready"), sem("sq_used"), sem("var_ps")
        std_ready, z_ready, y_ready = sem("std_ready"), sem("z_ready"), sem("y_ready")
        mix_ps, mix_read = sem("mix_ps"), sem("mix_read")
        ssq2_done, sqrt2_done = sem("ssq2_done"), sem("sqrt2_done")
        h2_ready, h2T_ps, h2T_ready, logit_ps = sem("h2_ready"), sem("h2T_ps"), sem("h2T_ready"), sem("logit_ps")
        sig_ready, mask_ready, rank_ps = sem("sig_ready"), sem("mask_ready"), sem("rank_ps")
        routed, scattered = sem("routed"), sem("scattered")
        xs_zero_src, xs_zero = sem("xs_zero_src"), sem("xs_zero")
        L = range(2)
        S2 = range(2)

        def sems(name):
            return [sem(f"{name}{s}") for s in S2]

        gu_in, d_in = ([sem(f"{name}{s}") for s in range(SLOTS)] for name in ("gu_in", "d_in"))
        gu_ps, d_ps = sems("gu_ps"), sems("d_ps")
        x_tile = sems("x_tile")
        xt_ps, xt_ready = sems("xt_ps"), sems("xt_ready")
        silu_done, h_ready = sems("silu_done"), sems("h_ready")
        ht_ps, ht_ready = sems("ht_ps"), sems("ht_ready")
        y_ready_m, y_out = sems("y_ready_m"), sems("y_out")
        further_x = sems("further_x")
        ov = {k: sem(f"further_{k}") for k in ("xt_ps", "xt", "gu", "silu", "h", "ht_ps", "ht", "y_ps", "y", "out")}
        USES = [[len(range(RING[0].index(s), NE, SLOTS)) * l for s in range(SLOTS)] for l in range(2)]
        PAIRS = NE // 2
        moe_done = [sem(f"moe_done{l}") for l in L]
        got, comb_read = [sem(f"got{i}") for i in range(2)], sem("comb_read")
        scaled = sem("scaled")
        comb_done = sem("comb_done")
        qkv_in, wo_in, mask_in = sem("qkv_in"), sem("wo_in"), sem("mask_in")
        proj_ps, v_copied, k_ready, kT_ps, kT_ready = sem("proj_ps"), sem("v_copied"), sem("k_ready"), sem("kT_ps"), sem("kT_ready")
        q_ready, qT_ps, qT_ready = sem("q_ready"), sem("qT_ps"), sem("qT_ready")
        s_ps, s_ready, p_ready, pT_ps, pT_ready, o_ps = (sem(n) for n in ("s_ps", "s_ready", "p_ready", "pT_ps", "pT_ready", "o_ps"))
        sinkarg, sinkexp, o_ready, oT_ps, oT_ready = (sem(n) for n in ("sinkarg", "sinkexp", "o_ready", "oT_ps", "oT_ready"))
        vec1_in, fin_in = sem("vec1_in"), sem("fin_in")
        out_ready, out_done = sem("out_ready"), sem("out_done")
        dve_order, act_order = sem("dve_order"), sem("act_order")
        conv_order, tail_order = sem("conv_order"), sem("tail_order")

        block = es.enter_context(nc.Block())

        def row(v, n):
            return v.partition_broadcast(n)

        wg_v = [w_gate[l].rearrange("e (h p j) f -> e p h (j f)", h=2, j=4) for l in L]
        wu_v = [w_up[l].rearrange("e (h p j) f -> e p h (j f)", h=2, j=4) for l in L]
        wd_v = [w_down[l].rearrange("e (h p j) n -> e p h (j n)", h=2, j=2) for l in L]

        @block.sync
        def _(sp):
            for i in range(4):
                for k in (2 * i, 2 * i + 1):
                    sp.dma_start(mod0_w[k], w_mod[0].rearrange("(p k) n -> p k n", k=KD)[:, k, 0:MOD_THIRD]).then_inc(mod0_in[i], 16)
            sp.dma_start(R[:, 0:16384], w_pw1[0].rearrange("(p j) n -> p (j n)", j=KD)).then_inc(pw1_in, 16)
            sp.wait_ge(mod_done, 1)
            with sp.Fori(0, KD) as k:
                w_k = [w_mod[l].rearrange("(p k) n -> k p n", k=KD) for l in L]
                sp.wait_ge(mod_used, k * 3)
                sp.dma_start(V[:, 0:4096], w_k[0][bass.ds(k, 1), :, MOD_THIRD:3 * MOD_THIRD].rearrange("k p n -> (k p) n")).then_inc(modk_in[0], 16)
                sp.wait_ge(mod_used, k * 3)
                sp.dma_start(V[:, 4096:8192], w_k[1][bass.ds(k, 1), :, 0:2 * MOD_THIRD].rearrange("k p n -> (k p) n")).then_inc(modk_in[1], 16)
                sp.dma_start(E[:, :], w_k[1][bass.ds(k, 1), :, 2 * MOD_THIRD:3 * MOD_THIRD].rearrange("k p n -> (k p) n")).then_inc(modk_in[2], 16)
            sp.dma_start(R[:, 16384:24576], w_pw2[0].rearrange("(p m) n -> p (m n)", m=KD)).then_inc(pw2_in, 16)

            extra = sp.alloc_register("further_sp")
            sp.reg_mov(extra, 0)

            def count(e, l):
                sp.reg_add(extra, extra, sp.value_load(more[0:1, bass.ds(e, 1)], min_val=0, max_val=MAXJ[l] - 1))

            def moe_weights(l):
                def load(w, e, dst, signal):
                    sp.dma_start(dst.rearrange("p (h n) -> p h n", h=2), w[bass.ds(e, 1)].rearrange("e p h n -> (e p) h n")).then_inc(signal, 16)

                def gate(e, slot):
                    load(wg_v[l], e, ring[slot][:, 0:4096], gu_in[slot])

                def up(e, slot):
                    load(wu_v[l], e, ring[slot][:, 4096:8192], gu_in[slot])

                def down(e, slot):
                    load(wd_v[l], e, ring[slot][:, 8192:12288], d_in[slot])

                at = RING[l]
                if l == 0:
                    sp.wait_ge(pw1_used, 1)
                else:
                    sp.wait_ge(proj_ps, 8)
                gate(0, at[0])
                up(0, at[0])
                down(0, at[0])
                if l == 0:
                    gate(1, at[1])
                    sp.wait_ge(mix_ps, NT)
                else:
                    sp.wait_ge(mix_ps, NT + NX)
                    gate(1, at[1])
                up(1, at[1])
                down(1, at[1])
                sp.wait_ge(routed, l + 1)
                sp.wait_ge(scattered, 32 * (NT if l == 0 else NT + NX))
                gate(2, at[2])
                up(2, at[2])
                down(2, at[2])

                def refill(e, r):
                    before = e - SLOTS
                    s, slot = r % 2, at[r % SLOTS]
                    count(before, l)
                    served = sp.snap(extra)
                    done = PAIRS * l + (before // 2 if isinstance(e, int) else 3 * e6 + r // 2) + 1
                    sp.wait_ge(gu_ps[s], done)
                    sp.wait_ge(ov["gu"], served)
                    gate(e, slot)
                    up(e, slot)
                    sp.wait_ge(d_ps[s], done)
                    sp.wait_ge(ov["y_ps"], served)
                    down(e, slot)

                with sp.Fori(0, 2) as e6:
                    for r in range(6):
                        refill(SLOTS + 6 * e6 + r, r)
                refill(NE - 1, 0)

            moe_weights(0)
            count(NE - 3, 0)
            served = sp.snap(extra)
            sp.wait_ge(d_ps[1], PAIRS - 1)
            sp.wait_ge(ov["y_ps"], served)
            sp.dma_start(R[:, 12288:24576], w_qkv[0].rearrange("(p j) n -> p (j n)", j=KD)).then_inc(qkv_in, 16)
            count(NE - 2, 0)
            count(NE - 1, 0)
            sp.wait_ge(moe_done[0], 1)
            sp.dma_start(wo, w_o[0].rearrange("(j p) n -> p j n", p=P)).then_inc(wo_in, 16)
            sp.dma_start(mask.rearrange("p b n -> p (b n)"), mask_c).then_inc(mask_in, 16)
            moe_weights(1)
            for t in range(NX):
                sp.wait_ge(out_ready, t + 1)
                sp.dma_start(out[0, t * P:(t + 1) * P, :], xr[:, t, :]).then_inc(out_done, 16)
            sp.wait_ge(out_done, 16 * NX)

        @block.gpsimd
        def _(pool):
            further = pool.alloc_register("further_pool")
            pool.reg_mov(further, 0)
            nc.gpsimd.memset(cs[:, :, :], 0.0).then_inc(cs_zero, 1)
            nc.gpsimd.memset(eps_t[:, :], EPS).then_inc(cs_zero, 1)
            nc.gpsimd.memset(modb[:, 0, :], 0.0).then_inc(modb_zero, 1)
            nc.gpsimd.memset(vpad[:, :, :, :], 0.0).then_inc(vpad_zero, 1)
            nc.gpsimd.memset(more[:, :], 0).then_inc(vpad_zero, 1)
            nc.gpsimd.memset(first[:, :], 0).then_inc(vpad_zero, 1)
            for i in range(2):
                nc.gpsimd.memset(cum[i][:, :], 0.0).then_inc(vpad_zero, 1)
            nc.gpsimd.memset(zrow[:, :], 0.0).then_inc(xs_zero_src, 1)
            pool.dma_start(small[:, :], small_c).then_inc(small_in, 16)

            def bias_rows(slot0, third):
                for g in range(4):
                    src = b_mod[third // 3:third // 3 + 1, (third % 3) * MOD_THIRD + g * HALF:(third % 3) * MOD_THIRD + (g + 1) * HALF]
                    pool.dma_start(modb[32 * g:32 * g + 2, slot0, :], src.broadcast_to([2, HALF])).then_inc(modb_in, 16)

            pool.wait_ge(modb_zero, 1)
            bias_rows(0, 0)
            loads = [(b1_c, b_pw1[0].rearrange("(h p m) -> p h m", h=2, m=KD)), (bdw_c, b_dw[0].rearrange("(p m) -> p m", m=KD)),
                     (lng_c, ln_g[0].rearrange("(p m) -> p m", m=KD)), (lnb_c, ln_b[0].rearrange("(p m) -> p m", m=KD)),
                     (n1_c, norm1_g.rearrange("l (p m) -> p l m", m=KD)),
                     (wdw[:, :, :], w_dw[0].rearrange("k (p m) -> p k m", m=KD)),
                     (rw[:, :, :], router_w.rearrange("(p m) e -> p m e", m=KD)),
                     (rb[:, :], row(router_b, P)), (sink_b[:, :], row(sink[0], P))]
            for dst, src in loads:
                pool.dma_start(dst, src).then_inc(par_in, 16)

            until = pool.alloc_register("until")

            def wait_count(signal, count):
                pool.reg_mov(until, count)
                pool.wait_ge(routed, 1)
                pool.wait_ge(signal, until)

            def shift_scale(l):
                pool.dma_start(mod1[:, l].rearrange("p r v j -> p (r v) j"),
                               mod_d[3 * l].rearrange("r (v p j) -> p (r v) j", v=2, j=KD)).then_inc(mod1_in, 16)

            pool.wait_ge(mod_out, 64)
            shift_scale(0)
            pool.wait_ge(xs_zero_src, 1)
            pool.wait_ge(v_ready, 2)
            pool.dma_start(xs_d[0:ROWS, :].rearrange("(p a) (b n) -> p (a b) n", p=P, n=HALF),
                           zrow[:, :].unsqueeze(1).to_broadcast([P, ROWS // P * 2, HALF])).then_inc(xs_zero, 16)
            pool.wait_ge(pw1_used, 1)
            nc.gpsimd.memset(modb[:, :, :], 0.0).then_inc(modb_zero, 1)
            pool.wait_ge(modb_zero, 2)
            for third in range(1, 6):
                bias_rows(third - 1, third)
            pool.wait_ge(mod_row, 2)
            for g in range(4):
                pool.dma_start(mod_d[1:6, :, g * HALF:(g + 1) * HALF].rearrange("q r n -> r q n"), modb[32 * g:32 * g + 2, :, :]).then_inc(mods_out, 16)
            pool.wait_ge(mods_out, 64)
            shift_scale(1)
            vecs = [(G1b, 1, 0), (B2b, 1, D), (A2b, 2, 0)]
            for dst, third, off in vecs:
                for r in range(2):
                    pool.dma_start(dst[r], row(mod_d[third, r, off:off + D], P)).then_inc(vec_in, 16)
            pool.dma_start(n2b, row(norm2_g[0], P)).then_inc(vec_in, 16)
            pool.dma_start(b2b, row(b_pw2[0], P)).then_inc(vec_in, 16)

            def moe_rows(l):
                nt = NTOK[l] // P
                pool.wait_ge(routed, l + 1)
                if l == 0:
                    pool.wait_ge(xs_zero, 16)
                for k in range(2):
                    for t in range(nt):
                        pool.indirect_dma_start(xs_d[0:ROWS, :], bass.IndirectOffsetOnAxis(ap=slot[:, k, t:t + 1].bitcast(mybir.dt.uint32), axis=0),
                                                h2[:, t, :], None).then_inc(scattered, 16)
                pool.wait_ge(scattered, 32 * (nt if l == 0 else NT + NX))

                def load_rows(dst, at, signal):
                    for h in range(2):
                        pool.dma_start(dst[h * TILE:(h + 1) * TILE, :], xs_d[bass.ds(at, TILE), h * HALF:(h + 1) * HALF]).then_inc(signal, 16)

                def store_rows(src, at, signal):
                    for h in range(2):
                        pool.dma_start(xs_d[bass.ds(at, TILE), h * HALF:(h + 1) * HALF], src[h * TILE:(h + 1) * TILE, :]).then_inc(signal, 16)

                def start_of(e):
                    return pool.value_load(first[0:1, bass.ds(e, 1)], min_val=0, max_val=ROWS - TILE)

                def further_of(e):
                    return pool.value_load(more[0:1, bass.ds(e, 1)], min_val=0, max_val=MAXJ[l] - 1)

                def further_rows(e, s):
                    with pool.If(further_of(e) > 0):
                        load_rows(X[2 + s], pool.snap(start_of(e) + TILE), further_x[s])

                for s in S2:
                    load_rows(X[s], start_of(s), x_tile[s])
                for s in S2:
                    further_rows(s, s)
                    pool.wait_ge(xt_ps[s], (PAIRS + 1) * l + 1)
                    load_rows(X[s], start_of(2 + s), x_tile[s])
                with pool.Fori(0, PAIRS) as i:
                    for s in S2:
                        e = 2 * i + s
                        with pool.If(i < PAIRS - 1):
                            wait_count(xt_ps[s], (PAIRS + 1) * l + i + 2)
                            load_rows(X[s], start_of(e + 4), x_tile[s])
                        at, n = start_of(e), further_of(e)
                        wait_count(y_ready_m[s], PAIRS * l + i + 1)
                        store_rows(Y[s], at, y_out[s])
                        with pool.If(n > 0):
                            with pool.Fori(1, MAXJ[l]) as j:
                                with pool.If(j < n + 1):
                                    q = pool.snap(further)
                                    with pool.If(j < n):
                                        wait_count(ov["xt_ps"], q + 1)
                                        load_rows(X[2 + s], pool.snap(at + j * TILE + TILE), further_x[s])
                                    wait_count(ov["y"], q + 1)
                                    store_rows(Y[2], pool.snap(at + j * TILE), ov["out"])
                                    pool.reg_add(further, further, 1)
                        further_rows(e + 2, s)
                if l == 0:
                    for r in range(2):
                        pool.dma_start(G2b[r], row(mod_d[2, r, D:2 * D], P)).then_inc(vec_in, 16)
                    for dst, src in [(G1n, mod_d[4, 0, 0:D]), (B2n, mod_d[4, 0, D:2 * D]), (A2n, mod_d[5, 0, 0:D]),
                                     (n2n, norm2_g[1])]:
                        pool.dma_start(dst, row(src, P)).then_inc(vec1_in, 16)
                else:
                    pool.dma_start(G2n, row(mod_d[5, 0, D:2 * D], P)).then_inc(fin_in, 16)
                    pool.dma_start(fin_b, row(final_g, P)).then_inc(fin_in, 16)
                for s in S2:
                    pool.wait_ge(y_out[s], 32 * PAIRS * (l + 1))
                wait_count(ov["out"], 32 * pool.snap(further))
                for t in range(nt):
                    b = t % 2
                    if t >= 2:
                        pool.wait_ge(xT_ps, NT + t - 1)
                    for k in range(2):
                        pool.indirect_dma_start(comb[:, 2 * b + k, :], None, xs_d[0:ROWS, :],
                                                bass.IndirectOffsetOnAxis(ap=slot[:, k, t:t + 1].bitcast(mybir.dt.uint32), axis=0)).then_inc(got[b], 16)

            moe_rows(0)
            moe_rows(1)

        @block.scalar
        def _(act):
            further = act.alloc_register("further_act")
            act.reg_mov(further, 0)
            order = Order(act, act_order)
            for r, v in ((0, c[0]), (1, c_ctx)):
                act.dma_start(cT[:, r, :], v.rearrange("(p j) -> p j", j=KD)).then_inc(c_in, 16)
            for t in range(NT):
                act.dma_start(xr[:, t, :], x_src[t]).then_inc(x_in[t], 16)
            act.wait_ge(c_in, 32)
            act.wait_ge(cs_zero, 2)
            nc.scalar.activation(cs[:, :, 0:2].rearrange("p j r -> p r j"), cT[:, :, :], ACT.Silu).then_inc(cs_ready, 1)
            for t in range(NT):
                act.wait_ge(x_in[t], 16)
                nc.scalar.activation(xn0[:, t, :], xr[:, t, :], ACT.Square, accum_out=ssq[:, t:t + 1]).then_inc(ssq_done, 1)
            act.wait_ge(ssq_done, NT)
            nc.scalar.activation(rstd[:, :], ssq[:, :], ACT.Sqrt, bias=eps_t[:, 0:1], scale=1.0 / D).then_inc(sqrt_done, 1)
            act.wait_ge(mod_row, 1)
            for g in range(4):
                act.dma_start(mod_d[0, :, g * HALF:(g + 1) * HALF], modb[32 * g:32 * g + 2, 0, :]).then_inc(mod_out, 16)

            def modulated(l, hT, t, n):
                act.wait_ge(xT_ps, n)
                for j in range(KD // 2):
                    last = nc.scalar.activation(hT[:, j, t * P:(t + 1) * P], bank[2 * t][:, j * P:(j + 1) * P],
                                                ACT.Identity, bias=mod1[:, l, t // NX, 0, j:j + 1], scale=A1[:, l, t // NX, j:j + 1])
                last.then_inc(hT_act, 1)

            act.wait_ge(A1_ready, 1)
            for n, t in enumerate(FIRST_ORDER):
                modulated(0, hT0, t, n + 1)
            act.wait_ge(par_in, 16 * 9)
            with act.Fori(0, KD) as m:
                act.wait_ge(g_ps, m + 1)
                act.wait_ge(v_ready, m)
                nc.scalar.activation(sg[:, :], bank[6][:, :], ACT.Sigmoid, bias=b1_c[:, 1, bass.ds(m, 1)]).then_inc(sg_ready, 1)
            act.wait_ge(sum_ps, 1)
            nc.scalar.activation(mean, bank[7][:, :], ACT.Copy, scale=1.0 / D).then_inc(mean_ready, 1)
            sq = [sq0, sg[:, :]]
            for m in range(KD):
                act.wait_ge(dif_ready, m + 1)
                if m >= 2:
                    act.wait_ge(sq_used, m - 1)
                nc.scalar.activation(sq[m % 2], u[:, m, :], ACT.Square).then_inc(sq_ready, 1)
            act.wait_ge(var_ps, 1)
            nc.scalar.activation(rs, bank[7][:, :], ACT.Sqrt, bias=eps_t[:, 0:1], scale=1.0 / D).then_inc(std_ready, 1)
            for m in range(KD):
                act.wait_ge(z_ready, m + 1)
                nc.scalar.activation(u[:, m, :], u[:, m, :], ACT.Silu, bias=lnb_c[:, m:m + 1], scale=lng_c[:, m:m + 1]).then_inc(y_ready, 1)

            def second_norm(l, ts, base):
                for n, t in enumerate(ts):
                    act.wait_ge(mix_read, base + n + 1)
                    nc.scalar.activation(h2[:, t, :], xr[:, t, :], ACT.Square, accum_out=ssq[:, t:t + 1]).then_inc(ssq2_done, 1)
                    act.wait_ge(ssq2_done, base + n + 1)
                    nc.scalar.activation(rstd[:, t:t + 1], ssq[:, t:t + 1], ACT.Sqrt, bias=eps_t[:, 0:1], scale=1.0 / D).then_inc(sqrt2_done, 1)
                for n, t in enumerate(ts):
                    act.wait_ge(h2T_ps, base + n + 1)
                    for half in range(2):
                        last = nc.scalar.activation(h2T[l][:, 4 * half:4 * half + 4, t * P:(t + 1) * P],
                                                    bank[2 * t + half][:, :].rearrange("p (j t) -> p j t", j=4), ACT.Copy)
                    last.then_inc(h2T_ready, 1)
                nt = len(ts)
                act.wait_ge(logit_ps, l + 1)
                nc.scalar.activation(lg_s[:, 0:nt, :], bank[0][:, 0:nt * NE].rearrange("p (t e) -> p t e", t=nt), ACT.Sigmoid).then_inc(sig_ready, 1)

            def moe_act(l):
                act.wait_ge(routed, l + 1)
                with act.Fori(0, NE // 2) as i:
                    for s in S2:
                        act.wait_ge(gu_ps[s], PAIRS * l + i + 1)
                        nc.scalar.activation(H[s], bank[s][:, 0:256], ACT.Silu).then_inc(silu_done[s], 1)
                    for s in S2:
                        n = act.value_load(more[0:1, bass.ds(2 * i + s, 1)], min_val=0, max_val=MAXJ[l] - 1)
                        act.wait_ge(d_ps[s], PAIRS * l + i + 1)
                        act.wait_ge(y_out[s], 32 * (PAIRS * l + i))
                        nc.scalar.activation(Y[s], bank[2 + s][:, :], ACT.Copy).then_inc(y_ready_m[s], 1)
                        with act.If(n > 0):
                            with act.Fori(1, MAXJ[l]) as j:
                                with act.If(j < n + 1):
                                    q = act.snap(further)
                                    act.wait_ge(ov["gu"], q + 1)
                                    nc.scalar.activation(H[s], bank[s][:, 0:256], ACT.Silu).then_inc(ov["silu"], 1)
                                    act.wait_ge(ov["y_ps"], q + 1)
                                    act.wait_ge(ov["out"], q * 32)
                                    nc.scalar.activation(Y[2], bank[2 + s][:, :], ACT.Copy).then_inc(ov["y"], 1)
                                    act.reg_add(further, further, 1)

            def combine_act(t, n):
                b = t % 2
                act.wait_ge(got[b], 32 * n)
                nc.scalar.activation(comb[:, 2 * b, :], comb[:, 2 * b, :], ACT.Copy, scale=wt[:, 0, t:t + 1]).then_inc(scaled, 1)

            second_norm(0, range(NT), 0)
            moe_act(0)
            for t in range(NT):
                combine_act(t, t // 2 + 1)
                act.wait_ge(comb_done, t + 1)
                nc.scalar.activation(comb[:, 2 * (t % 2) + 1, :], xr[:, t, :], ACT.Square, accum_out=ssq[:, t:t + 1]).then_inc(ssq_done, 1)
                act.wait_ge(ssq_done, NT + t + 1)
                nc.scalar.activation(rstd[:, t:t + 1], ssq[:, t:t + 1], ACT.Sqrt, bias=eps_t[:, 0:1], scale=1.0 / D).then_inc(sqrt_done, 1)
                act.wait_ge(A1_ready, 2)
                modulated(1, hT1, t, NT + t + 1)
            for n, (t, b) in enumerate(KV_BANKS):
                act.wait_ge(proj_ps, n + 1)
                nc.scalar.activation(vv[:, t, :], bank[b][:, 256:512], ACT.Copy).then_inc(v_copied, 1)
            for n, (t, b) in enumerate(KV_BANKS):
                act.wait_ge(kT_ps, n + 1)
                nc.scalar.activation(kT[:, :, t * P:(t + 1) * P], bank[b][:, :].rearrange("p (k t) -> p k t", k=NKV), ACT.Copy).then_inc(kT_ready, 1)
            for n, (t, h, b) in enumerate(Q_BANKS):
                act.wait_ge(qT_ps, n + 1)
                nc.scalar.activation(qT[:, 4 * h:4 * h + 4, t * P:(t + 1) * P], bank[b][:, :].rearrange("p (k t) -> p k t", k=4), ACT.Copy).then_inc(qT_ready, 1)

            def probs(n):
                b, h = n // NH, n % NH
                act.wait_ge(s_ready, n + 1)
                if n >= 2:
                    act.wait_ge(pT_ps, n - 1)
                nc.scalar.activation(Pm[n % 2], Sm[n % 2], ACT.Exp, bias=stat[:, b, 1, h:h + 1],
                                     accum_out=stat[:, b, 0, h:h + 1]).then_inc(p_ready, 1)

            def probs_T(n):
                act.wait_ge(pT_ps, n + 1)
                if n >= 2:
                    act.wait_ge(o_ps, n - 1)
                nc.scalar.activation(PT[n % 2], bank[4 + 2 * (n % 2)][:, :], ACT.Copy).then_inc(pT_ready, 1)

            for n in range(NX * NH):
                probs(n)
                if n:
                    probs_T(n - 1)
            probs_T(NX * NH - 1)
            act.wait_ge(sinkarg, 1)
            nc.scalar.activation(stat[:, :, 2, :], stat[:, :, 2, :], ACT.Exp).then_inc(sinkexp, 1)
            for t in range(NX):
                for h in range(2):
                    act.wait_ge(oT_ps, 2 * t + h + 1)
                    nc.scalar.activation(oT[:, 4 * h:4 * h + 4, t * P:(t + 1) * P], bank[4 * t + 2 * h + 1][:, :].rearrange("p (k t) -> p k t", k=4), ACT.Copy).then_inc(oT_ready, 1)
            second_norm(1, range(NX), NT)
            moe_act(1)
            for t in range(NX):
                combine_act(t, NT // 2 + 1)
                act.wait_ge(comb_done, NT + t + 1)
                nc.scalar.activation(comb[:, 2 * t + 1, :], xr[:, t, :], ACT.Square, accum_out=ssq[:, t:t + 1]).then_inc(ssq_done, 1)
                act.wait_ge(ssq_done, 2 * NT + t + 1)
                nc.scalar.activation(rstd[:, t:t + 1], ssq[:, t:t + 1], ACT.Sqrt, bias=eps_t[:, 0:1], scale=1.0 / D).then_inc(sqrt_done, 1)

        @block.tensor
        def _(pe):
            further = pe.alloc_register("further_pe")
            pe.reg_mov(further, 0)
            further_par = [pe.alloc_register(f"further_pe{s}") for s in S2]
            for s in S2:
                pe.reg_mov(further_par[s], 0)
            def transposes(dst, srcs, signal):
                for i, src in enumerate(srcs):
                    last = nc.tensor.transpose(dst[:, i * P:(i + 1) * P], src, ident)
                last.then_inc(signal, 1)

            def rows_T(t, rows, signal):
                v = rows.rearrange("p (c j) -> p j c", j=KD)
                for j in range(KD):
                    last = nc.tensor.transpose(bank[2 * t + j // 4][:, (j % 4) * P:(j % 4 + 1) * P], v[:, j, :], ident)
                last.then_inc(signal, 1)

            pe.wait_ge(small_in, 16)
            for n, t in enumerate(FIRST_ORDER[:3]):
                pe.wait_ge(xn_ready, n + 1)
                rows_T(t, xn0[:, t, :], xT_ps)
            pe.wait_ge(cs_ready, 1)
            for k in range(KD):
                pe.wait_ge(mod0_in[k // 2], 32)
                for g in range(4):
                    last = nc.tensor.matmul(bank[0][32 * g:32 * g + 32, :], cs[:, k, :], mod0_w[k][:, g * HALF:(g + 1) * HALF],
                                            start=(k == 0), stop=(k == KD - 1))
            last.then_inc(mod_done, 1)
            pe.wait_ge(mod_row, 1)
            pe.wait_ge(xn_ready, NT)
            rows_T(0, xn0[:, 0, :], xT_ps)

            pe.wait_ge(hT_act, NT)
            pe.wait_ge(hT_dve, NT)
            pe.wait_ge(pw1_in, 16)
            for m in range(KD):
                for half, b, signal in ((1, 6, g_ps), (0, 5, a_ps)):
                    if m and half:
                        pe.wait_ge(sg_ready, m)
                    elif m:
                        pe.wait_ge(v_ready, m)
                    for j in range(KD):
                        last = nc.tensor.matmul(bank[b][:, :], pw1[:, j, half, :, m], hT0[:, j, :], start=(j == 0), stop=(j == KD - 1))
                    last.then_inc(signal, 1)
                for q in range(5):
                    pe.wait_ge(modk_in[(0, 0, 1, 1, 2)[q]], 16 * (m + 1))
                    for g in range(4):
                        last = nc.tensor.matmul(bank[q][32 * g:32 * g + 32, :], cs[:, m, :], modk_w[q][:, g * HALF:(g + 1) * HALF],
                                                start=(m == 0), stop=(m == KD - 1))
                    if q in (1, 3, 4):
                        last.then_inc(mod_used, 1)
                if m:
                    pe.wait_ge(conv_done, m)
                    last = nc.tensor.matmul(bank[7][:, :], ones, u[:, m - 1, :], start=(m == 1), stop=False)
                if m == KD - 1:
                    last.then_inc(pw1_used, 1)
            pe.wait_ge(conv_done, KD)
            nc.tensor.matmul(bank[7][:, :], ones, u[:, KD - 1, :], start=False, stop=True).then_inc(sum_ps, 1)
            for m in range(KD):
                pe.wait_ge(sq_ready, m + 1)
                last = nc.tensor.matmul(bank[7][:, :], ones, [sq0, sg[:, :]][m % 2], start=(m == 0), stop=(m == KD - 1))
                last.then_inc(sq_used if m < KD - 1 else var_ps, 1)

            def project(lhs, rhs, ts):
                for t in ts:
                    for half in range(2):
                        for j in range(KD):
                            last = nc.tensor.matmul(bank[2 * t + half][:, :], lhs[:, j, t * P:(t + 1) * P],
                                                    rhs[:, j, half * HALF:(half + 1) * HALF], start=(j == 0), stop=(j == KD - 1))
                    last.then_inc(mix_ps, 1)

            def router(l, ts, base):
                for n, t in enumerate(ts):
                    pe.wait_ge(h2_ready, base + n + 1)
                    rows_T(t, h2[:, t, :], h2T_ps)
                pe.wait_ge(h2T_ready, base + len(ts))
                for t in ts:
                    for j in range(KD):
                        last = nc.tensor.matmul(bank[0][:, t * NE:(t + 1) * NE], h2T[l][:, j, t * P:(t + 1) * P], rw[:, j, :],
                                                start=(j == 0), stop=(j == KD - 1))
                last.then_inc(logit_ps, 1)
                pe.wait_ge(mask_ready, l + 1)
                nt = len(ts)
                for t in range(nt + 1):
                    own = [(ones, i) for i in range(min(t, nt))] + ([(before, t)] if t < nt else [])
                    for i, (w, c) in enumerate(own):
                        last = nc.tensor.matmul(bank[1][:, t * NE:(t + 1) * NE], w, msk[:, c, :], start=(i == 0), stop=(i == len(own) - 1))
                last.then_inc(rank_ps, 1)

            def gate_up(s, slot, xt, signal):
                for h in range(2):
                    for j in range(4):
                        for fh in range(2):
                            last = nc.tensor.matmul(bank[s][TILE * fh:TILE * (fh + 1), :].rearrange("p (g f) -> p g f", g=2), XT[xt][:, j, h, :],
                                                    gu_w[slot][:, :, 4 * h + j, fh * 256:(fh + 1) * 256], start=(h + j == 0), stop=(h + j == 4))
                last.then_inc(signal, 1)

            def down(s, slot, signal):
                for h in range(2):
                    for j in range(2):
                        for nh in range(2):
                            last = nc.tensor.matmul(bank[2 + s][TILE * nh:TILE * (nh + 1), :], HT[s][:, j, h, :],
                                                    d_w[slot][:, 2 * h + j, nh * HALF:(nh + 1) * HALF], start=(h + j == 0), stop=(h + j == 2))
                last.then_inc(signal, 1)

            def x_T(i, s, signal):
                transposes(bank[4 + s], [X[i].rearrange("p (c j) -> p j c", j=4)[:, j, :] for j in range(4)], signal)

            def h_T(s, signal):
                transposes(bank[6 + s], [H[s].rearrange("p (c j) -> p j c", j=2)[:, j, :] for j in range(2)], signal)

            def moe(l):
                pe.wait_ge(routed, l + 1)
                for s in S2:
                    pe.wait_ge(x_tile[s], 32 * (PAIRS + 1) * l + 32)
                    x_T(s, s, xt_ps[s])

                def experts(i, k, sixes):
                    slot = [RING[l][(2 * k + s) % SLOTS] for s in S2]
                    use = [USES[l][slot[s]] + 2 * sixes + (2 * k + s) // SLOTS + 1 for s in S2]
                    for s in S2:
                        pe.wait_ge(gu_in[slot[s]], 32 * use[s])
                        pe.wait_ge(xt_ready[s], (PAIRS + 1) * l + i + 1)
                        pe.wait_ge(h_ready[s], PAIRS * l + i)
                        gate_up(s, slot[s], s, gu_ps[s])
                    for s in S2:
                        n = pe.value_load(more[0:1, bass.ds(2 * i + s, 1)], min_val=0, max_val=MAXJ[l] - 1)
                        earlier = pe.snap(further)
                        pe.wait_ge(h_ready[s], PAIRS * l + i + 1)
                        pe.wait_ge(ht_ready[s], PAIRS * l + i)
                        h_T(s, ht_ps[s])
                        pe.wait_ge(x_tile[s], 32 * ((PAIRS + 1) * l + i + 2))
                        x_T(s, s, xt_ps[s])
                        pe.wait_ge(d_in[slot[s]], 16 * use[s])
                        pe.wait_ge(ht_ready[s], PAIRS * l + i + 1)
                        pe.wait_ge(y_ready_m[s], PAIRS * l + i)
                        pe.wait_ge(ov["y"], earlier)
                        down(s, slot[s], d_ps[s])
                        with pe.If(n > 0):
                            with pe.Fori(1, MAXJ[l]) as j:
                                with pe.If(j < n + 1):
                                    q, q_par = pe.snap(further), pe.snap(further_par[s])
                                    pe.wait_ge(further_x[s], 32 * q_par + 32)
                                    pe.wait_ge(xt_ready[s], (PAIRS + 1) * l + i + 2)
                                    x_T(2 + s, s, ov["xt_ps"])
                                    pe.wait_ge(ov["xt"], q + 1)
                                    gate_up(s, slot[s], 2, ov["gu"])
                                    pe.wait_ge(ov["h"], q + 1)
                                    h_T(s, ov["ht_ps"])
                                    pe.wait_ge(ov["ht"], q + 1)
                                    pe.wait_ge(y_ready_m[s], PAIRS * l + i + 1)
                                    pe.wait_ge(ov["y"], q)
                                    down(s, slot[s], ov["y_ps"])
                                    pe.reg_add(further, further, 1)
                                    pe.reg_add(further_par[s], further_par[s], 1)

                with pe.Fori(0, 2) as sixes:
                    for k in range(3):
                        experts(3 * sixes + k, k, sixes)
                for i in (6, 7):
                    experts(i, i % 3, 2)
                pe.wait_ge(y_ready_m[0], PAIRS * (l + 1))
                pe.wait_ge(y_ready_m[1], PAIRS * (l + 1))
                nc.tensor.transpose(bank[6][:, 0:P], ident, ident).then_inc(moe_done[l], 1)

            pe.wait_ge(y_ready, KD)
            pe.wait_ge(mod_row, 2)
            pe.wait_ge(pw2_in, 16)
            project(u, pw2, range(NT))
            router(0, range(NT), 0)
            moe(0)
            for t in range(NT):
                pe.wait_ge(xn_ready, NT + t + 1)
                rows_T(t, comb[:, 2 * (t % 2), :], xT_ps)
            pe.wait_ge(hT_act, 2 * NT)
            pe.wait_ge(hT_dve, 2 * NT)
            pe.wait_ge(qkv_in, 16)
            for t, b, n0 in [(t, b, 2) for t, b in KV_BANKS] + [(t, b, h) for t, h, b in Q_BANKS]:
                for j in range(KD):
                    last = nc.tensor.matmul(bank[b][:, :], hT1[:, j, t * P:(t + 1) * P], wqkv[:, j, n0 * HALF:(n0 + 1) * HALF],
                                            start=(j == 0), stop=(j == KD - 1))
                last.then_inc(proj_ps, 1)
            for n, (t, b) in enumerate(KV_BANKS):
                pe.wait_ge(k_ready, n + 1)
                transposes(bank[b], [kd[:, t, k, :, :].rearrange("p u d -> p (u d)") for k in range(NKV)], kT_ps)
            for n, (t, h, b) in enumerate(Q_BANKS):
                pe.wait_ge(q_ready, n + 1)
                transposes(bank[b], [qr[:, t, (4 * h + i) * P:(4 * h + i + 1) * P] for i in range(4)], qT_ps)
            pe.wait_ge(kT_ready, NT)
            pe.wait_ge(qT_ready, 4)

            def scores(n):
                b, h = n // NH, n % NH
                r = (h % 2) * HD
                if n >= 2:
                    pe.wait_ge(s_ready, n - 1)
                nc.tensor.matmul(bank[2 * (n % 2)][:, :], qT[r:r + HD, h // 2, b * P:(b + 1) * P], kT[r:r + HD, h // GROUP, :],
                                 start=True, stop=True).then_inc(s_ps, 1)

            def values(n):
                b, h = n // NH, n % NH
                pe.wait_ge(pT_ready, n + 1)
                at = bank[4 * b + 1 + 2 * (h // 8)][:, (h % 8) * HD:(h % 8 + 1) * HD]
                for k in range(4):
                    last = nc.tensor.matmul(at, PT[n % 2][:, k * P:(k + 1) * P], vv[:, k, (h // GROUP) * HD:(h // GROUP + 1) * HD],
                                            start=(k == 0), stop=(k == 3))
                last.then_inc(o_ps, 1)

            scores(0)
            for n in range(NX * NH):
                if n + 1 < NX * NH:
                    scores(n + 1)
                if n:
                    values(n - 1)
                pe.wait_ge(p_ready, n + 1)
                if n >= 2:
                    pe.wait_ge(pT_ready, n - 1)
                transposes(bank[4 + 2 * (n % 2)], [Pm[n % 2][:, k * P:(k + 1) * P] for k in range(4)], pT_ps)
            values(NX * NH - 1)
            for t in range(NX):
                for h in range(2):
                    pe.wait_ge(o_ready, 2 * t + h + 1)
                    transposes(bank[4 * t + 2 * h + 1], [o_t[:, t, (4 * h + i) * P:(4 * h + i + 1) * P] for i in range(4)], oT_ps)
            pe.wait_ge(oT_ready, 4)
            pe.wait_ge(wo_in, 16)
            project(oT, wo, range(NX))
            router(1, range(NX), NT)
            moe(1)

        @block.vector
        def _(dve):
            further = dve.alloc_register("further_dve")
            dve.reg_mov(further, 0)
            order = Order(dve, dve_order)
            step = order.step
            V_ = nc.vector

            dve.wait_ge(sqrt_done, 1)
            step(V_.reciprocal(rstd[:, :], rstd[:, :]))
            for t in FIRST_ORDER:
                V_.tensor_scalar(xn0[:, t, :], xr[:, t, :], rstd[:, t:t + 1], None, ALU.mult).then_inc(xn_ready, 1)
            dve.wait_ge(mod_done, 1)
            dve.wait_ge(modb_in, 64)
            V_.tensor_tensor(modb[:, 0, :], bank[0][:, :], modb[:, 0, :], ALU.add).then_inc(mod_row, 1)

            def scale_1(l):
                dve.wait_ge(mod1_in, 16 * (l + 1))
                V_.scalar_tensor_tensor(A1[:, l], mod1[:, l, :, 1, :], 1.0, n1_c[:, l:l + 1, :].to_broadcast([P, 2, KD]),
                                        ALU.add, ALU.mult).then_inc(A1_ready, 1)
                dve.wait_ge(A1_ready, l + 1)

            dve.wait_ge(par_in, 16 * 9)
            scale_1(0)

            def modulated(l, hT, t, n):
                dve.wait_ge(xT_ps, n)
                for j in range(KD // 2, KD):
                    last = V_.tensor_scalar(hT[:, j, t * P:(t + 1) * P], bank[2 * t + 1][:, (j - 4) * P:(j - 3) * P],
                                            A1[:, l, t // NX, j:j + 1], mod1[:, l, t // NX, 0, j:j + 1], ALU.mult, ALU.add)
                last.then_inc(hT_dve, 1)

            for n, t in enumerate(FIRST_ORDER):
                modulated(0, hT0, t, n + 1)

            dve.wait_ge(vpad_zero, 1)
            with dve.Fori(0, KD // 2) as mm:
                for b in range(2):
                    m = 2 * mm + b
                    dve.wait_ge(a_ps, m + 1)
                    dve.wait_ge(sg_ready, m + 1)
                    V_.scalar_tensor_tensor(vpad[:, b, :, PAD:PAD + SEQ], bank[5][:, :].rearrange("p (s t) -> p s t", s=2),
                                            b1_c[:, 0, bass.ds(m, 1)], sg[:, :].rearrange("p (s t) -> p s t", s=2), ALU.add, ALU.mult).then_inc(v_ready, 1)
                    dve.wait_ge(v_ready, m + 1)
                    um = u[:, bass.ds(m, 1), :].rearrange("p m (s t) -> p (m s) t", s=2)
                    sums, taps_done = (um, odd_sum[:, :].rearrange("p (s t) -> p s t", s=2)), m * TAPS
                    V_.tensor_scalar(sums[0], vpad[:, b, :, 0:SEQ], wdw[:, 0, bass.ds(m, 1)], bdw_c[:, bass.ds(m, 1)], ALU.mult, ALU.add).then_inc(conv_order, 1)
                    V_.tensor_scalar(sums[1], vpad[:, b, :, 1:1 + SEQ], wdw[:, 1, bass.ds(m, 1)], None, ALU.mult).then_inc(conv_order, 1)
                    for k in range(2, TAPS):
                        dve.wait_ge(conv_order, taps_done + k - 1)
                        V_.scalar_tensor_tensor(sums[k % 2], vpad[:, b, :, k:k + SEQ], wdw[:, k, bass.ds(m, 1)], sums[k % 2], ALU.mult, ALU.add).then_inc(conv_order, 1)
                    dve.wait_ge(conv_order, taps_done + TAPS)
                    V_.tensor_tensor(sums[0], sums[0], sums[1], ALU.add).then_inc(conv_done, 1)
                    dve.wait_ge(conv_done, m + 1)

            dve.wait_ge(conv_done, KD)
            dve.wait_ge(mean_ready, 1)
            for m in range(KD):
                V_.tensor_tensor(u[:, m, :], u[:, m, :], mean, ALU.subtract).then_inc(dif_ready, 1)
            dve.wait_ge(modb_in, 64 * 6)
            for q in range(5):
                last = V_.tensor_tensor(modb[:, q, :], bank[q][:, :], modb[:, q, :], ALU.add)
            last.then_inc(mod_row, 1)
            dve.wait_ge(std_ready, 1)
            step(V_.reciprocal(rs, rs))
            for m in range(KD):
                V_.tensor_tensor(u[:, m, :], u[:, m, :], rs, ALU.mult).then_inc(z_ready, 1)

            scale_1(1)
            dve.wait_ge(vec_in, 16 * 8)
            for r in range(2):
                last = V_.scalar_tensor_tensor(A2b[r], A2b[r], 1.0, n2b, ALU.add, ALU.mult)
            last.then_inc(A2_ready, 1)
            dve.wait_ge(A2_ready, 1)

            def residual(l, t, n, G1):
                dve.wait_ge(mix_ps, n)
                for half in range(2):
                    cols = slice(half * HALF, (half + 1) * HALF)
                    if l == 0:
                        step(V_.tensor_tensor(h2[:, t, cols], bank[2 * t + half][:, :], b2b[:, cols], ALU.add))
                        step(V_.tensor_tensor(h2[:, t, cols], h2[:, t, cols], G1[:, cols], ALU.mult))
                    else:
                        step(V_.tensor_tensor(h2[:, t, cols], bank[2 * t + half][:, :], G1[:, cols], ALU.mult))
                V_.tensor_tensor(xr[:, t, :], xr[:, t, :], h2[:, t, :], ALU.add).then_inc(mix_read, 1)

            def second_norm(t, n, A2, B2):
                dve.wait_ge(sqrt2_done, n)
                step(V_.reciprocal(rstd[:, t:t + 1], rstd[:, t:t + 1]))
                step(V_.scalar_tensor_tensor(h2[:, t, :], xr[:, t, :], rstd[:, t:t + 1], A2, ALU.mult, ALU.mult))
                V_.tensor_tensor(h2[:, t, :], h2[:, t, :], B2, ALU.add).then_inc(h2_ready, 1)

            def route(l, nt):
                def e3(x):
                    return x[:, 0:nt, :]

                def g4(x):
                    return x[:, 0:nt, :].rearrange("p t (g e) -> p t g e", g=NG)

                def over_e(x):
                    return x.unsqueeze(2).to_broadcast([P, nt, NE])

                sel, t_b, t_c = e3(r_a), e3(r_b), e3(r_c)
                dve.wait_ge(sig_ready, l + 1)
                step(V_.tensor_tensor(sel, e3(lg_s), rb[:, :].unsqueeze(1).to_broadcast([P, nt, NE]), ALU.add))
                hi, lo, top, sec = (x[:, 0:nt, :] for x in g_a)
                a, b, c_, d = (g4(r_a)[:, :, :, i] for i in range(4))
                pair = g4(r_b)
                step(V_.tensor_tensor(pair[:, :, :, 0], a, b, ALU.max))
                step(V_.tensor_tensor(pair[:, :, :, 1], a, b, ALU.min))
                step(V_.tensor_tensor(pair[:, :, :, 2], c_, d, ALU.max))
                step(V_.tensor_tensor(pair[:, :, :, 3], c_, d, ALU.min))
                step(V_.tensor_tensor(top, pair[:, :, :, 0], pair[:, :, :, 2], ALU.max))
                step(V_.tensor_tensor(hi, pair[:, :, :, 0], pair[:, :, :, 2], ALU.min))
                step(V_.tensor_tensor(lo, pair[:, :, :, 1], pair[:, :, :, 3], ALU.max))
                step(V_.tensor_tensor(sec, hi, lo, ALU.max))
                step(V_.tensor_tensor(top, top, sec, ALU.add))

                def first_max(out, vals, n, desc, tmp):
                    wide = [P, nt, n]
                    mt = m1[:, 0:nt]
                    step(V_.tensor_reduce(mt, vals, AX.X, ALU.max))
                    step(V_.tensor_tensor(tmp, vals, mt.unsqueeze(2).to_broadcast(wide), ALU.is_equal))
                    step(V_.tensor_tensor(tmp, tmp, desc.unsqueeze(1).to_broadcast(wide), ALU.mult))
                    step(V_.tensor_reduce(mt, tmp, AX.X, ALU.max))
                    step(V_.tensor_tensor(out, mt.unsqueeze(2).to_broadcast(wide), desc.unsqueeze(1).to_broadcast(wide), ALU.is_equal))

                first_max(hi, top, NG, down_g, lo)
                step(V_.tensor_scalar(lo, hi, BIG, -BIG, ALU.mult, ALU.add))
                step(V_.tensor_tensor(g4(r_a), g4(r_a), lo.unsqueeze(3).to_broadcast([P, nt, NG, EPG]), ALU.add))
                first_max(e3(oh[0]), sel, NE, down_e, t_b)
                step(V_.scalar_tensor_tensor(sel, e3(oh[0]), -2 * BIG, sel, ALU.mult, ALU.add))
                first_max(e3(oh[1]), sel, NE, down_e, t_b)
                V_.tensor_tensor(e3(msk), e3(oh[0]), e3(oh[1]), ALU.add).then_inc(mask_ready, 1)
                for i in range(2):
                    step(V_.tensor_tensor(t_b, e3(lg_s), e3(oh[i]), ALU.mult))
                    step(V_.tensor_reduce(wt[:, i, 0:nt], t_b, AX.X, ALU.add))
                ws = wsum[:, 0:nt]
                step(V_.tensor_tensor(ws, wt[:, 0, 0:nt], wt[:, 1, 0:nt], ALU.add))
                step(V_.reciprocal(ws, ws))
                step(V_.tensor_tensor(wt[:, :, 0:nt], wt[:, :, 0:nt], ws.unsqueeze(1).to_broadcast([P, 2, nt]), ALU.mult))
                dve.wait_ge(rank_ps, l + 1)
                dve.wait_ge(vpad_zero, 5)
                ranks, total = bank[1][:, 0:nt * NE].rearrange("p (t e) -> p t e", t=nt), bank[1][:, nt * NE:(nt + 1) * NE]
                step(V_.tensor_scalar(cnt_i[:, :], total, -1.0, None, ALU.add))
                step(V_.tensor_single_scalar(cnt_i[:, :], cnt_i[:, :], TILE.bit_length() - 1, ALU.arith_shift_right))
                step(V_.tensor_scalar(more[:, 0:NE], cnt_i[:, :], 0, None, ALU.max))
                step(V_.tensor_scalar(cum[0][:, 8:8 + NE], more[:, 0:NE], 1, None, ALU.add))
                for i, d_ in enumerate((1, 2, 4, 8)):
                    x_, y_ = cum[i % 2], cum[(i + 1) % 2]
                    step(V_.tensor_tensor(y_[:, 8:8 + NE], x_[:, 8:8 + NE], x_[:, 8 - d_:8 + NE - d_], ALU.add))
                step(V_.tensor_scalar(r_c[:, 0, :], cum[0][:, 7:7 + NE], float(TILE), None, ALU.mult))
                step(V_.tensor_copy(first[:, 0:NE], r_c[:, 0, :]))
                step(V_.tensor_tensor(sel, ranks, r_c[:, 0:1, :].to_broadcast([P, nt, NE]), ALU.add))
                for i in range(2):
                    step(V_.tensor_tensor(t_b, sel, e3(oh[i]), ALU.mult))
                    step(V_.tensor_reduce(slot_f[:, i, 0:nt], t_b, AX.X, ALU.add))
                V_.tensor_copy(slot[:, :, 0:nt], slot_f[:, :, 0:nt]).then_inc(routed, 1)
                dve.wait_ge(routed, l + 1)

            def moe_dve(l):

                def xt_copy(i, s):
                    return V_.tensor_copy(XT[i].rearrange("p j h s -> p (j h s)"), bank[4 + s][:, :])

                for s in S2:
                    dve.wait_ge(xt_ps[s], (PAIRS + 1) * l + 1)
                    xt_copy(s, s).then_inc(xt_ready[s], 1)
                with dve.Fori(0, NE // 2) as i:
                    for s in S2:
                        dve.wait_ge(silu_done[s], PAIRS * l + i + 1)
                        V_.tensor_tensor(H[s], H[s], bank[s][:, 256:512], ALU.mult).then_inc(h_ready[s], 1)
                    for s in S2:
                        n = dve.value_load(more[0:1, bass.ds(2 * i + s, 1)], min_val=0, max_val=MAXJ[l] - 1)
                        dve.wait_ge(ht_ps[s], PAIRS * l + i + 1)
                        V_.tensor_copy(HT[s].rearrange("p j h s -> p (j h s)"), bank[6 + s][:, 0:256]).then_inc(ht_ready[s], 1)
                        dve.wait_ge(xt_ps[s], (PAIRS + 1) * l + i + 2)
                        xt_copy(s, s).then_inc(xt_ready[s], 1)
                        with dve.If(n > 0):
                            with dve.Fori(1, MAXJ[l]) as j:
                                with dve.If(j < n + 1):
                                    q = dve.snap(further)
                                    dve.wait_ge(ov["xt_ps"], q + 1)
                                    xt_copy(2, s).then_inc(ov["xt"], 1)
                                    dve.wait_ge(ov["silu"], q + 1)
                                    V_.tensor_tensor(H[s], H[s], bank[s][:, 256:512], ALU.mult).then_inc(ov["h"], 1)
                                    dve.wait_ge(ov["ht_ps"], q + 1)
                                    V_.tensor_copy(HT[s].rearrange("p j h s -> p (j h s)"), bank[6 + s][:, 0:256]).then_inc(ov["ht"], 1)
                                    dve.reg_add(further, further, 1)

            def combine(l, t, n, G2):
                b = t % 2
                dve.wait_ge(scaled, n)
                step(V_.scalar_tensor_tensor(comb[:, 2 * b + 1, :], comb[:, 2 * b + 1, :], wt[:, 1, t:t + 1], comb[:, 2 * b, :], ALU.mult, ALU.add))
                step(V_.tensor_tensor(comb[:, 2 * b + 1, :], comb[:, 2 * b + 1, :], G2, ALU.mult))
                V_.tensor_tensor(xr[:, t, :], xr[:, t, :], comb[:, 2 * b + 1, :], ALU.add).then_inc(comb_done, 1)

            for t in range(NT):
                residual(0, t, t + 1, G1b[t // NX])
                second_norm(t, t + 1, A2b[t // NX], B2b[t // NX])
            route(0, NT)
            moe_dve(0)
            dve.wait_ge(vec_in, 16 * 10)
            dve.wait_ge(vec1_in, 16 * 4)
            step(V_.scalar_tensor_tensor(A2n, A2n, 1.0, n2n, ALU.add, ALU.mult))
            for t in range(NT):
                combine(0, t, t + 1, G2b[t // NX])
                dve.wait_ge(sqrt_done, 1 + t + 1)
                step(V_.reciprocal(rstd[:, t:t + 1], rstd[:, t:t + 1]))
                V_.tensor_scalar(comb[:, 2 * (t % 2), :], xr[:, t, :], rstd[:, t:t + 1], None, ALU.mult).then_inc(xn_ready, 1)
                modulated(1, hT1, t, NT + t + 1)

            def rotated(dst, raw, n, t, copies):
                a, b = rt[:, 0:n * HD], rt[:, n * HD:2 * n * HD] if copies else None
                cos = rope[:, t, 0, :].unsqueeze(1).to_broadcast([P, n, HD])
                first_half = dst if copies == 0 else a.rearrange("p (k d) -> p k d", d=HD)
                swapped = (a if copies == 0 else b)
                step(V_.tensor_tensor(first_half, raw.rearrange("p (k d) -> p k d", d=HD), cos, ALU.mult))
                src = raw.rearrange("p (k h q i) -> p k h q i", h=2, q=2, i=ROPE_PAIRS)
                to = swapped.rearrange("p (k h q i) -> p k h q i", h=2, q=2, i=ROPE_PAIRS)
                sin = rope[:, t, 1, :].rearrange("p (h q i) -> p h q i", h=2, q=2)
                for q in range(2):
                    step(V_.tensor_tensor(to[:, :, :, q, :], src[:, :, :, 1 - q, :],
                                          sin[:, :, q, :].unsqueeze(1).to_broadcast([P, n, 2, ROPE_PAIRS]), ALU.mult))
                return first_half, swapped.rearrange("p (k d) -> p k d", d=HD)

            for n, (t, b) in enumerate(KV_BANKS):
                dve.wait_ge(v_copied, n + 1)
                if t >= NX:
                    for up in range(2):
                        last = V_.tensor_copy(kd[:, t, :, up, :], bank[b][:, 0:256].rearrange("p (k d) -> p k d", d=HD))
                else:
                    x_, y_ = rotated(None, bank[b][:, 0:256], NKV, t, 2)
                    for up in range(2):
                        last = V_.tensor_tensor(kd[:, t, :, up, :], x_, y_, ALU.add)
                last.then_inc(k_ready, 1)
                dve.wait_ge(k_ready, n + 1)
            for n, (t, h, b) in enumerate(Q_BANKS):
                dve.wait_ge(proj_ps, NT + n + 1)
                to = qr[:, t, h * HALF:(h + 1) * HALF].rearrange("p (k d) -> p k d", d=HD)
                x_, y_ = rotated(to, bank[b][:, :], 8, t, 0)
                V_.tensor_tensor(to, x_, y_, ALU.add).then_inc(q_ready, 1)
                dve.wait_ge(q_ready, n + 1)

            dve.wait_ge(mask_in, 16)
            for n in range(NX * NH):
                b, h = n // NH, n % NH
                dve.wait_ge(s_ps, n + 1)
                if n >= 2:
                    dve.wait_ge(p_ready, n - 1)
                step(V_.tensor_tensor_reduce(out=Sm[n % 2], in0=bank[2 * (n % 2)][:, :], in1=mask[:, b, :], scale=HD ** -0.5,
                                             scalar=-3e38, op0=ALU.add, op1=ALU.max, accum_out=mx[:, n % 2:n % 2 + 1]))
                V_.tensor_scalar(stat[:, b, 1, h:h + 1], mx[:, n % 2:n % 2 + 1], sink_b[:, h:h + 1], -1.0, ALU.max, ALU.mult).then_inc(s_ready, 1)
            dve.wait_ge(s_ready, NX * NH)
            V_.tensor_tensor(stat[:, :, 2, :], stat[:, :, 1, :], sink_b[:, :].unsqueeze(1).to_broadcast([P, NX, NH]), ALU.add).then_inc(sinkarg, 1)
            dve.wait_ge(sinkexp, 1)
            step(V_.tensor_tensor(stat[:, :, 3, :], stat[:, :, 0, :], stat[:, :, 2, :], ALU.add))
            step(V_.reciprocal(stat[:, :, 3, :], stat[:, :, 3, :]))
            dve.wait_ge(o_ps, NX * NH)
            for t in range(NX):
                for h in range(2):
                    V_.tensor_tensor(o_t[:, t, h * HALF:(h + 1) * HALF].rearrange("p (k d) -> p k d", d=HD),
                                     bank[4 * t + 1 + 2 * h][:, :].rearrange("p (k d) -> p k d", d=HD),
                                     stat[:, t, 3, 8 * h:8 * h + 8].unsqueeze(2).to_broadcast([P, 8, HD]), ALU.mult).then_inc(o_ready, 1)
            for t in range(NX):
                residual(1, t, NT + t + 1, G1n)
                second_norm(t, NT + t + 1, A2n, B2n)
            route(1, NX)
            moe_dve(1)
            dve.wait_ge(fin_in, 32)
            for t in range(NX):
                combine(1, t, NT + t + 1, G2n)
                dve.wait_ge(sqrt_done, 1 + NT + t + 1)
                step(V_.reciprocal(rstd[:, t:t + 1], rstd[:, t:t + 1]))
                V_.scalar_tensor_tensor(xr[:, t, :], xr[:, t, :], rstd[:, t:t + 1], fin_b, ALU.mult, ALU.mult).then_inc(out_ready, 1)


_INS = ["x", "c", "ctx", "c_ctx", "w_mod", "b_mod", "norm1_g", "norm2_g", "conv_w_pw1", "conv_b_pw1", "conv_w_dw",
        "conv_b_dw", "conv_ln_g", "conv_ln_b", "conv_w_pw2", "conv_b_pw2", "attn_w_qkv", "attn_w_o", "attn_sink",
        "router_w", "router_b", "moe_w_gate", "moe_w_up", "moe_w_down", "final_g"]


def kernel(**inputs):
    import concourse.bacc as bacc
    from concourse.bass_utils import run_bass_kernel_spmd

    nc = bacc.Bacc("TRN2", target_bir_lowering=False, num_devices=1)
    small_c, mask_c = shape_constants()
    arrays = {f"in_{name}": np.ascontiguousarray(inputs[name]) for name in _INS}
    arrays["small_c"], arrays["mask_c"] = small_c, mask_c
    args = [nc.dram_tensor(name, a.shape, mybir.dt.from_np(a.dtype), kind="ExternalInput").ap() for name, a in arrays.items()]
    args.append(nc.dram_tensor("result", (1, SEQ, D), FP32, kind="ExternalOutput").ap())
    backbone(nc, *args)
    r = run_bass_kernel_spmd(nc, [arrays], core_ids=[0])
    return r.results[0]["result"]
```

```python
import numpy as np
import concourse.bass as bass
from concourse import mybir
from contextlib import ExitStack

FP32 = mybir.dt.float32
I32 = mybir.dt.int32
ALU = mybir.AluOpType
ACT = mybir.ActivationFunctionType
AX = mybir.AxisListType

P = 128
D = 1024
KD = D // P
SEQ, CTX = 256, 256
NT = (SEQ + CTX) // P
NX = SEQ // P
HALF = 512
TAPS, PAD = 31, 15
DVE_TAPS = 23
LAST_TAPS = TAPS - DVE_TAPS
HD, NH, NKV, GROUP = 64, 16, 4, 4
WINDOW = 128
GRID_W, ROPE_PAIRS, THETA = 64, 16, 10000.0
NE, NG, EPG = 16, 4, 4
F = 512
EPS = 1e-6
BIG = 1e30
TILE = 64
NTOK = (NT * P, NX * P)
MAXJ = tuple(n // TILE for n in NTOK)
ROWS = (NE + (2 * NTOK[0] - NE) // TILE) * TILE + TILE
ROOM = ROWS + MAXJ[0] * TILE
MOD_THIRD = 2048
DMA_CREDIT = 16
CREDIT = 1
SLOTS, SLOTW = 3, 3 * D * F // P
RING = ((0, 1, 2), (1, 0, 2))
PROJECTIONS = ((0, 2, 0), (0, 0, 1), (1, 2, 2), (1, 0, 3), (2, 2, 4), (3, 2, 6), (0, 1, 5), (1, 1, 7))
KV_BANKS = [(t, b, n + 1) for n, (t, c, b) in enumerate(PROJECTIONS) if c == 2]
Q_BANKS = [(t, c, b, n + 1) for n, (t, c, b) in enumerate(PROJECTIONS) if c < 2]
FIRST_ORDER = (1, 2, 3, 0)


def shape_constants():
    i = np.arange(P)
    ident = np.eye(P)
    before = (i[:, None] < i[None, :]) * 1.0
    ones = np.ones((P, P))
    mask = np.zeros((P, NX, 2 * SEQ))
    for b in range(NX):
        mask[:, b, :SEQ] = np.where(np.abs(b * P + i[:, None] - np.arange(SEQ)[None, :]) <= WINDOW, 0.0, -BIG)
    inv = np.power(np.float32(THETA), -np.arange(ROPE_PAIRS, dtype=np.float32) / np.float32(ROPE_PAIRS))
    tok = np.arange(SEQ)
    ang = np.stack([(tok // GRID_W).astype(np.float32)[:, None] * inv,
                    (tok % GRID_W).astype(np.float32)[:, None] * inv], axis=1)
    cos, sin = np.cos(ang), np.sin(ang)
    rope = np.concatenate([np.stack([cos, cos], 2).reshape(SEQ, HD),
                           np.stack([-sin, sin], 2).reshape(SEQ, HD)], axis=1)
    rope = rope.reshape(NX, P, 2 * HD).transpose(1, 0, 2)
    down = np.concatenate([np.broadcast_to(NE - np.arange(NE), (P, NE)),
                           np.broadcast_to(NG - np.arange(NG), (P, NG))], axis=1)
    stack = (i[:, None] % 32 == np.arange(NE)[None, :]) * 1.0
    small = np.concatenate([ident, before, ones, rope.reshape(P, -1), down, stack], axis=1)
    return small.astype(np.float32), mask.reshape(P, -1).astype(np.float32)


class Order:

    def __init__(self, eng, sem, base=0):
        self.eng, self.sem, self.base, self.n = eng, sem, base, 0

    def then(self, ins):
        self.n += 1
        ins.then_inc(self.sem, 1)

    def step(self, ins):
        self.n += 1
        ins.then_inc(self.sem, 1)
        self.eng.wait_ge(self.sem, self.base + self.n)


def backbone(nc, x, c, ctx_in, c_ctx, w_mod, b_mod, norm1_g, norm2_g, w_pw1, b_pw1, w_dw, b_dw, ln_g, ln_b,
             w_pw2, b_pw2, w_qkv, w_o, sink, router_w, router_b, w_gate, w_up, w_down, final_g,
             small_c, mask_c, out):
    mod_d = nc.dram_tensor("mod_d", [6, 2, MOD_THIRD], FP32, kind="Internal").ap()
    xs_d = nc.dram_tensor("xs_d", [ROOM, D], FP32, kind="Internal").ap()
    x_src = [x[0, t * P:(t + 1) * P, :] for t in range(NX)] + [ctx_in[0, t * P:(t + 1) * P, :] for t in range(NX)]

    es = ExitStack()
    with es:
        def sb(name, shape, dt=FP32):
            return es.enter_context(nc.sbuf_tensor(name, shape, dt))

        def sem(name):
            return es.enter_context(nc.semaphore(name))

        W = sb("W", [P, SLOTS * SLOTW])
        R = W[:, 0:24576]
        V = W[:, 24576:32768]
        P1 = W[:, 32768:36864]
        E = sb("E", [P, 2048])
        P2 = sb("P2", [P, 4096])
        xr = sb("xr", [P, NT, D])
        small = sb("small", [P, 3 * P + NX * 2 * HD + 2 * NE + NG])
        ident, before, ones = small[:, 0:P], small[:, P:2 * P], small[:, 2 * P:3 * P]
        rope = small[:, 3 * P:3 * P + NX * 2 * HD].rearrange("p (t s d) -> p t s d", t=NX, s=2)
        down_e = small[:, 3 * P + NX * 2 * HD:3 * P + NX * 2 * HD + NE]
        down_g = small[:, 3 * P + NX * 2 * HD + NE:3 * P + NX * 2 * HD + NE + NG]
        stack4 = small[:, 3 * P + NX * 2 * HD + NE + NG:]
        cT = sb("cT", [P, 2, KD])
        cs = sb("cs", [P, KD, 32])
        vpad = sb("vpad", [P, 2, 2, SEQ + 2 * PAD])
        sg = sb("sg", [P, HALF])
        odd_sum = sb("odd_sum", [P, HALF])
        last_sum = sb("last_sum", [P, HALF])
        par = sb("par", [P, 9 * KD])
        b1_c = par[:, 0:2 * KD].rearrange("p (h m) -> p h m", h=2)
        bdw_c, lng_c, lnb_c = (par[:, (2 + i) * KD:(3 + i) * KD] for i in range(3))
        n1_c = par[:, 5 * KD:7 * KD].rearrange("p (l m) -> p l m", l=2)
        bmod_c = par[:, 7 * KD:9 * KD].rearrange("p (v m) -> p v m", v=2)
        wdw = sb("wdw", [P, TAPS, KD])
        rw = sb("rw", [P, KD, 32])
        rb = sb("rb", [P, NE])
        sink_b = sb("sink_b", [P, NH])
        eps_t = sb("eps_t", [P, 1])
        spare = sb("spare", [P, 16])
        mod1 = sb("mod1", [P, 2, 2, 2, KD])
        A1 = sb("A1", [P, 2, 2, KD])
        zrow = sb("zrow", [P, HALF])
        ssq = sb("ssq", [P, NT])
        ssq_h = sb("ssq_h", [P, 2, NT])
        rstd = sb("rstd", [P, NT])
        lg_s = sb("lg_s", [P, NT, NE])
        r_a = sb("r_a", [P, NT, NE])
        r_b = sb("r_b", [P, NT, NE])
        r_c = sb("r_c", [P, NT, NE])
        oh = [sb(f"oh{i}", [P, NT, NE]) for i in range(2)]
        msk = sb("msk", [P, NT + 1, NE])
        g_a = [sb(f"g_a{i}", [P, NT, NG]) for i in range(4)]
        cum = [sb(f"cum{i}", [P, 8 + NE]) for i in range(2)]
        m1 = sb("m1", [P, NT])
        wt = sb("wt", [P, 2, NT])
        wsum = sb("wsum", [P, NT])
        slot_f = sb("slot_f", [P, 2, NT])
        slot = sb("slot", [P, 2, NT], I32)
        cnt_i = sb("cnt_i", [P, NE], I32)
        more = sb("more", [P, NE + 4], I32)
        first = sb("first", [P, NE + 4], I32)
        stat = sb("stat", [P, NX, 4, NH])
        mx = sb("mx", [P, 2])

        bank = [es.enter_context(nc.psum_tensor(f"bank{i}", [P, HALF], FP32)) for i in range(8)]

        pw1 = R[:, 0:16384].rearrange("p (j h c m) -> p j h c m", j=KD, h=2, m=KD)
        pw2 = R[:, 16384:24576].rearrange("p (m n) -> p m n", m=KD)
        mod0_w = [R[:, 16384 + MOD_THIRD * k:16384 + MOD_THIRD * (k + 1)] for k in range(4)] + \
                 [V[:, MOD_THIRD * k:MOD_THIRD * (k + 1)] for k in range(4)]
        modk_w = [V[:, MOD_THIRD * q:MOD_THIRD * (q + 1)] for q in range(4)] + [E[:, :]]
        hT0 = P1[:, :].rearrange("p (j t) -> p j t", j=KD)
        xn0 = P2[:, :].rearrange("p (t d) -> p t d", t=NT)
        u = P2[:, :].rearrange("p (m t) -> p m t", m=KD)
        modb = R[:, 16384:16384 + 5 * HALF].rearrange("p (q n) -> p q n", q=5)
        mean, rs, sq0 = (P1[:, HALF * i:HALF * (i + 1)] for i in range(5, 8))
        Vb = V[:, :].rearrange("p (v d) -> p v d", v=8)
        G1b = [Vb[:, 0, :], Vb[:, 1, :]]
        A2b = [Vb[:, 2, :], Vb[:, 3, :]]
        B2b = [Vb[:, 4, :], Vb[:, 5, :]]
        G2b = [Vb[:, 6, :], Vb[:, 7, :]]
        n2b, b2b = E[:, 0:D], E[:, D:2 * D]
        h2 = [P1[:, :].rearrange("p (t d) -> p t d", t=NT), P2[:, 2048:4096].rearrange("p (t d) -> p t d", t=NX)]
        h2T = [P2[:, :].rearrange("p (j t) -> p j t", j=KD), E[:, :].rearrange("p (j t) -> p j t", j=KD)]
        logitT = sg
        prod = [zrow[:, :], R[:, 18944:18944 + HALF]]
        ring = [W[:, s * SLOTW:(s + 1) * SLOTW] for s in range(SLOTS)]
        gu_w = [w[:, 0:8192].rearrange("p (g k f) -> p g k f", g=2, k=8) for w in ring]
        d_w = [w[:, 8192:12288].rearrange("p (k n) -> p k n", k=4) for w in ring]
        X = [P2[:, HALF * i:HALF * (i + 1)] for i in range(3)] + [E[:, 3 * HALF:4 * HALF]]
        XT = [P2[:, HALF * (3 + i):HALF * (4 + i)].rearrange("p (j h s) -> p j h s", j=4, h=2) for i in range(3)]
        H = [P2[:, 3072 + 256 * i:3072 + 256 * (i + 1)] for i in range(2)]
        HT = [P2[:, 3584 + 256 * i:3584 + 256 * (i + 1)].rearrange("p (j h s) -> p j h s", j=2, h=2) for i in range(2)]
        Y = [E[:, HALF * i:HALF * (i + 1)] for i in range(3)]
        comb = [w[:, D * i:D * (i + 1)] for w in (P1, R[:, 0:4096]) for i in range(4)]
        hT1 = P2[:, :].rearrange("p (j t) -> p j t", j=KD)
        wqkv = R[:, 12288:24576].rearrange("p (j n) -> p j n", j=KD)
        wo = R[:, 0:8192].rearrange("p (j n) -> p j n", j=KD)
        kd = P1[:, 0:2048].rearrange("p (t k u d) -> p t k u d", t=NT, k=NKV, u=2)
        kT = [w[:, 2048:4096].rearrange("p (k n) -> p k n", k=NKV) for w in (P1, P2)]
        vv = V[:, 4096:5120].rearrange("p (t n) -> p t n", t=NT)
        qr = V[:, 5120:7168].rearrange("p (t n) -> p t n", t=NX)
        rt = V[:, 7168:8192]
        qT = E[:, :].rearrange("p (j t) -> p j t", j=KD)
        Sm = [R[:, 8192 + HALF * i:8192 + HALF * (i + 1)] for i in range(2)]
        Pm = [R[:, 9216 + HALF * i:9216 + HALF * (i + 1)] for i in range(2)]
        PT = [R[:, 10240 + HALF * i:10240 + HALF * (i + 1)] for i in range(2)] + [rt[:, HALF * i:HALF * (i + 1)] for i in range(2)]
        mask = R[:, 11264:12288].rearrange("p (b n) -> p b n", b=NX)
        oT = P2[:, 0:2048].rearrange("p (j t) -> p j t", j=KD)
        fin_b = Vb[:, 7, :]
        G1n, B2n, A2n, G2n, n2n = (Vb[:, i, :] for i in range(5))

        c_in, cs_zero, cs_ready = sem("c_in"), sem("cs_zero"), sem("cs_ready")
        x_in = [sem(f"x_in{t}") for t in range(NT)]
        small_in, par_in, first_in = sem("small_in"), sem("par_in"), sem("first_in")
        modb_zero, modb_in = sem("modb_zero"), sem("modb_in")
        mod0_in = [sem(f"mod0_in{i}") for i in range(4)]
        pw1_in, pw2_in = sem("pw1_in"), sem("pw2_in")
        modk_in = [sem(f"modk_in{i}") for i in range(3)]
        mod_used = sem("mod_used")
        mod_done = sem("mod_done")
        mod_row = sem("mod_row")
        mod_cols, mods_out = sem("mod_cols"), sem("mods_out")
        mod1_in, A1_ready = sem("mod1_in"), sem("A1_ready")
        vec_in, A2_ready = sem("vec_in"), sem("A2_ready")
        ssq_done, sqrt_done, rstd_ready, xn_ready = sem("ssq_done"), sem("sqrt_done"), sem("rstd_ready"), sem("xn_ready")
        xT_ps, hT_act, hT_dve = sem("xT_ps"), sem("hT_act"), sem("hT_dve")
        vpad_zero, prod_ready, last_added = sem("vpad_zero"), sem("prod_ready"), sem("last_added")
        g_ps, a_ps, sg_ready, v_ready, conv_done = sem("g_ps"), sem("a_ps"), sem("sg_ready"), sem("v_ready"), sem("conv_done")
        pw1_used, sum_ps, mean_ready = sem("pw1_used"), sem("sum_ps"), sem("mean_ready")
        dif_ready, sq_ready, sq_used, var_ps = sem("dif_ready"), sem("sq_ready"), sem("sq_used"), sem("var_ps")
        std_ready, z_ready, y_ready = sem("std_ready"), sem("z_ready"), sem("y_ready")
        mix_ps, mix_read = sem("mix_ps"), sem("mix_read")
        ssq2_done, sqrt2_done = sem("ssq2_done"), sem("sqrt2_done")
        h2_scaled = sem("h2_scaled")
        h2_ready, h2T_ps, h2T_ready, logit_ps = sem("h2_ready"), sem("h2T_ps"), sem("h2T_ready"), sem("logit_ps")
        warm = sem("warm")
        logitT_ps, logitT_ready = sem("logitT_ps"), sem("logitT_ready")
        sig_ready, mask_ready, rank_ps = sem("sig_ready"), sem("mask_ready"), sem("rank_ps")
        routed, scattered = sem("routed"), sem("scattered")
        xs_zero_src, xs_zero = sem("xs_zero_src"), sem("xs_zero")
        L = range(2)
        S2 = range(2)

        def sems(name):
            return [sem(f"{name}{s}") for s in S2]

        gu_in, d_in = ([sem(f"{name}{s}") for s in range(SLOTS)] for name in ("gu_in", "d_in"))
        gu_ps, d_ps = sems("gu_ps"), sems("d_ps")
        x_tile = sems("x_tile")
        xt_ps, xt_ready = sems("xt_ps"), sems("xt_ready")
        silu_done, h_ready = sems("silu_done"), sems("h_ready")
        ht_ps, ht_ready = sems("ht_ps"), sems("ht_ready")
        y_ready_m, y_out = sems("y_ready_m"), sems("y_out")
        further_x = sems("further_x")
        ov = {k: sem(f"further_{k}") for k in ("xt_ps", "xt", "gu", "silu", "h", "ht_ps", "ht", "y_ps", "y", "out")}
        USES = [[len(range(RING[0].index(s), NE, SLOTS)) * l for s in range(SLOTS)] for l in range(2)]
        PAIRS = NE // 2
        moe_done = [sem(f"moe_done{l}") for l in L]
        got = [sem(f"got{t}") for t in range(NT)]
        scaled = sem("scaled")
        comb_done = sem("comb_done")
        qkv_in, wo_in, mask_in = sem("qkv_in"), sem("wo_in"), sem("mask_in")
        proj_ps, v_copied, k_ready, kT_ps, kT_ready = sem("proj_ps"), sem("v_copied"), sem("k_ready"), sem("kT_ps"), sem("kT_ready")
        kT_zero = sem("kT_zero")
        q_ready, qT_ps, qT_ready = sem("q_ready"), sem("qT_ps"), sem("qT_ready")
        s_ps, s_ready, p_ready, pT_ps, pT_ready, o_ps = (sem(n) for n in ("s_ps", "s_ready", "p_ready", "pT_ps", "pT_ready", "o_ps"))
        sinkexp, normed, oT_ready = (sem(n) for n in ("sinkexp", "normed", "oT_ready"))
        vec1_in, fin_in = sem("vec1_in"), sem("fin_in")
        out_ready, out_done = sem("out_ready"), sem("out_done")
        dve_order, act_order = sem("dve_order"), sem("act_order")
        conv_order = sem("conv_order")

        block = es.enter_context(nc.Block())

        def row(v, n):
            return v.partition_broadcast(n)

        wg_v = [w_gate[l].rearrange("e (h p j) f -> e p h (j f)", h=2, j=4) for l in L]
        wu_v = [w_up[l].rearrange("e (h p j) f -> e p h (j f)", h=2, j=4) for l in L]
        wd_v = [w_down[l].rearrange("e (h p j) n -> e p h (j n)", h=2, j=2) for l in L]

        @block.sync
        def _(sp):
            for i in range(4):
                if i == 1:
                    for t in FIRST_ORDER:
                        sp.dma_start(xr[:, t, :], x_src[t]).then_inc(x_in[t], 16)
                for k in (2 * i, 2 * i + 1):
                    sp.dma_start(mod0_w[k], w_mod[0].rearrange("(p k) n -> p k n", k=KD)[:, k, 0:MOD_THIRD]).then_inc(mod0_in[i], 16)
            sp.dma_start(R[:, 0:16384], w_pw1[0].rearrange("(p j) n -> p (j n)", j=KD)).then_inc(pw1_in, 16)
            sp.wait_ge(mod_done, 1)
            with sp.Fori(0, KD) as k:
                w_k = [w_mod[l].rearrange("(p k) n -> k p n", k=KD) for l in L]
                sp.wait_ge(mod_used, k * 3 + CREDIT)
                sp.dma_start(V[:, 0:4096], w_k[0][bass.ds(k, 1), :, MOD_THIRD:3 * MOD_THIRD].rearrange("k p n -> (k p) n")).then_inc(modk_in[0], 16)
                sp.wait_ge(mod_used, k * 3 + CREDIT)
                sp.dma_start(V[:, 4096:8192], w_k[1][bass.ds(k, 1), :, 0:2 * MOD_THIRD].rearrange("k p n -> (k p) n")).then_inc(modk_in[1], 16)
                sp.dma_start(E[:, :], w_k[1][bass.ds(k, 1), :, 2 * MOD_THIRD:3 * MOD_THIRD].rearrange("k p n -> (k p) n")).then_inc(modk_in[2], 16)
            pw2_rows = w_pw2[0].rearrange("(p m) n -> p m n", m=KD)
            sp.dma_start(pw2[:, 3:, :], pw2_rows[:, 3:, :]).then_inc(pw2_in, 16)

            extra = sp.alloc_register("further_sp")
            sp.reg_mov(extra, CREDIT)
            done_reg, landed_reg = sp.alloc_register("done_sp"), sp.alloc_register("landed_sp")

            def count(e, l):
                sp.reg_add(extra, extra, sp.value_load(more[0:1, bass.ds(e, 1)], min_val=0, max_val=MAXJ[l] - 1))

            def moe_weights(l):
                def load(w, e, dst, signal):
                    sp.dma_start(dst.rearrange("p (h n) -> p h n", h=2), w[bass.ds(e, 1)].rearrange("e p h n -> (e p) h n")).then_inc(signal, 16)

                def gate(e, slot):
                    load(wg_v[l], e, ring[slot][:, 0:4096], gu_in[slot])

                def up(e, slot):
                    load(wu_v[l], e, ring[slot][:, 4096:8192], gu_in[slot])

                def down(e, slot):
                    load(wd_v[l], e, ring[slot][:, 8192:12288], d_in[slot])

                at = RING[l]
                if l == 0:
                    sp.wait_ge(pw1_used, 1)
                else:
                    sp.wait_ge(proj_ps, 8)
                gate(0, at[0])
                up(0, at[0])
                down(0, at[0])
                if l == 0:
                    sp.wait_ge(mods_out, 64)
                    sp.dma_start(pw2[:, 0:3, :], pw2_rows[:, 0:3, :]).then_inc(pw2_in, 16)
                    gate(1, at[1])
                    sp.wait_ge(mix_ps, 2 * NT)
                else:
                    sp.wait_ge(oT_ready, 4)
                    down(1, at[1])
                    down(2, at[2])
                    sp.wait_ge(mix_ps, 2 * (NT + NX))
                    gate(1, at[1])
                up(1, at[1])
                if l == 0:
                    down(1, at[1])
                sp.wait_ge(h2_ready, NT if l == 0 else NT + NX)
                gate(2, at[2])
                up(2, at[2])
                sp.wait_ge(routed, l + 1)
                if l == 0:
                    sp.wait_ge(x_tile[1], 32)
                    down(2, at[2])

                def refill(e, r):
                    before = e - SLOTS
                    s, slot = r % 2, at[r % SLOTS]
                    count(before, l)
                    served = sp.snap(extra)
                    last = at[(r + SLOTS - 1) % SLOTS]
                    if isinstance(e, int):
                        done = PAIRS * l + before // 2 + 1
                        landed = 32 * (USES[l][last] + (e - 1) // SLOTS + 1)
                    else:
                        done, landed = done_reg, landed_reg
                        sp.reg_mov(done, PAIRS * l + 3 * e6 + r // 2 + 1)
                        sp.reg_mov(landed, 32 * (USES[l][last] + 2 * e6 + (r + SLOTS - 1) // SLOTS + 1))
                    sp.wait_ge(gu_in[last], landed)
                    sp.wait_ge(gu_ps[s], done)
                    sp.wait_ge(ov["gu"], served)
                    gate(e, slot)
                    up(e, slot)
                    sp.wait_ge(d_ps[s], done)
                    sp.wait_ge(ov["y_ps"], served)
                    down(e, slot)

                with sp.Fori(0, 2) as e6:
                    for r in range(6):
                        refill(SLOTS + 6 * e6 + r, r)
                refill(NE - 1, 0)

            moe_weights(0)
            count(NE - 3, 0)
            served = sp.snap(extra)
            sp.wait_ge(d_ps[1], PAIRS - 1)
            sp.wait_ge(ov["y_ps"], served)
            sp.dma_start(R[:, 12288:24576], w_qkv[0].rearrange("(p j) n -> p (j n)", j=KD)).then_inc(qkv_in, 16)
            count(NE - 2, 0)
            count(NE - 1, 0)
            sp.wait_ge(moe_done[0], 1)
            sp.wait_ge(xT_ps, 2 * NT)
            sp.dma_start(wo, w_o[0].rearrange("(j p) n -> p j n", p=P)).then_inc(wo_in, 16)
            sp.dma_start(mask.rearrange("p b n -> p (b n)"), mask_c).then_inc(mask_in, 16)
            moe_weights(1)
            for t in range(NX):
                sp.wait_ge(out_ready, t + 1)
                sp.dma_start(out[0, t * P:(t + 1) * P, :], xr[:, t, :]).then_inc(out_done, 16)
            sp.wait_ge(out_done, 16 * NX)

        @block.gpsimd
        def _(pool):
            further = pool.alloc_register("further_pool")
            pool.reg_mov(further, 0)
            nc.gpsimd.memset(cs[:, :, :], 0.0).then_inc(cs_zero, 1)
            nc.gpsimd.memset(eps_t[:, :], EPS).then_inc(cs_zero, 1)
            nc.gpsimd.memset(vpad[:, :, :, :], 0.0).then_inc(vpad_zero, 1)
            nc.gpsimd.memset(rw[:, :, NE:32], 0.0).then_inc(vpad_zero, 1)
            nc.gpsimd.memset(more[:, :], 0).then_inc(vpad_zero, 1)
            nc.gpsimd.memset(first[:, :], 0).then_inc(vpad_zero, 1)
            for i in range(2):
                nc.gpsimd.memset(cum[i][:, :], 0.0).then_inc(vpad_zero, 1)
            credits = [signal for signal in (v_ready, *h_ready, *ht_ready, *y_ready_m, ov["gu"], ov["y_ps"], ov["y"], mod_used)]
            for i, signal in enumerate(credits):
                nc.gpsimd.memset(spare[0:1, i:i + 1], 0.0).then_inc(signal, CREDIT)

            def bias_rows(slot0, third):
                for g in range(4):
                    src = b_mod[third // 3:third // 3 + 1, (third % 3) * MOD_THIRD + g * HALF:(third % 3) * MOD_THIRD + (g + 1) * HALF]
                    pool.dma_start(modb[32 * g:32 * g + 2, slot0, :], src.broadcast_to([2, HALF])).then_inc(modb_in, 16)

            for i, signal in enumerate((*y_out, ov["out"])):
                pool.dma_start(spare[0:1, 12 + i:13 + i], small_c[0:1, 0:1]).then_inc(signal, DMA_CREDIT)
            loads = [(bdw_c, b_dw[0].rearrange("(p m) -> p m", m=KD)),
                     (lng_c, ln_g[0].rearrange("(p m) -> p m", m=KD)), (lnb_c, ln_b[0].rearrange("(p m) -> p m", m=KD)),
                     (wdw[:, :, :], w_dw[0].rearrange("k (p m) -> p k m", m=KD)),
                     (rw[:, :, 0:NE], router_w.rearrange("(p m) e -> p m e", m=KD)),
                     (rb[:, :], row(router_b, P)), (sink_b[:, :], row(sink[0], P))]
            for dst, src in loads:
                pool.dma_start(dst, src).then_inc(par_in, 16)

            until = pool.alloc_register("until")

            def wait_count(signal, count):
                pool.reg_mov(until, count)
                pool.wait_ge(routed, 1)
                pool.wait_ge(signal, until)

            def shift_scale(l):
                pool.dma_start(mod1[:, l].rearrange("p r v j -> p (r v) j"),
                               mod_d[3 * l].rearrange("r (v p j) -> p (r v) j", v=2, j=KD)).then_inc(mod1_in, 16)

            pool.wait_ge(mod_cols, 1)
            nc.gpsimd.memset(modb[:, :, :], 0.0).then_inc(modb_zero, 1)
            pool.wait_ge(modb_zero, 1)
            for third in range(1, 6):
                bias_rows(third - 1, third)
            n_add = 0
            for m in range(KD):
                for i in range(1, LAST_TAPS):
                    pool.wait_ge(prod_ready, m * LAST_TAPS + i + 1)
                    if i > 1:
                        pool.wait_ge(last_added, n_add)
                    n_add += 1
                    add = nc.gpsimd.tensor_tensor(last_sum[:, :], last_sum[:, :], prod[i % 2], ALU.add).then_inc(last_added, 1)
            pool.wait_ge(mod_row, 2)
            for g in range(4):
                pool.dma_start(mod_d[1:6, :, g * HALF:(g + 1) * HALF].rearrange("q r n -> r q n"), modb[32 * g:32 * g + 2, :, :]).then_inc(mods_out, 16)
            pool.wait_ge(mods_out, 64)
            shift_scale(1)
            vecs = [(G1b, 1, 0), (B2b, 1, D), (A2b, 2, 0)]
            for dst, third, off in vecs:
                for r in range(2):
                    pool.dma_start(dst[r], row(mod_d[third, r, off:off + D], P)).then_inc(vec_in, 16)
            pool.dma_start(n2b, row(norm2_g[0], P)).then_inc(vec_in, 16)
            pool.dma_start(b2b, row(b_pw2[0], P)).then_inc(vec_in, 16)
            nc.gpsimd.memset(zrow[:, :], 0.0).then_inc(xs_zero_src, 1)
            pool.wait_ge(xs_zero_src, 1)
            pool.dma_start(xs_d[0:ROWS, :].rearrange("(p a) (b n) -> p (a b) n", p=P, n=HALF),
                           zrow[:, :].unsqueeze(1).to_broadcast([P, ROWS // P * 2, HALF])).then_inc(xs_zero, 16)

            def moe_rows(l):
                nt = NTOK[l] // P
                pool.wait_ge(routed, l + 1)
                if l == 0:
                    pool.wait_ge(xs_zero, 16)
                for k in range(2):
                    for t in range(nt):
                        pool.indirect_dma_start(xs_d[0:ROWS, :], bass.IndirectOffsetOnAxis(ap=slot[:, k, t:t + 1].bitcast(mybir.dt.uint32), axis=0),
                                                h2[l][:, t, :], None).then_inc(scattered, 16)
                pool.wait_ge(scattered, 32 * (nt if l == 0 else NT + NX))

                def load_rows(dst, at, signal):
                    for h in range(2):
                        pool.dma_start(dst[h * TILE:(h + 1) * TILE, :], xs_d[bass.ds(at, TILE), h * HALF:(h + 1) * HALF]).then_inc(signal, 16)

                def store_rows(src, at, signal):
                    for h in range(2):
                        pool.dma_start(xs_d[bass.ds(at, TILE), h * HALF:(h + 1) * HALF], src[h * TILE:(h + 1) * TILE, :]).then_inc(signal, 16)

                def start_of(e):
                    return pool.value_load(first[0:1, bass.ds(e, 1)], min_val=0, max_val=ROWS - TILE)

                def further_of(e):
                    return pool.value_load(more[0:1, bass.ds(e, 1)], min_val=0, max_val=MAXJ[l] - 1)

                def further_rows(e, s):
                    with pool.If(further_of(e) > 0):
                        load_rows(X[2 + s], pool.snap(start_of(e) + TILE), further_x[s])

                for s in S2:
                    load_rows(X[s], start_of(s), x_tile[s])
                for s in S2:
                    further_rows(s, s)
                    pool.wait_ge(xt_ps[s], (PAIRS + 1) * l + 1)
                    load_rows(X[s], start_of(2 + s), x_tile[s])
                with pool.Fori(0, PAIRS) as i:
                    with pool.If(i < PAIRS - 1):
                        for s in S2:
                            wait_count(xt_ps[s], (PAIRS + 1) * l + i + 2)
                            load_rows(X[s], start_of(2 * i + s + 4), x_tile[s])
                    for s in S2:
                        e = 2 * i + s
                        if s:
                            with pool.If(i > PAIRS - 2):
                                if l == 0:
                                    for r in range(2):
                                        pool.dma_start(G2b[r], row(mod_d[2, r, D:2 * D], P)).then_inc(vec_in, 16)
                                else:
                                    pool.dma_start(G2n, row(mod_d[5, 0, D:2 * D], P)).then_inc(fin_in, 16)
                                    pool.dma_start(fin_b, row(final_g, P)).then_inc(fin_in, 16)
                        at, n = start_of(e), further_of(e)
                        wait_count(y_ready_m[s], PAIRS * l + i + 1 + CREDIT)
                        store_rows(Y[s], at, y_out[s])
                        with pool.If(n > 0):
                            with pool.Fori(1, MAXJ[l]) as j:
                                with pool.If(j < n + 1):
                                    q = pool.snap(further)
                                    with pool.If(j < n):
                                        wait_count(ov["xt_ps"], q + 1)
                                        load_rows(X[2 + s], pool.snap(at + j * TILE + TILE), further_x[s])
                                    wait_count(ov["y"], q + 1 + CREDIT)
                                    store_rows(Y[2], pool.snap(at + j * TILE), ov["out"])
                                    pool.reg_add(further, further, 1)
                        further_rows(e + 2, s)
                for s in S2:
                    pool.wait_ge(y_out[s], 32 * PAIRS * (l + 1) + DMA_CREDIT)
                wait_count(ov["out"], 32 * pool.snap(further) + DMA_CREDIT)
                for t in range(nt):
                    for k in range(2):
                        pool.indirect_dma_start(comb[2 * t + k], None, xs_d[0:ROWS, :],
                                                bass.IndirectOffsetOnAxis(ap=slot[:, k, t:t + 1].bitcast(mybir.dt.uint32), axis=0)).then_inc(got[t], 16)
                    if l == 0 and t == 1:
                        for dst, src in [(G1n, mod_d[4, 0, 0:D]), (B2n, mod_d[4, 0, D:2 * D]), (A2n, mod_d[5, 0, 0:D]),
                                         (n2n, norm2_g[1])]:
                            pool.dma_start(dst, row(src, P)).then_inc(vec1_in, 16)

            moe_rows(0)
            pool.wait_ge(xn_ready, 2 * NT)
            pool.wait_ge(xT_ps, 2 * NT)
            nc.gpsimd.memset(kT[0][HD:P, :, :], 0.0).then_inc(kT_zero, 1)
            pool.wait_ge(proj_ps, 8)
            nc.gpsimd.memset(kT[1][0:HD, :, :], 0.0).then_inc(kT_zero, 1)
            moe_rows(1)

        @block.scalar
        def _(act):
            further = act.alloc_register("further_act")
            act.reg_mov(further, 0)
            order = Order(act, act_order)
            for r, v in ((0, c[0]), (1, c_ctx)):
                act.dma_start(cT[:, r, :], v.rearrange("(p j) -> p j", j=KD)).then_inc(c_in, 16)
            for dst, src in ((bmod_c, b_mod[0, 0:MOD_THIRD].rearrange("(v p j) -> p v j", v=2, j=KD)),
                             (n1_c, norm1_g.rearrange("l (p m) -> p l m", m=KD)),
                             (b1_c, b_pw1[0].rearrange("(h p m) -> p h m", h=2, m=KD))):
                act.dma_start(dst, src).then_inc(first_in, 16)
            act.dma_start(small[:, :], small_c).then_inc(small_in, 16)
            act.wait_ge(c_in, 32)
            act.wait_ge(cs_zero, 2)
            nc.scalar.activation(cs[:, :, 0:2].rearrange("p j r -> p r j"), cT[:, :, :], ACT.Silu).then_inc(cs_ready, 1)
            for t in range(NT):
                act.wait_ge(x_in[t], 16)
                nc.scalar.activation(xn0[:, t, :], xr[:, t, :], ACT.Square, accum_out=ssq[:, t:t + 1]).then_inc(ssq_done, 1)
            act.wait_ge(ssq_done, NT)
            nc.scalar.activation(rstd[:, :], ssq[:, :], ACT.Sqrt, bias=eps_t[:, 0:1], scale=1.0 / D).then_inc(sqrt_done, 1)

            def modulated(l, hT, t, n):
                act.wait_ge(xT_ps, n)
                for j in range(KD // 2):
                    last = nc.scalar.activation(hT[:, j, t * P:(t + 1) * P], bank[2 * t][:, j * P:(j + 1) * P],
                                                ACT.Identity, bias=mod1[:, l, t // NX, 0, j:j + 1], scale=A1[:, l, t // NX, j:j + 1])
                last.then_inc(hT_act, 1)

            act.wait_ge(A1_ready, 1)
            for n, t in enumerate(FIRST_ORDER):
                modulated(0, hT0, t, n + 1)
            act.wait_ge(first_in, 16 * 3)
            act.wait_ge(par_in, 16 * 7)
            with act.Fori(0, KD // 2) as mm:
                for b in range(2):
                    m = 2 * mm + b
                    act.wait_ge(g_ps, m + 1)
                    act.wait_ge(v_ready, m + CREDIT)
                    nc.scalar.activation(sg[:, :], bank[6][:, :], ACT.Sigmoid, bias=b1_c[:, 1, bass.ds(m, 1)]).then_inc(sg_ready, 1)
                    act.wait_ge(v_ready, m + 1 + CREDIT)
                    for i in range(LAST_TAPS):
                        if i >= 3:
                            act.wait_ge(last_added, m * (LAST_TAPS - 1) + i - 2)
                        nc.scalar.activation((prod[i % 2] if i else last_sum[:, :]).rearrange("p (s t) -> p s t", s=2),
                                             vpad[:, b, :, DVE_TAPS + i:DVE_TAPS + i + SEQ], ACT.Copy,
                                             scale=wdw[:, DVE_TAPS + i, bass.ds(m, 1)]).then_inc(prod_ready, 1)
            act.wait_ge(sum_ps, 1)
            nc.scalar.activation(mean, bank[7][:, :], ACT.Copy, scale=1.0 / D).then_inc(mean_ready, 1)
            sq = [sq0, sg[:, :]]
            for m in range(KD):
                act.wait_ge(dif_ready, m + 1)
                if m >= 2:
                    act.wait_ge(sq_used, m - 1)
                nc.scalar.activation(sq[m % 2], u[:, m, :], ACT.Square).then_inc(sq_ready, 1)
            act.wait_ge(var_ps, 1)
            nc.scalar.activation(rs, bank[7][:, :], ACT.Sqrt, bias=eps_t[:, 0:1], scale=1.0 / D).then_inc(std_ready, 1)
            for m in range(KD):
                act.wait_ge(z_ready, m + 1)
                nc.scalar.activation(u[:, m, :], u[:, m, :], ACT.Silu, bias=lnb_c[:, m:m + 1], scale=lng_c[:, m:m + 1]).then_inc(y_ready, 1)

            def second_norm(l, ts, base):
                for n, t in enumerate(ts):
                    act.wait_ge(mix_read, 2 * (base + n) + 1)
                    nc.scalar.activation(h2[l][:, t, 0:HALF], xr[:, t, 0:HALF], ACT.Square, accum_out=ssq_h[:, 0, t:t + 1]).then_inc(ssq2_done, 1)
                    act.wait_ge(ssq2_done, 3 * (base + n) + 1)
                    nc.scalar.activation(ssq[:, t:t + 1], ssq_h[:, 0, t:t + 1], ACT.Identity, bias=eps_t[:, 0:1], scale=1.0 / D).then_inc(ssq2_done, 1)
                    act.wait_ge(mix_read, 2 * (base + n) + 2)
                    nc.scalar.activation(h2[l][:, t, HALF:D], xr[:, t, HALF:D], ACT.Square, accum_out=ssq_h[:, 1, t:t + 1]).then_inc(ssq2_done, 1)
                    act.wait_ge(ssq2_done, 3 * (base + n) + 3)
                    nc.scalar.activation(rstd[:, t:t + 1], ssq_h[:, 1, t:t + 1], ACT.Sqrt, bias=ssq[:, t:t + 1], scale=1.0 / D).then_inc(sqrt2_done, 1)
                for n, t in enumerate(ts):
                    act.wait_ge(h2T_ps, base + n + 1)
                    for half in range(2):
                        last = nc.scalar.activation(h2T[l][:, 4 * half:4 * half + 4, t * P:(t + 1) * P],
                                                    bank[2 * t + half][:, :].rearrange("p (j t) -> p j t", j=4), ACT.Copy)
                    last.then_inc(h2T_ready, 1)
                nt = len(ts)
                nc.scalar.activation(spare[0:1, 15:16], eps_t[0:1, 0:1], ACT.Sigmoid).then_inc(warm, 1)
                act.wait_ge(logitT_ps, l + 1)
                nc.scalar.activation(logitT[:, 0:nt * P], bank[0][:, 0:nt * P], ACT.Copy).then_inc(logitT_ready, 1)
                act.wait_ge(logit_ps, l + 1)
                nc.scalar.activation(lg_s[:, 0:nt, :], bank[0][:, 0:nt * NE].rearrange("p (t e) -> p t e", t=nt), ACT.Sigmoid).then_inc(sig_ready, 1)

            def moe_act(l):
                act.wait_ge(routed, l + 1)
                with act.Fori(0, NE // 2) as i:
                    for s in S2:
                        act.wait_ge(gu_ps[s], PAIRS * l + i + 1)
                        nc.scalar.activation(H[s], bank[s][:, 0:256], ACT.Silu).then_inc(silu_done[s], 1)
                    for s in S2:
                        n = act.value_load(more[0:1, bass.ds(2 * i + s, 1)], min_val=0, max_val=MAXJ[l] - 1)
                        act.wait_ge(d_ps[s], PAIRS * l + i + 1)
                        act.wait_ge(y_out[s], 32 * (PAIRS * l + i) + DMA_CREDIT)
                        nc.scalar.activation(Y[s], bank[2 + s][:, :], ACT.Copy).then_inc(y_ready_m[s], 1)
                        with act.If(n > 0):
                            with act.Fori(1, MAXJ[l]) as j:
                                with act.If(j < n + 1):
                                    q = act.snap(further)
                                    act.wait_ge(ov["gu"], q + 1 + CREDIT)
                                    nc.scalar.activation(H[s], bank[s][:, 0:256], ACT.Silu).then_inc(ov["silu"], 1)
                                    act.wait_ge(ov["y_ps"], q + 1 + CREDIT)
                                    act.wait_ge(ov["out"], q * 32 + DMA_CREDIT)
                                    nc.scalar.activation(Y[2], bank[2 + s][:, :], ACT.Copy).then_inc(ov["y"], 1)
                                    act.reg_add(further, further, 1)

            def combine_act(l, t):
                act.wait_ge(got[t], 32 * (l + 1))
                nc.scalar.activation(comb[2 * t], comb[2 * t], ACT.Copy, scale=wt[:, 0, t:t + 1]).then_inc(scaled, 1)

            second_norm(0, range(NT), 0)
            moe_act(0)
            combine_act(0, 0)
            for t in range(NT):
                if t + 1 < NT:
                    combine_act(0, t + 1)
                act.wait_ge(comb_done, t + 1)
                nc.scalar.activation(comb[2 * t + 1], xr[:, t, :], ACT.Square, accum_out=ssq[:, t:t + 1]).then_inc(ssq_done, 1)
                act.wait_ge(ssq_done, NT + t + 1)
                nc.scalar.activation(rstd[:, t:t + 1], ssq[:, t:t + 1], ACT.Sqrt, bias=eps_t[:, 0:1], scale=1.0 / D).then_inc(sqrt_done, 1)
                act.wait_ge(rstd_ready, t + 1)
                nc.scalar.activation(comb[2 * t], xr[:, t, :], ACT.Copy, scale=rstd[:, t:t + 1]).then_inc(xn_ready, 1)
                act.wait_ge(A1_ready, 2)
                modulated(1, hT1, t, NT + t + 1)
            for t, b, which in KV_BANKS:
                act.wait_ge(proj_ps, which)
                nc.scalar.activation(vv[:, t, :], bank[b][:, 256:512], ACT.Copy).then_inc(v_copied, 1)
            for n, (t, b, _) in enumerate(KV_BANKS):
                act.wait_ge(kT_ps, n + 1)
                for odd in range(2):
                    half = slice(HD * odd, HD * (odd + 1))
                    last = nc.scalar.activation(kT[odd][half, :, t * P:(t + 1) * P], bank[b][half, :].rearrange("p (k t) -> p k t", k=NKV), ACT.Copy)
                last.then_inc(kT_ready, 1)
            for n, (t, h, b, which) in enumerate(Q_BANKS):
                act.wait_ge(qT_ps, n + 1)
                nc.scalar.activation(qT[:, 4 * h:4 * h + 4, t * P:(t + 1) * P], bank[b][:, :].rearrange("p (k t) -> p k t", k=4), ACT.Copy).then_inc(qT_ready, 1)

            def probs(n):
                b, h = n // NH, n % NH
                act.wait_ge(s_ready, n + 1)
                if n >= 2:
                    act.wait_ge(pT_ps, n - 1)
                nc.scalar.activation(Pm[n % 2], Sm[n % 2], ACT.Exp, bias=stat[:, b, 1, h:h + 1],
                                     accum_out=stat[:, b, 0, h:h + 1]).then_inc(p_ready, 1)
                nc.scalar.activation(stat[:, b, 2, h:h + 1], stat[:, b, 1, h:h + 1], ACT.Exp, bias=sink_b[:, h:h + 1]).then_inc(sinkexp, 1)

            def probs_T(n):
                act.wait_ge(pT_ps, n + 1)
                if n >= 4:
                    act.wait_ge(o_ps, n // 2 - 1)
                nc.scalar.activation(PT[n % 4], bank[4 + 2 * (n % 2)][:, :], ACT.Copy).then_inc(pT_ready, 1)

            def mixed(t, h):
                act.wait_ge(o_ps, 8 * t + 4 * (h + 1))
                nc.scalar.activation(oT[:, 4 * h:4 * h + 4, t * P:(t + 1) * P], bank[4 * t + 2 * h + 1][:, :].rearrange("p (k t) -> p k t", k=4), ACT.Copy).then_inc(oT_ready, 1)

            for n in range(NX * NH):
                probs(n)
                if n:
                    probs_T(n - 1)
                if n % 8 == 5 and n > 8:
                    mixed((n - 8) // NH, (n - 8) % NH // 8)
            probs_T(NX * NH - 1)
            mixed(NX - 1, 1)
            second_norm(1, range(NX), NT)
            moe_act(1)
            combine_act(1, 0)
            for t in range(NX):
                if t + 1 < NX:
                    combine_act(1, t + 1)
                act.wait_ge(comb_done, NT + t + 1)
                nc.scalar.activation(comb[2 * t + 1], xr[:, t, :], ACT.Square, accum_out=ssq[:, t:t + 1]).then_inc(ssq_done, 1)
                act.wait_ge(ssq_done, 2 * NT + t + 1)
                nc.scalar.activation(rstd[:, t:t + 1], ssq[:, t:t + 1], ACT.Sqrt, bias=eps_t[:, 0:1], scale=1.0 / D).then_inc(sqrt_done, 1)

        @block.tensor
        def _(pe):
            further = pe.alloc_register("further_pe")
            pe.reg_mov(further, 0)
            further_par = [pe.alloc_register(f"further_pe{s}") for s in S2]
            for s in S2:
                pe.reg_mov(further_par[s], 0)
            def transposes(dst, srcs, signal):
                for i, src in enumerate(srcs):
                    last = nc.tensor.transpose(dst[:, i * P:(i + 1) * P], src, ident)
                last.then_inc(signal, 1)

            def rows_T(t, rows, signal):
                v = rows.rearrange("p (c j) -> p j c", j=KD)
                for j in range(KD):
                    last = nc.tensor.transpose(bank[2 * t + j // 4][:, (j % 4) * P:(j % 4 + 1) * P], v[:, j, :], ident)
                last.then_inc(signal, 1)

            pe.wait_ge(small_in, 16)
            for n, t in enumerate(FIRST_ORDER[:3]):
                pe.wait_ge(xn_ready, n + 1)
                rows_T(t, xn0[:, t, :], xT_ps)
            pe.wait_ge(cs_ready, 1)
            for k in range(KD):
                pe.wait_ge(mod0_in[k // 2], 32)
                for g in range(4):
                    last = nc.tensor.matmul(bank[0][32 * g:32 * g + 32, :], cs[:, k, :], mod0_w[k][:, g * HALF:(g + 1) * HALF],
                                            start=(k == 0), stop=(k == KD - 1))
            last.then_inc(mod_done, 1)
            pe.wait_ge(mod_row, 1)
            for v in range(2):
                for half in range(2):
                    g = 2 * v + half
                    grp = slice(32 * g, 32 * g + 32)
                    for j in range(KD):
                        col = 2 * j
                        last = nc.tensor.matmul(bank[v][64 * half:64 * half + 64, col:col + 2],
                                                modb[grp, 0, :].rearrange("p (c j) -> p j c", j=KD)[:, j, :], ident[grp, 32 * g:32 * g + 2],
                                                start=True, stop=True)
            last.then_inc(mod_cols, 1)
            pe.wait_ge(A1_ready, 1)
            pe.wait_ge(xn_ready, NT)
            rows_T(0, xn0[:, 0, :], xT_ps)

            pe.wait_ge(hT_act, NT)
            pe.wait_ge(hT_dve, NT)
            pe.wait_ge(pw1_in, 16)
            for m in range(KD):
                for half, b, signal in ((1, 6, g_ps), (0, 5, a_ps)):
                    if m and half:
                        pe.wait_ge(sg_ready, m)
                    elif m:
                        pe.wait_ge(v_ready, m + CREDIT)
                    for j in range(KD):
                        last = nc.tensor.matmul(bank[b][:, :], pw1[:, j, half, :, m], hT0[:, j, :], start=(j == 0), stop=(j == KD - 1))
                    last.then_inc(signal, 1)
                for q in range(5):
                    pe.wait_ge(modk_in[(0, 0, 1, 1, 2)[q]], 16 * (m + 1))
                    for g in range(4):
                        last = nc.tensor.matmul(bank[q][32 * g:32 * g + 32, :], cs[:, m, :], modk_w[q][:, g * HALF:(g + 1) * HALF],
                                                start=(m == 0), stop=(m == KD - 1))
                    if q in (1, 3, 4):
                        last.then_inc(mod_used, 1)
                if m:
                    pe.wait_ge(conv_done, m)
                    last = nc.tensor.matmul(bank[7][:, :], ones, u[:, m - 1, :], start=(m == 1), stop=False)
                if m == KD - 1:
                    last.then_inc(pw1_used, 1)
            pe.wait_ge(conv_done, KD)
            nc.tensor.matmul(bank[7][:, :], ones, u[:, KD - 1, :], start=False, stop=True).then_inc(sum_ps, 1)
            for m in range(KD):
                pe.wait_ge(sq_ready, m + 1)
                last = nc.tensor.matmul(bank[7][:, :], ones, [sq0, sg[:, :]][m % 2], start=(m == 0), stop=(m == KD - 1))
                last.then_inc(sq_used if m < KD - 1 else var_ps, 1)

            def project(lhs, rhs, ts, ready=None):
                for t in ts:
                    for half in range(2):
                        for j in range(KD):
                            if ready and t == ts[0] and half == 0:
                                pe.wait_ge(ready, j + 1)
                            last = nc.tensor.matmul(bank[2 * t + half][:, :], lhs[:, j, t * P:(t + 1) * P],
                                                    rhs[:, j, half * HALF:(half + 1) * HALF], start=(j == 0), stop=(j == KD - 1))
                        last.then_inc(mix_ps, 1)

            def router(l, ts, base):
                for n, t in enumerate(ts):
                    pe.wait_ge(h2_ready, base + n + 1)
                    rows_T(t, h2[l][:, t, :], h2T_ps)
                pe.wait_ge(h2T_ready, base + len(ts))
                pe.wait_ge(par_in, 16 * 7)
                pe.wait_ge(vpad_zero, 6)
                for r in range(2):
                    for g in range(4):
                        last = nc.tensor.matmul(bank[0][32 * g:32 * g + 32, 0:len(ts) * P], rw[:, 4 * r + g, :],
                                                h2T[l][:, 4 * r + g, :], start=(r == 0), stop=(r == 1))
                last.then_inc(logitT_ps, 1)
                pe.wait_ge(logitT_ready, l + 1)
                for t in ts:
                    last = nc.tensor.matmul(bank[0][:, t * NE:(t + 1) * NE], logitT[:, t * P:(t + 1) * P], stack4, start=True, stop=True)
                last.then_inc(logit_ps, 1)
                pe.wait_ge(mask_ready, l + 1)
                nt = len(ts)
                for d in range(nt + 1):
                    last = nc.tensor.matmul(bank[1][:, d * NE:(nt + 1) * NE], ones if d else before, msk[:, 0:nt + 1 - d, :].rearrange("p t e -> p (t e)"),
                                            start=(d == 0), stop=(d == nt))
                last.then_inc(rank_ps, 1)

            def gate_up(s, slot, xt, signal):
                for h in range(2):
                    for j in range(4):
                        for fh in range(2):
                            last = nc.tensor.matmul(bank[s][TILE * fh:TILE * (fh + 1), :].rearrange("p (g f) -> p g f", g=2), XT[xt][:, j, h, :],
                                                    gu_w[slot][:, :, 4 * h + j, fh * 256:(fh + 1) * 256], start=(h + j == 0), stop=(h + j == 4))
                last.then_inc(signal, 1)

            def down(s, slot, signal):
                for h in range(2):
                    for j in range(2):
                        for nh in range(2):
                            last = nc.tensor.matmul(bank[2 + s][TILE * nh:TILE * (nh + 1), :], HT[s][:, j, h, :],
                                                    d_w[slot][:, 2 * h + j, nh * HALF:(nh + 1) * HALF], start=(h + j == 0), stop=(h + j == 2))
                last.then_inc(signal, 1)

            def x_T(i, s, signal):
                transposes(bank[4 + s], [X[i].rearrange("p (c j) -> p j c", j=4)[:, j, :] for j in range(4)], signal)

            def h_T(s, signal):
                transposes(bank[6 + s], [H[s].rearrange("p (c j) -> p j c", j=2)[:, j, :] for j in range(2)], signal)

            def moe(l):
                pe.wait_ge(routed, l + 1)
                for s in S2:
                    pe.wait_ge(x_tile[s], 32 * (PAIRS + 1) * l + 32)
                    x_T(s, s, xt_ps[s])

                def further_T(i, s):
                    q_par = pe.snap(further_par[s])
                    pe.wait_ge(further_x[s], 32 * q_par + 32)
                    pe.wait_ge(xt_ready[s], (PAIRS + 1) * l + i + 2)
                    x_T(2 + s, s, ov["xt_ps"])
                    pe.reg_add(further_par[s], further_par[s], 1)

                def experts(i, k, sixes):
                    slot = [RING[l][(2 * k + s) % SLOTS] for s in S2]
                    use = [USES[l][slot[s]] + 2 * sixes + (2 * k + s) // SLOTS + 1 for s in S2]
                    for s in S2:
                        pe.wait_ge(gu_in[slot[s]], 32 * use[s])
                        pe.wait_ge(xt_ready[s], (PAIRS + 1) * l + i + 1)
                        pe.wait_ge(h_ready[s], PAIRS * l + i + CREDIT)
                        gate_up(s, slot[s], s, gu_ps[s])
                    for s in S2:
                        pe.wait_ge(h_ready[s], PAIRS * l + i + 1 + CREDIT)
                        pe.wait_ge(ht_ready[s], PAIRS * l + i + CREDIT)
                        h_T(s, ht_ps[s])
                        pe.wait_ge(x_tile[s], 32 * ((PAIRS + 1) * l + i + 2))
                        x_T(s, s, xt_ps[s])
                    for s in S2:
                        n = pe.value_load(more[0:1, bass.ds(2 * i + s, 1)], min_val=0, max_val=MAXJ[l] - 1)
                        earlier = pe.snap(further)
                        with pe.If(n > 0):
                            further_T(i, s)
                        pe.wait_ge(d_in[slot[s]], 16 * use[s])
                        pe.wait_ge(ht_ready[s], PAIRS * l + i + 1 + CREDIT)
                        pe.wait_ge(y_ready_m[s], PAIRS * l + i + CREDIT)
                        pe.wait_ge(ov["y"], earlier + CREDIT)
                        down(s, slot[s], d_ps[s])
                        with pe.If(n > 0):
                            with pe.Fori(1, MAXJ[l]) as j:
                                with pe.If(j < n + 1):
                                    q = pe.snap(further)
                                    with pe.If(j > 1):
                                        further_T(i, s)
                                    pe.wait_ge(ov["xt"], q + 1)
                                    gate_up(s, slot[s], 2, ov["gu"])
                                    pe.wait_ge(ov["h"], q + 1)
                                    h_T(s, ov["ht_ps"])
                                    pe.wait_ge(ov["ht"], q + 1)
                                    pe.wait_ge(y_ready_m[s], PAIRS * l + i + 1 + CREDIT)
                                    pe.wait_ge(ov["y"], q + CREDIT)
                                    down(s, slot[s], ov["y_ps"])
                                    pe.reg_add(further, further, 1)

                with pe.Fori(0, 2) as sixes:
                    for k in range(3):
                        experts(3 * sixes + k, k, sixes)
                for i in (6, 7):
                    experts(i, i % 3, 2)
                pe.wait_ge(y_ready_m[0], PAIRS * (l + 1) + CREDIT)
                pe.wait_ge(y_ready_m[1], PAIRS * (l + 1) + CREDIT)
                nc.tensor.transpose(bank[6][:, 0:P], ident, ident).then_inc(moe_done[l], 1)

            pe.wait_ge(mod_row, 2)
            pe.wait_ge(pw2_in, 32)
            project(u, pw2, range(NT), y_ready)
            router(0, range(NT), 0)
            moe(0)
            for n, (t, cols, b) in enumerate(PROJECTIONS):
                if n in (0, 1, 3, 4):
                    at = (0, 1, None, 2, 3)[n]
                    pe.wait_ge(xn_ready, NT + at + 1)
                    rows_T(at, comb[2 * at], xT_ps)
                if n == 0:
                    pe.wait_ge(qkv_in, 16)
                pe.wait_ge(hT_act, NT + t + 1)
                pe.wait_ge(hT_dve, NT + t + 1)
                for j in range(KD):
                    last = nc.tensor.matmul(bank[b][:, :], hT1[:, j, t * P:(t + 1) * P], wqkv[:, j, cols * HALF:(cols + 1) * HALF],
                                            start=(j == 0), stop=(j == KD - 1))
                last.then_inc(proj_ps, 1)
            for n, (t, b, _) in enumerate(KV_BANKS):
                pe.wait_ge(k_ready, n + 1)
                transposes(bank[b], [kd[:, t, k, :, :].rearrange("p u d -> p (u d)") for k in range(NKV)], kT_ps)
            for n, (t, h, b, which) in enumerate(Q_BANKS):
                pe.wait_ge(q_ready, n + 1)
                transposes(bank[b], [qr[:, t, (4 * h + i) * P:(4 * h + i + 1) * P] for i in range(4)], qT_ps)
            pe.wait_ge(kT_ready, NT)
            pe.wait_ge(kT_zero, 2)
            pe.wait_ge(qT_ready, 4)

            def scores(n):
                b, h = n // NH, n % NH
                if n >= 2:
                    pe.wait_ge(s_ready, n - 1)
                nc.tensor.matmul(bank[2 * (n % 2)][:, :], qT[:, h // 2, b * P:(b + 1) * P], kT[h % 2][:, h // GROUP, :],
                                 start=True, stop=True).then_inc(s_ps, 1)

            def values(m):
                b, pair = 2 * m // NH, m % (NH // 2)
                pe.wait_ge(pT_ready, 2 * m + 2)
                kv = 2 * pair // GROUP
                for k in range(4):
                    for hh in range(2):
                        last = nc.tensor.matmul(bank[4 * b + 1 + 2 * (pair // 4)][HD * hh:HD * (hh + 1), (pair % 4) * P:(pair % 4 + 1) * P],
                                                vv[:, k, kv * HD:(kv + 1) * HD], PT[(2 * m + hh) % 4][:, k * P:(k + 1) * P],
                                                start=(k == 0), stop=(k == 3))
                last.then_inc(o_ps, 1)

            scores(0)
            scores(1)
            for n in range(NX * NH):
                if n + 2 < NX * NH:
                    scores(n + 2)
                pe.wait_ge(normed, n + 1)
                if n >= 2:
                    pe.wait_ge(pT_ready, n - 1)
                transposes(bank[4 + 2 * (n % 2)], [Pm[n % 2][:, k * P:(k + 1) * P] for k in range(4)], pT_ps)
                if n >= 2 and n % 2 == 0:
                    values(n // 2 - 1)
            values(NX * NH // 2 - 1)
            pe.wait_ge(oT_ready, 4)
            pe.wait_ge(wo_in, 16)
            project(oT, wo, range(NX))
            router(1, range(NX), NT)
            moe(1)

        @block.vector
        def _(dve):
            further = dve.alloc_register("further_dve")
            dve.reg_mov(further, 0)
            order = Order(dve, dve_order)
            step = order.step
            V_ = nc.vector

            dve.wait_ge(sqrt_done, 1)
            step(V_.reciprocal(rstd[:, :], rstd[:, :]))
            for t in FIRST_ORDER:
                V_.tensor_scalar(xn0[:, t, :], xr[:, t, :], rstd[:, t:t + 1], None, ALU.mult).then_inc(xn_ready, 1)
            dve.wait_ge(mod_done, 1)
            V_.tensor_copy(modb[:, 0, :], bank[0][:, :]).then_inc(mod_row, 1)
            dve.wait_ge(mod_cols, 1)
            dve.wait_ge(first_in, 16 * 3)
            for v in range(2):
                step(V_.tensor_tensor(mod1[:, 0, :, v, :], bank[v][:, 0:2 * KD].rearrange("p (j r) -> p r j", r=2),
                                      bmod_c[:, v:v + 1, :].to_broadcast([P, 2, KD]), ALU.add))

            def scale_1(l):
                if l:
                    dve.wait_ge(mod1_in, 16)
                V_.scalar_tensor_tensor(A1[:, l], mod1[:, l, :, 1, :], 1.0, n1_c[:, l:l + 1, :].to_broadcast([P, 2, KD]),
                                        ALU.add, ALU.mult).then_inc(A1_ready, 1)
                dve.wait_ge(A1_ready, l + 1)

            scale_1(0)

            def modulated(l, hT, t, n):
                dve.wait_ge(xT_ps, n)
                for j in range(KD // 2, KD):
                    last = V_.tensor_scalar(hT[:, j, t * P:(t + 1) * P], bank[2 * t + 1][:, (j - 4) * P:(j - 3) * P],
                                            A1[:, l, t // NX, j:j + 1], mod1[:, l, t // NX, 0, j:j + 1], ALU.mult, ALU.add)
                last.then_inc(hT_dve, 1)

            for n, t in enumerate(FIRST_ORDER):
                modulated(0, hT0, t, n + 1)

            dve.wait_ge(vpad_zero, 1)
            dve.wait_ge(par_in, 16 * 7)
            with dve.Fori(0, KD // 2) as mm:
                for b in range(2):
                    m = 2 * mm + b
                    dve.wait_ge(a_ps, m + 1)
                    dve.wait_ge(sg_ready, m + 1)
                    V_.scalar_tensor_tensor(vpad[:, b, :, PAD:PAD + SEQ], bank[5][:, :].rearrange("p (s t) -> p s t", s=2),
                                            b1_c[:, 0, bass.ds(m, 1)], sg[:, :].rearrange("p (s t) -> p s t", s=2), ALU.add, ALU.mult).then_inc(v_ready, 1)
                    dve.wait_ge(v_ready, m + 1 + CREDIT)
                    um = u[:, bass.ds(m, 1), :].rearrange("p m (s t) -> p (m s) t", s=2)
                    sums, taps_done = (um, odd_sum[:, :].rearrange("p (s t) -> p s t", s=2)), m * (DVE_TAPS + 1)
                    V_.tensor_scalar(sums[0], vpad[:, b, :, 0:SEQ], wdw[:, 0, bass.ds(m, 1)], bdw_c[:, bass.ds(m, 1)], ALU.mult, ALU.add).then_inc(conv_order, 1)
                    V_.tensor_scalar(sums[1], vpad[:, b, :, 1:1 + SEQ], wdw[:, 1, bass.ds(m, 1)], None, ALU.mult).then_inc(conv_order, 1)
                    for k in range(2, DVE_TAPS):
                        dve.wait_ge(conv_order, taps_done + k - 1)
                        V_.scalar_tensor_tensor(sums[k % 2], vpad[:, b, :, k:k + SEQ], wdw[:, k, bass.ds(m, 1)], sums[k % 2], ALU.mult, ALU.add).then_inc(conv_order, 1)
                    dve.wait_ge(conv_order, taps_done + DVE_TAPS)
                    V_.tensor_tensor(sums[0], sums[0], sums[1], ALU.add).then_inc(conv_order, 1)
                    dve.wait_ge(conv_order, taps_done + DVE_TAPS + 1)
                    dve.wait_ge(last_added, (m + 1) * (LAST_TAPS - 1))
                    V_.tensor_tensor(sums[0], sums[0], last_sum[:, :].rearrange("p (s t) -> p s t", s=2), ALU.add).then_inc(conv_done, 1)
                    dve.wait_ge(conv_done, m + 1)

            dve.wait_ge(conv_done, KD)
            dve.wait_ge(modb_in, 64 * 5)
            dve.wait_ge(pw1_used, 1)
            for q in range(5):
                last = V_.tensor_tensor(modb[:, q, :], bank[q][:, :], modb[:, q, :], ALU.add)
            last.then_inc(mod_row, 1)
            dve.wait_ge(mean_ready, 1)
            for m in range(KD):
                V_.tensor_tensor(u[:, m, :], u[:, m, :], mean, ALU.subtract).then_inc(dif_ready, 1)
            dve.wait_ge(std_ready, 1)
            step(V_.reciprocal(rs, rs))
            for m in range(KD):
                V_.tensor_tensor(u[:, m, :], u[:, m, :], rs, ALU.mult).then_inc(z_ready, 1)

            scale_1(1)
            dve.wait_ge(vec_in, 16 * 8)
            for r in range(2):
                last = V_.scalar_tensor_tensor(A2b[r], A2b[r], 1.0, n2b, ALU.add, ALU.mult)
            last.then_inc(A2_ready, 1)
            dve.wait_ge(A2_ready, 1)

            def residual(l, t, n, G1):
                tmp = h2[l][:, t, :]
                if l == 0:
                    step(V_.tensor_tensor(tmp, b2b, G1, ALU.mult))
                    step(V_.tensor_tensor(xr[:, t, :], xr[:, t, :], tmp, ALU.add))
                for half in range(2):
                    cols = slice(half * HALF, (half + 1) * HALF)
                    dve.wait_ge(mix_ps, 2 * n - 1 + half)
                    step(V_.tensor_tensor(tmp[:, cols], bank[2 * t + half][:, :], G1[:, cols], ALU.mult))
                    V_.tensor_tensor(xr[:, t, cols], xr[:, t, cols], tmp[:, cols], ALU.add).then_inc(mix_read, 1)

            def second_norm(l, t, n, A2, B2):
                dve.wait_ge(sqrt2_done, n)
                step(V_.reciprocal(rstd[:, t:t + 1], rstd[:, t:t + 1]))
                for half in range(2):
                    cols = slice(half * HALF, (half + 1) * HALF)
                    V_.scalar_tensor_tensor(h2[l][:, t, cols], xr[:, t, cols], rstd[:, t:t + 1], A2[:, cols], ALU.mult, ALU.mult).then_inc(h2_scaled, 1)
                for half in range(2):
                    cols = slice(half * HALF, (half + 1) * HALF)
                    dve.wait_ge(h2_scaled, 2 * n - 1 + half)
                    last = V_.tensor_tensor(h2[l][:, t, cols], h2[l][:, t, cols], B2[:, cols], ALU.add)
                last.then_inc(h2_ready, 1)

            def route(l, nt):
                def e3(x):
                    return x[:, 0:nt, :]

                def g4(x):
                    return x[:, 0:nt, :].rearrange("p t (g e) -> p t g e", g=NG)

                def over_e(x):
                    return x.unsqueeze(2).to_broadcast([P, nt, NE])

                sel, t_b, t_c = e3(r_a), e3(r_b), e3(r_c)
                step(V_.memset(msk[:, nt, :], 0.0))
                dve.wait_ge(sig_ready, l + 1)
                step(V_.tensor_tensor(sel, e3(lg_s), rb[:, :].unsqueeze(1).to_broadcast([P, nt, NE]), ALU.add))
                hi, lo, top, sec = (x[:, 0:nt, :] for x in g_a)
                a, b, c_, d = (g4(r_a)[:, :, :, i] for i in range(4))
                pair = g4(r_b)
                order.then(V_.tensor_tensor(pair[:, :, :, 0], a, b, ALU.max))
                order.then(V_.tensor_tensor(pair[:, :, :, 1], a, b, ALU.min))
                order.then(V_.tensor_tensor(pair[:, :, :, 2], c_, d, ALU.max))
                step(V_.tensor_tensor(pair[:, :, :, 3], c_, d, ALU.min))
                order.then(V_.tensor_tensor(hi, pair[:, :, :, 0], pair[:, :, :, 2], ALU.min))
                order.then(V_.tensor_tensor(lo, pair[:, :, :, 1], pair[:, :, :, 3], ALU.max))
                step(V_.tensor_tensor(top, pair[:, :, :, 0], pair[:, :, :, 2], ALU.max))
                step(V_.tensor_tensor(sec, hi, lo, ALU.max))
                step(V_.tensor_tensor(top, top, sec, ALU.add))

                def first_max(out, vals, n, desc, tmp):
                    wide = [P, nt, n]
                    mt = m1[:, 0:nt]
                    step(V_.tensor_reduce(mt, vals, AX.X, ALU.max))
                    step(V_.tensor_tensor(tmp, vals, mt.unsqueeze(2).to_broadcast(wide), ALU.is_equal))
                    step(V_.tensor_tensor(tmp, tmp, desc.unsqueeze(1).to_broadcast(wide), ALU.mult))
                    step(V_.tensor_reduce(mt, tmp, AX.X, ALU.max))
                    step(V_.tensor_tensor(out, mt.unsqueeze(2).to_broadcast(wide), desc.unsqueeze(1).to_broadcast(wide), ALU.is_equal))

                first_max(hi, top, NG, down_g, lo)
                step(V_.tensor_scalar(lo, hi, BIG, -BIG, ALU.mult, ALU.add))
                step(V_.tensor_tensor(g4(r_a), g4(r_a), lo.unsqueeze(3).to_broadcast([P, nt, NG, EPG]), ALU.add))
                first_max(e3(oh[0]), sel, NE, down_e, t_b)
                step(V_.scalar_tensor_tensor(sel, e3(oh[0]), -2 * BIG, sel, ALU.mult, ALU.add))
                first_max(e3(oh[1]), sel, NE, down_e, t_b)
                V_.tensor_tensor(e3(msk), e3(oh[0]), e3(oh[1]), ALU.add).then_inc(mask_ready, 1)
                for i in range(2):
                    step(V_.tensor_tensor(t_b, e3(lg_s), e3(oh[i]), ALU.mult))
                    step(V_.tensor_reduce(wt[:, i, 0:nt], t_b, AX.X, ALU.add))
                ws = wsum[:, 0:nt]
                step(V_.tensor_tensor(ws, wt[:, 0, 0:nt], wt[:, 1, 0:nt], ALU.add))
                step(V_.reciprocal(ws, ws))
                step(V_.tensor_tensor(wt[:, :, 0:nt], wt[:, :, 0:nt], ws.unsqueeze(1).to_broadcast([P, 2, nt]), ALU.mult))
                dve.wait_ge(rank_ps, l + 1)
                dve.wait_ge(vpad_zero, 6)
                ranks, total = bank[1][:, 0:nt * NE].rearrange("p (t e) -> p t e", t=nt), bank[1][:, nt * NE:(nt + 1) * NE]
                step(V_.tensor_scalar(cnt_i[:, :], total, -1.0, None, ALU.add))
                step(V_.tensor_single_scalar(cnt_i[:, :], cnt_i[:, :], TILE.bit_length() - 1, ALU.arith_shift_right))
                step(V_.tensor_scalar(more[:, 0:NE], cnt_i[:, :], 0, None, ALU.max))
                step(V_.tensor_scalar(cum[0][:, 8:8 + NE], more[:, 0:NE], 1, None, ALU.add))
                for i, d_ in enumerate((1, 2, 4, 8)):
                    x_, y_ = cum[i % 2], cum[(i + 1) % 2]
                    step(V_.tensor_tensor(y_[:, 8:8 + NE], x_[:, 8:8 + NE], x_[:, 8 - d_:8 + NE - d_], ALU.add))
                step(V_.tensor_scalar(r_c[:, 0, :], cum[0][:, 7:7 + NE], float(TILE), None, ALU.mult))
                step(V_.tensor_copy(first[:, 0:NE], r_c[:, 0, :]))
                step(V_.tensor_tensor(sel, ranks, r_c[:, 0:1, :].to_broadcast([P, nt, NE]), ALU.add))
                for i in range(2):
                    step(V_.tensor_tensor(t_b, sel, e3(oh[i]), ALU.mult))
                    step(V_.tensor_reduce(slot_f[:, i, 0:nt], t_b, AX.X, ALU.add))
                V_.tensor_copy(slot[:, :, 0:nt], slot_f[:, :, 0:nt]).then_inc(routed, 1)
                dve.wait_ge(routed, l + 1)

            def moe_dve(l):

                def xt_copy(i, s):
                    return V_.tensor_copy(XT[i].rearrange("p j h s -> p (j h s)"), bank[4 + s][:, :])

                for s in S2:
                    dve.wait_ge(xt_ps[s], (PAIRS + 1) * l + 1)
                    xt_copy(s, s).then_inc(xt_ready[s], 1)
                with dve.Fori(0, NE // 2) as i:
                    for s in S2:
                        dve.wait_ge(silu_done[s], PAIRS * l + i + 1)
                        V_.tensor_tensor(H[s], H[s], bank[s][:, 256:512], ALU.mult).then_inc(h_ready[s], 1)
                    for s in S2:
                        dve.wait_ge(ht_ps[s], PAIRS * l + i + 1)
                        V_.tensor_copy(HT[s].rearrange("p j h s -> p (j h s)"), bank[6 + s][:, 0:256]).then_inc(ht_ready[s], 1)
                        dve.wait_ge(xt_ps[s], (PAIRS + 1) * l + i + 2)
                        xt_copy(s, s).then_inc(xt_ready[s], 1)
                    for s in S2:
                        n = dve.value_load(more[0:1, bass.ds(2 * i + s, 1)], min_val=0, max_val=MAXJ[l] - 1)
                        with dve.If(n > 0):
                            with dve.Fori(1, MAXJ[l]) as j:
                                with dve.If(j < n + 1):
                                    q = dve.snap(further)
                                    dve.wait_ge(ov["xt_ps"], q + 1)
                                    xt_copy(2, s).then_inc(ov["xt"], 1)
                                    dve.wait_ge(ov["silu"], q + 1)
                                    V_.tensor_tensor(H[s], H[s], bank[s][:, 256:512], ALU.mult).then_inc(ov["h"], 1)
                                    dve.wait_ge(ov["ht_ps"], q + 1)
                                    V_.tensor_copy(HT[s].rearrange("p j h s -> p (j h s)"), bank[6 + s][:, 0:256]).then_inc(ov["ht"], 1)
                                    dve.reg_add(further, further, 1)

            def combine(l, t, n, G2):
                dve.wait_ge(scaled, n)
                step(V_.scalar_tensor_tensor(comb[2 * t + 1], comb[2 * t + 1], wt[:, 1, t:t + 1], comb[2 * t], ALU.mult, ALU.add))
                step(V_.tensor_tensor(comb[2 * t + 1], comb[2 * t + 1], G2, ALU.mult))
                V_.tensor_tensor(xr[:, t, :], xr[:, t, :], comb[2 * t + 1], ALU.add).then_inc(comb_done, 1)

            for t in range(NT):
                residual(0, t, t + 1, G1b[t // NX])
                second_norm(0, t, t + 1, A2b[t // NX], B2b[t // NX])
            route(0, NT)
            moe_dve(0)
            dve.wait_ge(vec_in, 16 * 10)
            combine(0, 0, 1, G2b[0])
            for t in range(NT):
                if t + 1 < NT:
                    combine(0, t + 1, t + 2, G2b[(t + 1) // NX])
                if t == NT - 1:
                    dve.wait_ge(vec1_in, 16 * 4)
                    step(V_.scalar_tensor_tensor(A2n, A2n, 1.0, n2n, ALU.add, ALU.mult))
                dve.wait_ge(sqrt_done, 1 + t + 1)
                V_.reciprocal(rstd[:, t:t + 1], rstd[:, t:t + 1]).then_inc(rstd_ready, 1)
                modulated(1, hT1, t, NT + t + 1)

            def rotated(dst, raw, n, t, copies):
                a, b = rt[:, 0:n * HD], rt[:, n * HD:2 * n * HD] if copies else None
                cos = rope[:, t, 0, :].unsqueeze(1).to_broadcast([P, n, HD])
                first_half = dst if copies == 0 else a.rearrange("p (k d) -> p k d", d=HD)
                swapped = (a if copies == 0 else b)
                step(V_.tensor_tensor(first_half, raw.rearrange("p (k d) -> p k d", d=HD), cos, ALU.mult))
                src = raw.rearrange("p (k h q i) -> p k h q i", h=2, q=2, i=ROPE_PAIRS)
                to = swapped.rearrange("p (k h q i) -> p k h q i", h=2, q=2, i=ROPE_PAIRS)
                sin = rope[:, t, 1, :].rearrange("p (h q i) -> p h q i", h=2, q=2)
                for q in range(2):
                    step(V_.tensor_tensor(to[:, :, :, q, :], src[:, :, :, 1 - q, :],
                                          sin[:, :, q, :].unsqueeze(1).to_broadcast([P, n, 2, ROPE_PAIRS]), ALU.mult))
                return first_half, swapped.rearrange("p (k d) -> p k d", d=HD)

            for n, (t, b, _) in enumerate(KV_BANKS):
                dve.wait_ge(v_copied, n + 1)
                if t >= NX:
                    for up in range(2):
                        last = V_.tensor_copy(kd[:, t, :, up, :], bank[b][:, 0:256].rearrange("p (k d) -> p k d", d=HD))
                else:
                    x_, y_ = rotated(None, bank[b][:, 0:256], NKV, t, 2)
                    for up in range(2):
                        last = V_.tensor_tensor(kd[:, t, :, up, :], x_, y_, ALU.add)
                last.then_inc(k_ready, 1)
                dve.wait_ge(k_ready, n + 1)
            for n, (t, h, b, which) in enumerate(Q_BANKS):
                dve.wait_ge(proj_ps, which)
                to = qr[:, t, h * HALF:(h + 1) * HALF].rearrange("p (k d) -> p k d", d=HD)
                x_, y_ = rotated(to, bank[b][:, :], 8, t, 0)
                V_.tensor_tensor(to, x_, y_, ALU.add).then_inc(q_ready, 1)
                dve.wait_ge(q_ready, n + 1)

            dve.wait_ge(mask_in, 16)
            def masked(n):
                b, h = n // NH, n % NH
                dve.wait_ge(s_ps, n + 1)
                if n >= 2:
                    dve.wait_ge(p_ready, n - 1)
                step(V_.tensor_tensor_reduce(out=Sm[n % 2], in0=bank[2 * (n % 2)][:, :], in1=mask[:, b, :], scale=HD ** -0.5,
                                             scalar=-3e38, op0=ALU.add, op1=ALU.max, accum_out=mx[:, n % 2:n % 2 + 1]))
                V_.tensor_scalar(stat[:, b, 1, h:h + 1], mx[:, n % 2:n % 2 + 1], sink_b[:, h:h + 1], -1.0, ALU.max, ALU.mult).then_inc(s_ready, 1)

            masked(0)
            for n in range(NX * NH):
                b, h = n // NH, n % NH
                if n + 1 < NX * NH:
                    masked(n + 1)
                dve.wait_ge(p_ready, n + 1)
                dve.wait_ge(sinkexp, n + 1)
                step(V_.tensor_tensor(stat[:, b, 3, h:h + 1], stat[:, b, 0, h:h + 1], stat[:, b, 2, h:h + 1], ALU.add))
                step(V_.reciprocal(stat[:, b, 3, h:h + 1], stat[:, b, 3, h:h + 1]))
                V_.tensor_scalar(Pm[n % 2], Pm[n % 2], stat[:, b, 3, h:h + 1], None, ALU.mult).then_inc(normed, 1)
            for t in range(NX):
                residual(1, t, NT + t + 1, G1n)
                second_norm(1, t, NT + t + 1, A2n, B2n)
            route(1, NX)
            moe_dve(1)
            dve.wait_ge(fin_in, 32)
            combine(1, 0, NT + 1, G2n)
            for t in range(NX):
                if t + 1 < NX:
                    combine(1, t + 1, NT + t + 2, G2n)
                dve.wait_ge(sqrt_done, 1 + NT + t + 1)
                step(V_.reciprocal(rstd[:, t:t + 1], rstd[:, t:t + 1]))
                V_.scalar_tensor_tensor(xr[:, t, :], xr[:, t, :], rstd[:, t:t + 1], fin_b, ALU.mult, ALU.mult).then_inc(out_ready, 1)


_INS = ["x", "c", "ctx", "c_ctx", "w_mod", "b_mod", "norm1_g", "norm2_g", "conv_w_pw1", "conv_b_pw1", "conv_w_dw",
        "conv_b_dw", "conv_ln_g", "conv_ln_b", "conv_w_pw2", "conv_b_pw2", "attn_w_qkv", "attn_w_o", "attn_sink",
        "router_w", "router_b", "moe_w_gate", "moe_w_up", "moe_w_down", "final_g"]


def kernel(**inputs):
    import concourse.bacc as bacc
    from concourse.bass_utils import run_bass_kernel_spmd

    nc = bacc.Bacc("TRN2", target_bir_lowering=False, num_devices=1)
    small_c, mask_c = shape_constants()
    arrays = {f"in_{name}": np.ascontiguousarray(inputs[name]) for name in _INS}
    arrays["small_c"], arrays["mask_c"] = small_c, mask_c
    args = [nc.dram_tensor(name, a.shape, mybir.dt.from_np(a.dtype), kind="ExternalInput").ap() for name, a in arrays.items()]
    args.append(nc.dram_tensor("result", (1, SEQ, D), FP32, kind="ExternalOutput").ap())
    backbone(nc, *args)
    r = run_bass_kernel_spmd(nc, [arrays], core_ids=[0])
    return r.results[0]["result"]
```
